# Optimizing a Trainium2 kernel written in Bass

```python
import functools
import jax, jax.numpy as jnp
from jax import lax
import numpy as np

D_MODEL = 1024
BATCH = 1
SEQ = 512
DEPTH = 2

GRID_W = 64
CTX_LEN = 256
HEAD_DIM = 64
EPS = 1e-6
HG_HEADS = 4
HG_DK = 64
HG_DV = 64
HG_WIDTH = HG_HEADS * HG_DK
HG_CHUNK = 64
SWA_HEADS = 6
SWA_KV_HEADS = 2
SWA_GROUP = SWA_HEADS // SWA_KV_HEADS
SWA_WINDOW = 128
SWA_BLOCK = 128
ROPE_BASE = 10000.0
NAT_HEADS = 6
NAT_ROWS = 8
NAT_COLS = 16
NAT_QCOLS = 16
NAT_SLAB = 32
MIX_WIDTH = HG_WIDTH + SWA_HEADS * HEAD_DIM + NAT_HEADS * HEAD_DIM
PROJ_SPLITS = (HG_WIDTH,) * 5 + (SWA_HEADS * HEAD_DIM, SWA_KV_HEADS * HEAD_DIM, SWA_KV_HEADS * HEAD_DIM) + (NAT_HEADS * HEAD_DIM,) * 3
PROJ_WIDTH = sum(PROJ_SPLITS)
PEER_HEADS = 8
PEER_NKEYS = 128
PEER_EXPERTS = PEER_NKEYS * PEER_NKEYS
PEER_DK = 256
PEER_TOPK = 16
PEER_BLOCK = 128

kernel_name = "hybrid_hgrn2_swa_natten_peer_dit"

def rms_norm(x, w):
    xf = x.astype(jnp.float32)
    y = xf * lax.rsqrt(jnp.mean(xf * xf, axis=-1, keepdims=True) + EPS)
    return (y * w.astype(jnp.float32)).astype(x.dtype)

def modulate(h, shift, scale):
    return h * (1.0 + scale) + shift

def split_proj(p):
    idx = [int(i) for i in np.cumsum(PROJ_SPLITS)[:-1]]
    return jnp.split(p, idx, axis=-1)

def _heads(a, h):
    return a.reshape(a.shape[0], a.shape[1], h, a.shape[-1] // h)

def joint_softmax(scores, sink=None):
    m = functools.reduce(jnp.maximum, [s.max(axis=-1, keepdims=True) for s in scores])
    if sink is not None:
        m = jnp.maximum(m, sink)
    ps = [jnp.exp(s - m) for s in scores]
    den = ps[0].sum(axis=-1, keepdims=True)
    for p in ps[1:]:
        den = den + p.sum(axis=-1, keepdims=True)
    if sink is not None:
        den = den + jnp.exp(sink - m)
    return [p / den for p in ps]

def axial_rope(x, pos_row, pos_col):
    d = x.shape[-1]
    half = d // 2
    nf = half // 2
    inv_freq = ROPE_BASE ** (-jnp.arange(nf, dtype=jnp.float32) / nf)
    xf = x.astype(jnp.float32)

    def rot(xa, pos):
        ang = pos.astype(jnp.float32)[:, None] * inv_freq
        cos = jnp.cos(ang)[None, :, None, :]
        sin = jnp.sin(ang)[None, :, None, :]
        x1, x2 = xa[..., :nf], xa[..., nf:]
        return jnp.concatenate([x1 * cos - x2 * sin, x2 * cos + x1 * sin], axis=-1)

    out = jnp.concatenate([rot(xf[..., :half], pos_row), rot(xf[..., half:], pos_col)], axis=-1)
    return out.astype(x.dtype)

def gla_chunk_scan(q, k, v, log_f, s0):
    B, L, H, dk = q.shape
    dv = v.shape[-1]
    n = L // HG_CHUNK

    def chunks(a):
        return a.reshape(B, n, HG_CHUNK, H, a.shape[-1]).transpose(1, 0, 3, 2, 4)

    tri = jnp.tril(jnp.ones((HG_CHUNK, HG_CHUNK), dtype=bool))[:, :, None]

    def step(S, inp):
        qc, kc, vc, gc = inp
        b = jnp.cumsum(gc, axis=2)
        b_last = b[:, :, -1:, :]
        decay = jnp.exp(jnp.where(tri, b[:, :, :, None, :] - b[:, :, None, :, :], -jnp.inf))
        scores = jnp.einsum('bhtd,bhsd,bhtsd->bhts', qc, kc, decay)
        o = jnp.einsum('bhts,bhse->bhte', scores, vc) + jnp.einsum('bhtd,bhde->bhte', qc * jnp.exp(b), S)
        S = jnp.exp(b_last)[:, :, 0, :, None] * S + jnp.einsum('bhsd,bhse->bhde', kc * jnp.exp(b_last - b), vc)
        return S, o

    S, o = lax.scan(step, s0, (chunks(q), chunks(k), chunks(v), chunks(log_f)))
    return o.transpose(1, 0, 3, 2, 4).reshape(B, L, H, dv), S

def _hgrn2_gates(z, lb):
    z = z.astype(jnp.float32)
    log_f = jnp.logaddexp(jnp.log(lb), jnp.log1p(-lb) + jax.nn.log_sigmoid(z))
    k = (1.0 - lb) * jax.nn.sigmoid(-z)
    return _heads(log_f, HG_HEADS), _heads(k, HG_HEADS)

def hgrn2_mixer(parts_ctx, parts_lat, lb_fwd, lb_bwd, norm_w, need_ctx):
    def prep(parts):
        q, zf, zb, v, g = parts
        q = _heads(jax.nn.silu(q.astype(jnp.float32)), HG_HEADS)
        v = _heads(v.astype(jnp.float32), HG_HEADS)
        return q, _hgrn2_gates(zf, lb_fwd), _hgrn2_gates(zb, lb_bwd), v, g

    qc, fwd_c, bwd_c, vc, gc = prep(parts_ctx)
    ql, fwd_l, bwd_l, vl, gl = prep(parts_lat)
    s0 = jnp.zeros((qc.shape[0], HG_HEADS, HG_DK, HG_DV), jnp.float32)
    rev = lambda a: jnp.flip(a, axis=1)
    oc_f, sc_f = gla_chunk_scan(qc, fwd_c[1], vc, fwd_c[0], s0)
    ol_f, _ = gla_chunk_scan(ql, fwd_l[1], vl, fwd_l[0], sc_f)
    oc_b, sc_b = gla_chunk_scan(rev(qc), rev(bwd_c[1]), rev(vc), rev(bwd_c[0]), s0)
    ol_b, _ = gla_chunk_scan(rev(ql), rev(bwd_l[1]), rev(vl), rev(bwd_l[0]), sc_b)

    def readout(o, g):
        o = o * lax.rsqrt(jnp.mean(o * o, axis=-1, keepdims=True) + EPS)
        o = o.reshape(o.shape[0], o.shape[1], HG_WIDTH) * norm_w.astype(jnp.float32)
        return (o * jax.nn.silu(g.astype(jnp.float32))).astype(g.dtype)

    out_lat = readout(ol_f + rev(ol_b), gl)
    out_ctx = readout(oc_f + rev(oc_b), gc) if need_ctx else None
    return out_lat, out_ctx

def swa_mixer(parts_ctx, parts_lat, sink, pos_row, pos_col, need_ctx):
    q_c, k_c, v_c = parts_ctx
    q_l, k_l, v_l = parts_lat
    B, L = q_l.shape[:2]
    C = q_c.shape[1]
    scale = HEAD_DIM ** -0.5
    ql = axial_rope(_heads(q_l, SWA_HEADS), pos_row, pos_col)
    kl = axial_rope(_heads(k_l, SWA_KV_HEADS), pos_row, pos_col)
    vl = _heads(v_l, SWA_KV_HEADS)
    qc = _heads(q_c, SWA_HEADS).reshape(B, C, SWA_KV_HEADS, SWA_GROUP, HEAD_DIM)
    kc = _heads(k_c, SWA_KV_HEADS)
    vc = _heads(v_c, SWA_KV_HEADS)
    sink_g = sink.astype(jnp.float32).reshape(SWA_KV_HEADS, SWA_GROUP)[None, :, :, None, None]
    pad = ((0, 0), (SWA_BLOCK, SWA_BLOCK), (0, 0), (0, 0))
    kp, vp = jnp.pad(kl, pad), jnp.pad(vl, pad)
    offs_q = jnp.arange(SWA_BLOCK)
    offs_k = jnp.arange(3 * SWA_BLOCK) - SWA_BLOCK

    def block(i):
        start = i * SWA_BLOCK
        qb = lax.dynamic_slice_in_dim(ql, start, SWA_BLOCK, axis=1).reshape(B, SWA_BLOCK, SWA_KV_HEADS, SWA_GROUP, HEAD_DIM)
        kb = lax.dynamic_slice_in_dim(kp, start, 3 * SWA_BLOCK, axis=1)
        vb = lax.dynamic_slice_in_dim(vp, start, 3 * SWA_BLOCK, axis=1)
        qpos = start + offs_q
        kpos = start + offs_k
        mask = (jnp.abs(qpos[:, None] - kpos[None, :]) <= SWA_WINDOW) & (kpos >= 0)[None, :] & (kpos < L)[None, :]
        s_loc = jnp.einsum('bqkgd,bskd->bkgqs', qb, kb).astype(jnp.float32) * scale
        s_loc = jnp.where(mask, s_loc, -jnp.inf)
        s_ctx = jnp.einsum('bqkgd,bskd->bkgqs', qb, kc).astype(jnp.float32) * scale
        p_loc, p_ctx = joint_softmax([s_loc, s_ctx], sink_g)
        o = jnp.einsum('bkgqs,bskd->bqkgd', p_loc.astype(vb.dtype), vb) + jnp.einsum('bkgqs,bskd->bqkgd', p_ctx.astype(vc.dtype), vc)
        return o.reshape(B, SWA_BLOCK, SWA_HEADS * HEAD_DIM)

    o_lat = lax.map(block, jnp.arange(L // SWA_BLOCK))
    o_lat = o_lat.transpose(1, 0, 2, 3).reshape(B, L, SWA_HEADS * HEAD_DIM).astype(q_l.dtype)
    o_ctx = None
    if need_ctx:
        s = jnp.einsum('bqkgd,bskd->bkgqs', qc, kc).astype(jnp.float32) * scale
        (p,) = joint_softmax([s], sink_g)
        o_ctx = jnp.einsum('bkgqs,bskd->bqkgd', p.astype(vc.dtype), vc).reshape(B, C, SWA_HEADS * HEAD_DIM).astype(q_c.dtype)
    return o_lat, o_ctx

def natten_mixer(parts_ctx, parts_lat, rpb, need_ctx):
    q_c, k_c, v_c = parts_ctx
    q_l, k_l, v_l = parts_lat
    B, L = q_l.shape[:2]
    C = q_c.shape[1]
    rows = L // GRID_W
    wr = min(NAT_ROWS, rows)
    scale = HEAD_DIM ** -0.5
    qg = _heads(q_l, NAT_HEADS).reshape(B, rows, GRID_W, NAT_HEADS, HEAD_DIM)
    kg = _heads(k_l, NAT_HEADS).reshape(B, rows, GRID_W, NAT_HEADS, HEAD_DIM)
    vg = _heads(v_l, NAT_HEADS).reshape(B, rows, GRID_W, NAT_HEADS, HEAD_DIM)
    qc, kc, vc = _heads(q_c, NAT_HEADS), _heads(k_c, NAT_HEADS), _heads(v_c, NAT_HEADS)
    n_cb = GRID_W // NAT_QCOLS
    qcol = np.arange(GRID_W).reshape(n_cb, NAT_QCOLS)
    slab_start = np.clip(np.arange(n_cb) * NAT_QCOLS - NAT_COLS // 2, 0, GRID_W - NAT_SLAB)
    slab_cols = slab_start[:, None] + np.arange(NAT_SLAB)
    win_start = np.clip(qcol - NAT_COLS // 2, 0, GRID_W - NAT_COLS)
    col_mask = (slab_cols[:, None, :] >= win_start[..., None]) & (slab_cols[:, None, :] < win_start[..., None] + NAT_COLS)
    col_idx = slab_cols[:, None, :] - qcol[..., None] + NAT_COLS - 1
    col_mask_b = jnp.asarray(col_mask)[:, :, None, :]
    rpb = rpb.astype(jnp.float32)

    def row_block(r):
        rs = jnp.clip(r - wr // 2, 0, rows - wr)
        q_r = lax.dynamic_index_in_dim(qg, r, axis=1, keepdims=False).reshape(B, n_cb, NAT_QCOLS, NAT_HEADS, HEAD_DIM)
        k_slab = lax.dynamic_slice_in_dim(kg, rs, wr, axis=1)[:, :, slab_cols]
        v_slab = lax.dynamic_slice_in_dim(vg, rs, wr, axis=1)[:, :, slab_cols]
        s = jnp.einsum('bjqhd,brjkhd->bhjqrk', q_r, k_slab).astype(jnp.float32) * scale
        row_idx = rs + jnp.arange(wr) - r + NAT_ROWS - 1
        bias = rpb[:, row_idx[None, None, :, None], col_idx[:, :, None, :]]
        s = jnp.where(col_mask_b, s + bias[None], -jnp.inf)
        s = s.reshape(B, NAT_HEADS, n_cb, NAT_QCOLS, wr * NAT_SLAB)
        s_ctx = jnp.einsum('bjqhd,bshd->bhjqs', q_r, kc).astype(jnp.float32) * scale
        p_loc, p_ctx = joint_softmax([s, s_ctx])
        p_loc = p_loc.reshape(B, NAT_HEADS, n_cb, NAT_QCOLS, wr, NAT_SLAB)
        o = jnp.einsum('bhjqrk,brjkhd->bjqhd', p_loc.astype(v_slab.dtype), v_slab) + jnp.einsum('bhjqs,bshd->bjqhd', p_ctx.astype(vc.dtype), vc)
        return o.reshape(B, GRID_W, NAT_HEADS * HEAD_DIM)

    o_lat = lax.map(row_block, jnp.arange(rows))
    o_lat = o_lat.transpose(1, 0, 2, 3).reshape(B, L, NAT_HEADS * HEAD_DIM).astype(q_l.dtype)
    o_ctx = None
    if need_ctx:
        s = jnp.einsum('bqhd,bshd->bhqs', qc, kc).astype(jnp.float32) * scale
        (p,) = joint_softmax([s])
        o_ctx = jnp.einsum('bhqs,bshd->bqhd', p.astype(vc.dtype), vc).reshape(B, C, NAT_HEADS * HEAD_DIM).astype(q_c.dtype)
    return o_lat, o_ctx

def peer_ffn(h, wq, subkeys, u_tab, v_tab):
    T, D = h.shape

    def block(hb):
        q = (hb @ wq).reshape(PEER_BLOCK, PEER_HEADS, 2, PEER_DK // 2)
        s = jnp.einsum('thpd,hpnd->thpn', q, subkeys).astype(jnp.float32)
        top_s, top_i = lax.top_k(s, PEER_TOPK)
        cand_s = (top_s[:, :, 0, :, None] + top_s[:, :, 1, None, :]).reshape(PEER_BLOCK, PEER_HEADS, PEER_TOPK * PEER_TOPK)
        cand_i = (top_i[:, :, 0, :, None] * PEER_NKEYS + top_i[:, :, 1, None, :]).reshape(PEER_BLOCK, PEER_HEADS, PEER_TOPK * PEER_TOPK)
        best_s, pos = lax.top_k(cand_s, PEER_TOPK)
        idx = jnp.take_along_axis(cand_i, pos, axis=-1)
        g = jax.nn.softmax(best_s, axis=-1)
        a = jax.nn.gelu(jnp.einsum('td,thkd->thk', hb, u_tab[idx]).astype(jnp.float32), approximate=False)
        return jnp.einsum('thk,thkd->td', (g * a).astype(hb.dtype), v_tab[idx])

    return lax.map(block, h.reshape(T // PEER_BLOCK, PEER_BLOCK, D)).reshape(T, D)

def setup_inputs(seed: int = 0) -> dict:
    key = jax.random.key(seed)
    ks = jax.random.split(key, 19)
    D = D_MODEL

    def n(k, shape, s):
        return jax.random.normal(k, shape, jnp.float32) * s

    return {
        "x": n(ks[0], (BATCH, SEQ, D), 1.0),
        "c": n(ks[1], (BATCH, D), 1.0),
        "ctx": n(ks[2], (BATCH, CTX_LEN, D), 1.0),
        "c_ctx": n(ks[3], (D,), 1.0),
        "w_mod": n(ks[4], (DEPTH, D, 6 * D), 0.5 * D ** -0.5),
        "b_mod": n(ks[5], (DEPTH, 6 * D), 0.01),
        "norm_mix_w": 1.0 + n(ks[6], (DEPTH, D), 0.02),
        "norm_ffn_w": 1.0 + n(ks[7], (DEPTH, D), 0.02),
        "w_in": n(ks[8], (DEPTH, D, PROJ_WIDTH), D ** -0.5),
        "hgrn_lb_logits": n(ks[9], (2, DEPTH, HG_WIDTH), 0.5),
        "hgrn_norm_w": 1.0 + n(ks[10], (DEPTH, HG_WIDTH), 0.02),
        "swa_sink": n(ks[11], (DEPTH, SWA_HEADS), 1.0),
        "nat_rpb": n(ks[12], (DEPTH, NAT_HEADS, 2 * NAT_ROWS - 1, 2 * NAT_COLS - 1), 0.5),
        "w_out": n(ks[13], (DEPTH, MIX_WIDTH, D), MIX_WIDTH ** -0.5),
        "peer_wq": n(ks[14], (DEPTH, D, PEER_HEADS * PEER_DK), D ** -0.5),
        "peer_subkeys": n(ks[15], (DEPTH, PEER_HEADS, 2, PEER_NKEYS, PEER_DK // 2), (PEER_DK // 2) ** -0.5),
        "peer_u": n(ks[16], (DEPTH, PEER_EXPERTS, D), D ** -0.5),
        "peer_v": n(ks[17], (DEPTH, PEER_EXPERTS, D), 0.5),
        "final_norm_w": 1.0 + n(ks[18], (D,), 0.02),
    }

def reference(x, c, ctx, c_ctx, w_mod, b_mod, norm_mix_w, norm_ffn_w, w_in, hgrn_lb_logits, hgrn_norm_w,
              swa_sink, nat_rpb, w_out, peer_wq, peer_subkeys, peer_u, peer_v, final_norm_w):
    B, L, D = x.shape
    C = ctx.shape[1]
    pos = jnp.arange(L)
    pos_row, pos_col = pos // GRID_W, pos % GRID_W
    lb = jnp.cumsum(jax.nn.softmax(hgrn_lb_logits.astype(jnp.float32), axis=1), axis=1)
    lb = lb - lb[:, :1]
    xc = ctx
    s_c = jax.nn.silu(c)
    s_cc = jax.nn.silu(c_ctx)
    for l in range(DEPTH):
        last = l == DEPTH - 1
        need_ctx = not last
        mod = jnp.split(s_c @ w_mod[l] + b_mod[l], 6, axis=-1)
        mod_c = jnp.split(s_cc @ w_mod[l] + b_mod[l], 6, axis=-1)
        h = modulate(rms_norm(x, norm_mix_w[l]), mod[0][:, None], mod[1][:, None])
        hc = modulate(rms_norm(xc, norm_mix_w[l]), mod_c[0], mod_c[1])
        pl = split_proj(h @ w_in[l])
        pc = split_proj(hc @ w_in[l])
        a_l, a_c = hgrn2_mixer(pc[:5], pl[:5], lb[0, l], lb[1, l], hgrn_norm_w[l], need_ctx)
        b_l, b_c = swa_mixer(pc[5:8], pl[5:8], swa_sink[l], pos_row, pos_col, need_ctx)
        n_l, n_c = natten_mixer(pc[8:], pl[8:], nat_rpb[l], need_ctx)
        x = x + mod[2][:, None] * (jnp.concatenate([a_l, b_l, n_l], axis=-1) @ w_out[l])
        if need_ctx:
            xc = xc + mod_c[2] * (jnp.concatenate([a_c, b_c, n_c], axis=-1) @ w_out[l])
        h = modulate(rms_norm(x, norm_ffn_w[l]), mod[3][:, None], mod[4][:, None])
        if need_ctx:
            hc = modulate(rms_norm(xc, norm_ffn_w[l]), mod_c[3], mod_c[4])
            tokens = jnp.concatenate([hc.reshape(B * C, D), h.reshape(B * L, D)], axis=0)
            y_all = peer_ffn(tokens, peer_wq[l], peer_subkeys[l], peer_u[l], peer_v[l])
            xc = xc + mod_c[5] * y_all[:B * C].reshape(B, C, D)
            y = y_all[B * C:].reshape(B, L, D)
        else:
            y = peer_ffn(h.reshape(B * L, D), peer_wq[l], peer_subkeys[l], peer_u[l], peer_v[l]).reshape(B, L, D)
        x = x + mod[5][:, None] * y
    return rms_norm(x, final_norm_w)


_drawn_inputs = setup_inputs


def setup_inputs(seed=0):
    import zlib

    import numpy as np

    out = dict(_drawn_inputs(seed))
    spreads = {}
    factors = {'b_mod': 3.154,
     'norm_mix_w': 6.19,
     'norm_ffn_w': 12.89,
     'hgrn_lb_logits': 6.305,
     'hgrn_norm_w': 7.176,
     'swa_sink': 8.0,
     'nat_rpb': 3.878,
     'final_norm_w': 8.366}
    for name, (base, spread) in spreads.items():
        noise = np.random.default_rng([zlib.crc32(name.encode()), seed]).standard_normal(out[name].shape)
        drawn = base * np.exp(spread * noise) if base else spread * noise
        out[name] = __import__('jax').numpy.asarray(drawn.astype(out[name].dtype))
    for name, factor in factors.items():
        out[name] = (out[name] * factor).astype(out[name].dtype)
    return out
```

```python
import numpy as np
import concourse.bass as bass
from concourse import mybir
from contextlib import ExitStack, contextmanager

D = 1024
P = 128
KD = D // P
CTX, SEQ, DEPTH = 256, 512, 2
TOK = CTX + SEQ
NB = TOK // P
CB = CTX // P
GRID_W, GRID_H = 64, SEQ // 64
HD = 64
SWA_H, SWA_KV, NAT_H = 6, 2, 6
NAT_ROWS, NAT_COLS = 8, 16
HEADS, PK, NK, TOPK = 8, 128, 128, 16
TW = 256
SLOTS = 4
TILE_F = KD * TW
MOD_TILES, IN_TILES, OUT_TILES, WQ_TILES = 24, 12, 4, 8
PASS = 2 * P
LEVELS = 7
EPS = 1e-6
NEG = -1e30

F32 = mybir.dt.float32
U32 = mybir.dt.uint32
U8 = mybir.dt.uint8
ALU = mybir.AluOpType
ACT = mybir.ActivationFunctionType
AX = mybir.AxisListType.X


def passes_of(layer):
    return range(0 if layer < DEPTH - 1 else CB, NB, 2)


def first_block(layer):
    return 0 if layer < DEPTH - 1 else CB


class Chain:

    def __init__(self, eng, sem):
        self.eng, self.sem, self.n, self.term = eng, sem, 0, 0

    def __call__(self, ins):
        ins.then_inc(self.sem, 1)
        self.n += 1
        self.eng.wait_ge(self.sem, self.term + self.n if not isinstance(self.term, int) else self.n + self.term)

    @contextmanager
    def loop(self, count, per):
        base, outer = self.n, self.term
        with self.eng.Fori(0, count) as i:
            self.term = i * per + outer
            yield i
            assert self.n - base == per, f"{self.n - base} links in a body of {per}"
        self.term, self.n = outer, base + count * per


def build(nc, d, out):
    with ExitStack() as ctx:
        def sb(name, shape, dt=F32):
            return ctx.enter_context(nc.sbuf_tensor(name, shape, dt))

        def sem(name):
            return ctx.enter_context(nc.semaphore(name))

        x = sb("x", [P, NB, D])
        ring = sb("ring", [P, SLOTS, TILE_F])
        ident = sb("ident", [P, P])
        iota = sb("iota", [P, P])
        sT = sb("sT", [P, KD, 2])
        modp = sb("modp", [P, 4 * KD, 2])
        modA = sb("modA", [P, 2, KD, 2])
        small = sb("small", [P, 160])
        arena = sb("arena", [P, 38000])

        def view(start, *dims):
            size = int(np.prod(dims))
            assert start + size <= 38000
            names = "abcde"[:len(dims)]
            spec = " ".join(names)
            flat = arena[:, start:start + size]
            if len(dims) == 1:
                return flat
            return flat.rearrange(f"p ({spec}) -> p {spec}", **dict(zip(names, dims)))

        bT = small[:, 0:64].rearrange("p (n s) -> p n s", s=2)
        nw = small[:, 64:64 + 16].rearrange("p (n k) -> p n k", n=2)
        ss = small[:, 80:82]
        rs = small[:, 82:84]
        lbx = small[:, 84:92].rearrange("p (d q l) -> p d q l", d=2, q=2)
        lbc = small[:, 92:100].rearrange("p (d q v) -> p d q v", d=2, q=2)
        lbt = small[:, 100:108].rearrange("p (d q l) -> p d q l", d=2, q=2)
        sink = small[:, 108:114]
        nm = small[:, 114:116]
        rsum = small[:, 116:118]
        esink = small[:, 118:120]
        rden = small[:, 120:122]
        lbst = small[:, 122:126].rearrange("p (d v) -> p d v", d=2)
        mxs = small[:, 126:128]
        den = small[:, 128:130]
        sinkst = small[:, 158:159]
        c0 = small[:, 130:146].rearrange("p (k s) -> p k s", s=2)

        hT = view(0, KD, TOK)
        mix = view(6144, NB, D)
        hgF = view(12288, 6, TOK)
        hvg = view(16896, NB, 512)
        W = 19968
        z_s, q_s, k_s, lf_s, t_s = (view(W + i * TOK, TOK) for i in range(5))
        Bx = view(W + 5 * TOK, NB, P + 1)
        W2 = W + 5 * TOK + NB * (P + 1)
        Dl = [view(W2 + i * TOK, TOK) for i in range(2)]
        Qt = [view(W2 + (2 + i) * TOK, TOK) for i in range(2)]
        Kt = [view(W2 + (4 + i) * TOK, TOK) for i in range(2)]
        Asc = view(W2 + 6 * TOK, 2, NB, P)
        Qh, Kh, KhT = (view(W2 + (8 + i) * TOK, TOK) for i in range(3))
        Ub = view(W2 + 11 * TOK, NB, 64)
        Sh = view(W2 + 11 * TOK + NB * 64, NB, 64)
        Fd = view(W2 + 12 * TOK, NB)
        ones = view(W2 + 12 * TOK + 8, P)
        gS = view(W, NB, 256)
        gT = view(W + 1536, NB, 256)
        rr = view(W + 3072, NB, 4)
        CST = 38000 - 1600
        masks = arena[:, CST:CST + 512].bitcast(U8).rearrange("p (d l t) -> p d l t", d=2, l=LEVELS + 1)
        cosT = view(CST + 512, 4, 32)
        sinT = view(CST + 640, 4, 32)
        swam = view(CST + 768, 2, P)
        natm = view(CST + 1024, GRID_W)
        hnw = view(CST + 1088, 256)

        q12 = view(12288, 12 * TOK)
        k8 = view(21504, 8 * TOK)
        v8 = view(27648, NB, 512)
        sqk = view(30720, NB, 512)
        rq = view(33792, 512)
        rt = view(34304, 512)
        qst = view(30720, TOK)
        Pm = [view(31488 + i * TOK, TOK) for i in range(2)]
        PT = [view(33024 + i * TOK, TOK) for i in range(2)]
        biast = [view(34560 + i * 512, 512) for i in range(2)]
        mixT = hT
        gateb = view(12288, 2, D)
        ytmp = view(14336, TW)
        grow = view(0, 2048)
        brow = view(2048, 2048)
        xn = [view(6144 + i * D, D) for i in range(2)]

        G = view(0, PK, PASS)
        hP = view(32768, KD, PASS)
        kT = view(34816, 3, PASS)
        oneA = view(35584, 8, P)
        oneB = view(36608, 8, P)
        gel = [view(35584 + i * PASS, PASS) for i in range(2)]
        gat = [view(36096 + i * PASS, PASS) for i in range(2)]
        xp = [view(16384 + i * D, D) for i in range(2)]
        qP = view(0, 16, PASS)
        subk = view(4096, 16, P)
        sc = view(6144, 16, P)
        sc2 = view(8192, 16, P)
        cand = view(10240, HEADS, 256)
        cand2 = view(12288, HEADS, 256)
        eq = view(14336, HEADS, TOPK, TOPK)
        tv = view(20480, 16, TOPK)
        tif = view(20736, 16, TOPK)
        tiu = arena[:, 20992:21248].bitcast(U32).rearrange("p (a b) -> p a b", a=16)
        bs = view(21248, HEADS, TOPK)
        pu = arena[:, 21376:21504].bitcast(U32).rearrange("p (a b) -> p a b", a=HEADS)
        pa = arena[:, 21504:21632].bitcast(U32).rearrange("p (a b) -> p a b", a=HEADS)
        paf = view(21632, HEADS, TOPK)
        pbf = view(21760, HEADS, TOPK)
        sel = view(21888, 3, P)
        gs1 = view(22272, HEADS)
        gbP = view(0, D)
        yP = view(1024, D)

        PS = [ctx.enter_context(nc.psum_tensor(f"PS{i}", [P, 1024], F32)) for i in range(4)]
        bank = [PS[i // 2][:, 512 * (i % 2):512 * (i % 2) + 512] for i in range(8)]

        s = {n: sem(n) for n in (
            "consts_in", "x_in", "stage_end", "slot_free", "dve_chain", "act_chain",
            "layer_in", "mod_done", "gates_out", "gate_in", "silu_done",
            "sq_done", "var_ready", "rms_ready", "xn_ready", "xT_done", "hT_act", "hT_dve",
            "proj_done", "ev_act", "ev_dve",
            "hg_absz", "hg_lsig", "hg_mix", "hg_mixed", "hg_karg", "hg_k", "hg_qarg", "hg_qexp", "hg_qk",
            "lv_diff", "lv_exp", "lv_ops", "lv_pe", "lv_used", "st_diff", "st_exp", "st_ops", "st_tr", "st_kht",
            "st_u", "st_hist", "st_out", "st_saved", "ro_ms", "ro_r", "ro_garg", "ro_g",
            "rope_ready", "rope_T", "rope_used",
            "q_staged", "scores_done", "max_ready", "exp_done", "trans_done", "pt_ready", "pv_done", "norm_done",
            "bias_used", "bias_in0", "bias_in1", "bias_ready",
            "mixT_done", "mixT_used", "y_done", "y_used",
            "pq_done", "pq_used", "set_v", "set_a", "sub_in", "s_done", "s_used", "gexp", "gready", "sel_ready", "selT_done", "selT_used",
            "one_ready", "one_used", "g_used", "hu_done", "gelu_done", "gated", "y_acc", "x_out", "fin_ready", "fin_out0", "fin_out1", "nrm_in")}
        w_ready = [sem(f"w_ready{i}") for i in range(SLOTS)]
        block = ctx.enter_context(nc.Block())
        N_STAGED = 4

        def stage_end(eng, tally, name):
            tally["stage"] = tally.get("stage", 0) + 1
            eng.drain().then_inc(s["stage_end"], 1)
            eng.wait_ge(s["stage_end"], N_STAGED * tally["stage"])


        def staged(eng, tally):
            def end(name):
                stage_end(eng, tally, name)
            return end

        @block.sync
        def _(sp):
            tally = {"tiles": 0}

            def stream(src, count):
                base = tally["tiles"]

                def four(i, first):
                    for sl in range(SLOTS):
                        if not first:
                            sp.wait_ge(s["slot_free"], i * SLOTS + (base + sl - SLOTS + 1))
                        sp.dma_start(ring[:, sl, :], src[bass.ds(i * SLOTS + sl, 1)].rearrange("o p f -> p (o f)")
                                     ).then_inc(w_ready[sl], 16)
                if base == 0:
                    four(0, True)
                    with sp.Fori(1, count // SLOTS) as i:
                        four(i, False)
                else:
                    with sp.Fori(0, count // SLOTS) as i:
                        four(i, False)
                tally["tiles"] += count

            for l in range(DEPTH):
                stream(d["wcat"][l], MOD_TILES + IN_TILES + OUT_TILES)
                for _ in passes_of(l):
                    stream(d["wq"][l], WQ_TILES)
                    stream(d["experts"][l], PK)

        @block.gpsimd
        def _(pool):
            t = {}
            end = staged(pool, t)

            def const(dst, src):
                pool.dma_start(dst, src).then_inc(s["consts_in"], 16)

            pool.nop().then_inc(s["bias_ready"], 1)
            for dst, src in ((ident[:, :], d["ident"]), (iota[:, :], d["iota"]), (c0, d["c"]), (lbx, d["lb"])):
                const(dst, src)
            for b in range(NB):
                pool.dma_start(x[:, b, :], (d["ctx"][b * P:(b + 1) * P, :] if b < CB else
                                            d["x"][(b - CB) * P:(b - CB + 1) * P, :])).then_inc(s["x_in"], 16)
            for l in range(DEPTH):
                for dst, src in ((bT, d["bT"][l]), (nw, d["nw"][l]),
                                 (brow[0:2, :], d["bgate"][l:l + 1, :].broadcast_to([2, 2048])),
                                 (sink, d["sink"][l:l + 1, :].broadcast_to([P, SWA_H])),
                                 (arena[:, CST:CST + 512], d["masks"]), (arena[:, CST + 512:CST + 768], d["rope"]),
                                 (arena[:, CST + 768:CST + 1024], d["swam"]), (natm, d["natm"]),
                                 (hnw, d["hnw"][l:l + 1, :].broadcast_to([P, 256]))):
                    pool.dma_start(dst, src).then_inc(s["layer_in"], 16)
                pool.wait_ge(s["mod_done"], l + 1)
                pool.dma_start(d["gates"][l], grow[0:2, :]).then_inc(s["gates_out"], 16)
                pool.wait_ge(s["gates_out"], 16 * (l + 1))
                end(f"mod{l}")
                end(f"norm{l}")
                end(f"projA{l}")
                end(f"hg{l}")
                end(f"readout{l}")
                end(f"projB{l}")
                end(f"rope{l}")
                U = 4 + (CB if first_block(l) == 0 else 0)
                nbase = t.get("nat", 0)

                def bias(h, qb, wait_value):
                    pool.wait_ge(s["bias_used"], wait_value)
                    for r2 in range(2):
                        x0 = NAT_ROWS - 1 - (2 * qb + r2)
                        pool.dma_start(biast[qb % 2][64 * r2:64 * r2 + 64, :],
                                       d["rpb"][l, bass.ds(h, 1), :, x0 * 64:(x0 + 8) * 64].rearrange("o c f -> (o c) f")
                                       ).then_inc(s[f"bias_in{qb % 2}"], 16)

                def masked(h, qb):
                    pool.wait_ge(s[f"bias_in{qb % 2}"], h * 64 + (32 * (qb // 2) + 32 + 16 * nbase))
                    bt = biast[qb % 2].rearrange("p (r c) -> p r c", c=GRID_W)
                    pool.tensor_tensor(bt, bt, natm.unsqueeze(1).broadcast_to([P, 8, GRID_W]), ALU.add
                                       ).then_inc(s["bias_ready"], 1)

                ub = t.get("bu", 1)
                with pool.Fori(0, NAT_H) as h:
                    for qb in range(4):
                        bias(h, qb, h * 4 + (ub + max(qb - 1, 0)))
                        masked(h, qb)
                t["bu"] = ub + 4 * NAT_H
                t["nat"] = nbase + 4 * NAT_H
                end(f"attn{l}")
                for st in range(2):
                    pool.dma_start(gateb[:, st, :], d["gates"][l, st:st + 1, 0:D].broadcast_to([P, D])
                                   ).then_inc(s["gate_in"], 16)
                end(f"mixT{l}")
                end(f"mix{l}")
                for pn, b0 in enumerate(passes_of(l)):
                    pool.dma_start(subk, d["subk"][l]).then_inc(s["sub_in"], 16)
                    end(f"pnorm{l}{b0}")
                    end(f"pq{l}{b0}")
                    end(f"topk{l}{b0}")
                    end(f"gbuild{l}{b0}")
                    end(f"gemm{l}{b0}")
                    st = 1 if b0 < CB else 0
                    pool.dma_start(gbP, d["gates"][l, st:st + 1, D:2 * D].broadcast_to([P, D])
                                   ).then_inc(s["gate_in"], 16)
                    end(f"pres{l}{b0}")
            pool.dma_start(gbP, d["fnw"].broadcast_to([P, D])).then_inc(s["nrm_in"], 16)
            for b in range(4):
                pool.wait_ge(s["fin_ready"], b + 1)
                pool.dma_start(out[b * P:(b + 1) * P, :], xp[b % 2]).then_inc(s[f"fin_out{b % 2}"], 16)
            for b in range(2):
                pool.wait_ge(s[f"fin_out{b}"], 32)

        def pieces(kind, j):
            if j < 0:
                return [(0, 0, CTX)]
            lo, hi = (0, 4) if kind == "nat" else (max(0, j - 1), min(4, j + 2))
            n1 = min(2, hi - lo)
            res = [(0, 0, CTX), (CTX, CTX + lo * P, n1 * P)]
            if hi - lo > n1:
                res.append((CTX + n1 * P, CTX + (lo + n1) * P, (hi - lo - n1) * P))
            return res

        def units(l):
            return [-2, -1, 0, 1, 2, 3] if first_block(l) == 0 else [0, 1, 2, 3]

        def width(kind, j):
            return sum(n for _, _, n in pieces(kind, j))

        def key_blocks(kind, j):
            return [t0 // P + i for _, t0, n in pieces(kind, j) for i in range(n // P)]

        def items(tiles):
            res = []
            for t in tiles:
                if t < 3 or t >= 9:
                    res += [("feat", t, (m, h)) for m in range(2) for h in range(2)]
                else:
                    res += [("tok", t, b) for b in range(NB)]
            return res

        def evacuate(op, item, ps):
            kind, tl, part = item
            if kind == "tok":
                b = part
                dst = (hvg[:, b, (tl - 3) * TW:(tl - 2) * TW] if tl < 5 else
                       sqk[:, b, (tl - 5) * TW:(tl - 4) * TW] if tl < 7 else
                       v8[:, b, (tl - 7) * TW:(tl - 6) * TW])
                return op(dst, ps[:, 0:TW])
            m, h = part
            half = slice(h * 384, h * 384 + 384)
            if tl < 3:
                return op(hgF[:, 2 * tl + m, half], ps[:, 0:384])
            ft = 2 * (tl - 9) + m
            for e in range(2):
                if ft < 3:
                    base = (6 + 2 * ft + e) * TOK
                    dst = q12[0:64, base + h * 384:base + h * 384 + 384]
                else:
                    base = (2 + 2 * (ft - 3) + e) * TOK
                    dst = k8[0:64, base + h * 384:base + h * 384 + 384]
                last = op(dst, ps[64 * e:64 * e + 64, 0:384])
            return last

        def lv_halves(ap3, lv):
            H = 1 << lv
            v = ap3.rearrange("p c (b h) -> p c b h", h=2 * H)
            return v[:, :, :, 0:H], v[:, :, :, H:2 * H]

        def chunks3(ap):
            return ap.rearrange("p (c t) -> p c t", t=P)

        @block.tensor
        def _(pe):
            t = {"tiles": 0, "items": 0}
            end = staged(pe, t)

            def slot(sl):
                return ring[:, sl, :].rearrange("p (k c) -> p k c", k=KD)

            def tile_in(sl, i=0):
                pe.wait_ge(w_ready[sl], i * 16 + 16 * (t["tiles"] // SLOTS + 1))

            def project(tiles):
                its = items(tiles)
                for n, (kind, tl, part) in enumerate(its):
                    n += t["items"]
                    if n >= 4:
                        pe.wait_ge(s["ev_dve" if n % 2 else "ev_act"], (n - 4) // 2 + 1)
                    g = t["tiles"]
                    w = slot(g % SLOTS)
                    pe.wait_ge(w_ready[g % SLOTS], 16 * (g // SLOTS + 1))
                    for k in range(KD):
                        if kind == "feat":
                            m, h = part
                            mm = pe.matmul(bank[n % 4][:, 0:384], w[:, k, m * P:(m + 1) * P],
                                           hT[:, k, h * 384:h * 384 + 384], start=(k == 0), stop=(k == KD - 1))
                        else:
                            mm = pe.matmul(bank[n % 4][:, 0:TW], hT[:, k, part * P:(part + 1) * P], w[:, k, :],
                                           start=(k == 0), stop=(k == KD - 1))
                    mm.then_inc(s["proj_done"], 1)
                    if n - t["items"] + 1 == len(its) or its[n - t["items"] + 1][1] != tl:
                        pe.wait_ge(s["proj_done"], n + 1)
                        pe.nop().then_inc(s["slot_free"], 1)
                        t["tiles"] += 1
                t["items"] += len(its)

            def norm(nblk):
                base = t.get("norm", 0)
                for i in range(nblk):
                    n = base + i
                    pe.wait_ge(s["xn_ready"], n + 1)
                    if n >= 1:
                        pe.wait_ge(s["hT_act"], n)
                        pe.wait_ge(s["hT_dve"], n)
                    for k in range(KD):
                        mm = pe.transpose(bank[k // 4][:, (k % 4) * P:(k % 4 + 1) * P],
                                          t["xn"][i % 2][:, k * P:(k + 1) * P], ident[:, :])
                    mm.then_inc(s["xT_done"], 1)
                t["norm"] = base + nblk

            def attention(kind, l, head, first, last_g):
                us = units(l)
                def scores(i):
                    j = us[i]
                    if i == 0 or kind == "nat":
                        pe.wait_ge(s["rope_ready"], 4 * (l + 1))
                        pe.wait_ge(s["q_staged"], last_g)
                    if i >= 2:
                        pe.wait_ge(s["exp_done"], first + (i - 1))
                    for c, t0, n in pieces(kind, j):
                        if kind == "swa":
                            rhs = k8[0:64, (head // 3) * TOK + t0:(head // 3) * TOK + t0 + n]
                        else:
                            rhs = k8[0:64, bass.ds(head * TOK + (2 * TOK + t0), n)]
                        mm = pe.matmul(PS[i % 2][:, c:c + n], qst[0:64, (j + 2) * P:(j + 3) * P], rhs,
                                       start=True, stop=True)
                    mm.then_inc(s["scores_done"], 1)

                def trans(i):
                    pe.wait_ge(s["exp_done"], first + (i + 1))
                    if i >= 1:
                        pe.wait_ge(s["pt_ready"], first + i)
                    for c in range(width(kind, us[i]) // P):
                        mm = pe.transpose(PS[2][:, c * P:(c + 1) * P], Pm[i % 2][:, c * P:(c + 1) * P], ident[:, :])
                    mm.then_inc(s["trans_done"], 1)

                def values(i):
                    pe.wait_ge(s["pt_ready"], first + (i + 1))
                    pe.wait_ge(s["norm_done"], first + max(i - 1, 0))
                    kb = key_blocks(kind, us[i])
                    for c, b in enumerate(kb):
                        if kind == "swa":
                            rhs = v8[:, b, (head // 3) * 64:(head // 3) * 64 + 64]
                        else:
                            rhs = v8[:, b, bass.ds(head * 64 + 128, 64)]
                        mm = pe.matmul(bank[6 + i % 2][:, 0:64], PT[i % 2][:, c * P:(c + 1) * P], rhs,
                                       start=(c == 0), stop=(c == len(kb) - 1))
                    mm.then_inc(s["pv_done"], 1)

                n = len(us)
                scores(0)
                for i in range(n + 1):
                    if i + 1 < n:
                        scores(i + 1)
                    if i < n:
                        trans(i)
                    if i >= 1:
                        values(i - 1)

            for name in ("scores_done", "trans_done", "pv_done"):
                pe.nop().then_inc(s[name], 1)
            pe.wait_ge(s["consts_in"], 64)
            for l in range(DEPTH):
                fb = first_block(l)
                pe.wait_ge(s["silu_done"], 1)
                with pe.Fori(0, 4) as i:
                    for sl in range(SLOTS):
                        tile_in(sl, i)
                        for m in range(2):
                            for k in range(KD):
                                mm = pe.matmul(bank[0][:, bass.ds(i * 16 + (sl * 4 + m * 2), 2)],
                                               slot(sl)[:, k, m * P:(m + 1) * P], sT[:, k, :],
                                               start=(k == 0), stop=(k == KD - 1))
                        mm.then_inc(s["slot_free"], 1)
                t["tiles"] += 16
                for half in range(2):
                    for sl in range(SLOTS):
                        tile_in(sl)
                        c = sl * TW
                        for k in range(KD):
                            mm = pe.matmul(PS[1 + half][0:2, c:c + TW], sT[:, k, :],
                                           slot(sl)[:, k, :], start=(k == 0), stop=(k == KD - 1))
                        mm.then_inc(s["slot_free"], 1)
                    t["tiles"] += 4
                end(f"mod{l}")
                t["xn"] = xn
                norm(NB)
                end(f"norm{l}")
                project(range(0, 5))
                end(f"projA{l}")

                with pe.Fori(0, 2) as pr:
                    for dr in range(2):
                        def n_(per_dir, k):
                            return pr * (2 * per_dir) + (4 * l + dr) * per_dir + k

                        pe.wait_ge(s["hg_qk"], n_(1, 1))
                        pe.wait_ge(s["hg_k"], n_(1, 1))
                        for lv in range(LEVELS + 1):
                            if lv < LEVELS:
                                pe.wait_ge(s["lv_ops"], n_(LEVELS, lv + 1))
                            if lv >= 2:
                                pe.wait_ge(s["lv_used"], n_(LEVELS + 1, lv - 1))
                            kk, qq = (Kt[lv % 2], Qt[lv % 2]) if lv < LEVELS else (k_s, q_s)
                            for e in range(2):
                                for c in range(NB):
                                    mm = pe.matmul(PS[2 * (lv % 2) + e][:, c * P:(c + 1) * P],
                                                   kk[64 * e:64 * e + 64, c * P:(c + 1) * P],
                                                   qq[64 * e:64 * e + 64, c * P:(c + 1) * P], start=True, stop=True)
                            mm.then_inc(s["lv_pe"], 1)
                        pe.wait_ge(s["st_ops"], n_(1, 1))
                        pe.wait_ge(s["lv_used"], n_(LEVELS + 1, LEVELS + 1))
                        for c in range(NB):
                            mm = pe.transpose(PS[0][:, c * P:(c + 1) * P], Kh[:, c * P:(c + 1) * P], ident[:, :])
                        mm.then_inc(s["st_tr"], 1)
                        pe.wait_ge(s["st_kht"], n_(1, 1))
                        for c in range(NB):
                            mm = pe.matmul(PS[1][:, c * P:(c + 1) * P], KhT[:, c * P:(c + 1) * P],
                                           hvg[:, c, bass.ds(pr * P, P)], start=True, stop=True)
                        mm.then_inc(s["st_u"], 1)
                        pe.wait_ge(s["st_hist"], n_(1, 1))
                        order = [0, 1, 2, 3, 4, 5] if dr == 0 else [1, 0, 5, 4, 3, 2]
                        for e in range(2):
                            for n, c in enumerate(order):
                                if c < fb:
                                    continue
                                pe.matmul(bank[4 + e][:, c * 64:c * 64 + 64], Asc[:, e, c, :],
                                          hvg[:, c, bass.ds(pr * P + 64 * e, 64)], start=True, stop=False)
                                mm = pe.matmul(bank[4 + e][:, c * 64:c * 64 + 64],
                                               Qh[64 * e:64 * e + 64, c * P:(c + 1) * P],
                                               Sh[64 * e:64 * e + 64, n, :], start=False, stop=True)
                        mm.then_inc(s["st_out"], 1)
                        pe.wait_ge(s["st_saved"], n_(1, 1))
                end(f"hg{l}")
                end(f"readout{l}")
                project(range(5, 12))
                end(f"projB{l}")
                base = t.get("rope", 0)
                for b in range(NB):
                    n = base + b
                    if b >= CB:
                        pe.wait_ge(s["rope_ready"], 4 * l + b - CB + 1)
                    if n >= 1:
                        pe.wait_ge(s["rope_used"], n)
                    src = sqk[:, b, :] if b < CB else rq
                    for m in range(4):
                        mm = pe.transpose(bank[0][:, m * P:(m + 1) * P], src[:, m * P:(m + 1) * P], ident[:, :])
                    mm.then_inc(s["rope_T"], 1)
                t["rope"] = base + NB
                end(f"rope{l}")
                U = len(units(l))
                u0, h0 = t.get("units", 1), t.get("heads", 0)
                for kv in range(SWA_KV):
                    with pe.Fori(0, 3) as g:
                        attention("swa", l, kv * 3, g * U + (u0 + kv * 3 * U), g + (h0 + kv * 3 + 1))
                with pe.Fori(0, NAT_H) as h:
                    attention("nat", l, h, h * U + (u0 + 6 * U), h + (h0 + 7))
                t["units"], t["heads"] = u0 + 12 * U, h0 + 12
                end(f"attn{l}")
                base = t.get("mixb", 0)
                for i, b in enumerate(range(fb, NB)):
                    n = base + i
                    if n >= 1:
                        pe.wait_ge(s["mixT_used"], 2 * n)
                    for k in range(KD):
                        mm = pe.transpose(bank[k // 4][:, (k % 4) * P:(k % 4 + 1) * P],
                                          mix[:, b, k * P:(k + 1) * P], ident[:, :])
                    mm.then_inc(s["mixT_done"], 1)
                t["mixb"] = base + NB - fb
                end(f"mixT{l}")
                base = t.get("y", 0)
                for tl in range(OUT_TILES):
                    g = t["tiles"]
                    pe.wait_ge(w_ready[g % SLOTS], 16 * (g // SLOTS + 1))
                    for i, b in enumerate(range(fb, NB)):
                        n = base + tl * (NB - fb) + i
                        if n >= 4:
                            pe.wait_ge(s["y_used"], n - 3)
                        for k in range(KD):
                            mm = pe.matmul(bank[n % 4][:, 0:TW], mixT[:, k, b * P:(b + 1) * P],
                                           slot(g % SLOTS)[:, k, :], start=(k == 0), stop=(k == KD - 1))
                        mm.then_inc(s["y_done"], 1)
                    pe.wait_ge(s["y_done"], n + 1)
                    pe.nop().then_inc(s["slot_free"], 1)
                    t["tiles"] += 1
                t["y"] = base + OUT_TILES * (NB - fb)
                end(f"mix{l}")

                for b0 in passes_of(l):
                    t["xn"] = xp
                    norm(2)
                    end(f"pnorm{l}{b0}")
                    ps_ = t.get("pass", 0)
                    qb = 16 * ps_
                    with pe.Fori(0, WQ_TILES // SLOTS) as i:
                        for sl in range(SLOTS):
                            tile_in(sl, i)
                            w = ring[:, sl, :].rearrange("p (m k c) -> p m k c", m=2, k=KD)
                            for m in range(2):
                                n = sl * 2 + m
                                if n >= 4:
                                    pe.wait_ge(s["pq_used"], i * 8 + (qb + n - 3))
                                for k in range(KD):
                                    mm = pe.matmul(bank[n % 4][:, 0:PASS], w[:, m, k, :], hP[:, k, :],
                                                   start=(k == 0), stop=(k == KD - 1))
                                mm.then_inc(s["pq_done"], 1)
                            pe.wait_ge(s["pq_done"], i * 8 + (qb + sl * 2 + 2))
                            pe.nop().then_inc(s["slot_free"], 1)
                        pe.wait_ge(s["pq_used"], i * 8 + (qb + 8))
                    t["tiles"] += WQ_TILES
                    end(f"pq{l}{b0}")
                    pe.wait_ge(s["sub_in"], 16 * (ps_ + 1))
                    for tb in range(2):
                        if tb:
                            pe.wait_ge(s["s_used"], 2 * ps_ + 1)
                        for hp in range(16):
                            mm = pe.matmul(bank[hp // 4][:, (hp % 4) * P:(hp % 4 + 1) * P],
                                           qP[:, hp, tb * P:(tb + 1) * P], subk[:, hp, :], start=True, stop=True)
                        mm.then_inc(s["s_done"], 1)
                        pe.wait_ge(s["sel_ready"], 2 * ps_ + tb + 1)
                        if tb:
                            pe.wait_ge(s["selT_used"], 2 * ps_ + 1)
                        for v in range(3):
                            mm = pe.transpose(bank[4][:, v * P:(v + 1) * P], sel[:, v, :], ident[:, :])
                        mm.then_inc(s["selT_done"], 1)
                    end(f"topk{l}{b0}")
                    gb = ps_ * (PASS // 4)

                    def gates_of(i, first):
                        for g in range(2):
                            pe.wait_ge(s["one_ready"], i * 2 + (gb + g + 1))
                            if not first:
                                pe.wait_ge(s["g_used"], i * 2 + (gb + g - 1))
                            for q in range(4):
                                mm = pe.matmul(bank[5 + g][:, q * P:(q + 1) * P], oneA[:, g * 4 + q, :],
                                               oneB[:, g * 4 + q, :], start=True, stop=True)
                            mm.then_inc(s["one_used"], 1)

                    gates_of(0, True)
                    with pe.Fori(1, PASS // 8) as i:
                        gates_of(i, False)
                    end(f"gbuild{l}{b0}")

                    cbase = ps_ * PK

                    def up(i, c, sl):
                        tile_in(sl, i)
                        if not (isinstance(i, int) and i == 0 and c < 2):
                            pe.wait_ge(s["gelu_done"], i * SLOTS + (cbase + c - 1))
                        u = ring[:, sl, 0:D].rearrange("p (k e) -> p k e", k=KD)
                        for k in range(KD):
                            mm = pe.matmul(bank[c % 2][:, 0:PASS], u[:, k, :], hP[:, k, :],
                                           start=(k == 0), stop=(k == KD - 1))
                        mm.then_inc(s["hu_done"], 1)

                    def down(i, c, sl, start=False, stop=False):
                        pe.wait_ge(s["gated"], i * SLOTS + (cbase + c + 1))
                        for tb in range(2):
                            for h in range(2):
                                mm = pe.matmul(bank[4 + 2 * tb + h], gat[c % 2][:, tb * P:(tb + 1) * P],
                                               ring[:, sl, D + 512 * h:D + 512 * h + 512], start=start, stop=stop)
                        mm.then_inc(s["slot_free"], 1)

                    def group(i, first, last):
                        for sl in range(SLOTS):
                            if sl < SLOTS - 1:
                                up(i, sl + 1, sl + 1)
                            elif not last:
                                up(i + 1, 0, 0)
                            down(i, sl, sl, first and sl == 0, last and sl == SLOTS - 1)

                    up(0, 0, 0)
                    group(0, True, False)
                    with pe.Fori(1, PK // SLOTS - 1) as i:
                        group(i, False, False)
                    group(PK // SLOTS - 1, False, True)
                    t["tiles"] += PK
                    t["pass"] = ps_ + 1
                    end(f"gemm{l}{b0}")
                    end(f"pres{l}{b0}")

        @block.scalar
        def _(act):
            t = {"items": 0}
            end = staged(act, t)
            link = Chain(act, s["act_chain"])

            def norm(blocks, nidx, bufs, dst):
                base = t.get("norm", 0)

                def pre(i):
                    n = base + i
                    if i >= 2:
                        act.wait_ge(s["xT_done"], n - 1)
                    act.activation(bufs[i % 2], x[:, blocks[i], :], ACT.Square,
                                   accum_out=ss[:, i % 2:i % 2 + 1]).then_inc(s["sq_done"], 1)
                    act.wait_ge(s["var_ready"], n + 1)
                    link(act.activation(rs[:, i % 2:i % 2 + 1], ss[:, i % 2:i % 2 + 1], ACT.Ln))
                    act.activation(rs[:, i % 2:i % 2 + 1], rs[:, i % 2:i % 2 + 1], ACT.Exp, scale=-0.5
                                   ).then_inc(s["rms_ready"], 1)

                pre(0)
                for i, b in enumerate(blocks):
                    if i + 1 < len(blocks):
                        pre(i + 1)
                    st = 1 if b < CB else 0
                    act.wait_ge(s["xT_done"], base + i + 1)
                    for k in range(4):
                        last = act.activation(dst[:, k, i * P:(i + 1) * P], bank[0][:, k * P:(k + 1) * P], ACT.Identity,
                                              scale=modA[:, nidx, k, st:st + 1], bias=modp[:, nidx * 16 + k, st:st + 1])
                    last.then_inc(s["hT_act"], 1)
                t["norm"] = base + len(blocks)

            def project(tiles):
                its = items(tiles)
                for n, it in enumerate(its):
                    n += t["items"]
                    if n % 2 == 0:
                        act.wait_ge(s["proj_done"], n + 1)
                        evacuate(lambda dd, ss_: act.activation(dd, ss_, ACT.Copy), it, bank[n % 4]
                                 ).then_inc(s["ev_act"], 1)
                t["items"] += len(its)

            def attention(kind, l, head, first):
                us = units(l)

                def exps(i):
                    w = width(kind, us[i])
                    act.wait_ge(s["max_ready"], first + (i + 1))
                    act.wait_ge(s["norm_done"], first + max(i - 1, 0))
                    if i >= 2:
                        act.wait_ge(s["trans_done"], first + (i - 1))
                    if kind == "swa":
                        act.activation(esink[:, i % 2:i % 2 + 1], sinkst, ACT.Exp,
                                       bias=nm[:, i % 2:i % 2 + 1])
                    act.activation(Pm[i % 2][:, 0:w], PS[i % 2][:, 0:w], ACT.Exp, bias=nm[:, i % 2:i % 2 + 1],
                                   accum_out=rsum[:, i % 2:i % 2 + 1]).then_inc(s["exp_done"], 1)

                def evac(i):
                    w = width(kind, us[i])
                    act.wait_ge(s["trans_done"], first + (i + 1))
                    act.wait_ge(s["pv_done"], first + max(i - 1, 0))
                    act.activation(PT[i % 2][:, 0:w], PS[2][:, 0:w], ACT.Copy).then_inc(s["pt_ready"], 1)

                exps(0)
                for i in range(len(us)):
                    if i + 1 < len(us):
                        exps(i + 1)
                    evac(i)

            for name in ("exp_done", "pt_ready"):
                act.nop().then_inc(s[name], 1)
            act.wait_ge(s["set_v"], 2)
            act.activation(sT[:, :, :], sT[:, :, :], ACT.Exp).then_inc(s["set_a"], 1)
            act.activation(lbt, lbx, ACT.Exp).then_inc(s["set_a"], 1)
            act.wait_ge(s["set_v"], 3)
            act.activation(lbt[:, :, :, 1:2], lbt[:, :, :, 0:1], ACT.Ln).then_inc(s["set_a"], 1)
            for l in range(DEPTH):
                fb = first_block(l)
                end(f"mod{l}")
                norm(list(range(NB)), 0, xn, hT)
                end(f"norm{l}")
                project(range(0, 5))
                end(f"projA{l}")
                with link.loop(2, 4 if l else 2) as pr:
                    for dr in range(2):
                        def n_(per_dir, k):
                            return pr * (2 * per_dir) + (4 * l + dr) * per_dir + k

                        if dr == 0:
                            act.wait_ge(s["hg_qarg"], pr + (2 * l + 1))
                            act.activation(t_s, t_s, ACT.Exp).then_inc(s["hg_qexp"], 1)
                        act.wait_ge(s["hg_absz"], n_(1, 1))
                        link(act.activation(t_s, t_s, ACT.Exp))
                        act.activation(t_s, t_s, ACT.Ln, bias=1.0).then_inc(s["hg_lsig"], 1)
                        act.wait_ge(s["hg_karg"], n_(1, 1))
                        act.activation(k_s, k_s, ACT.Exp, bias=lbst[:, dr, 1:2] if l else 0.0).then_inc(s["hg_k"], 1)
                        if l:
                            act.wait_ge(s["hg_mix"], pr * 2 + (dr + 1))
                            link(act.activation(t_s, t_s, ACT.Exp))
                            act.activation(t_s, t_s, ACT.Ln, bias=1.0).then_inc(s["hg_mixed"], 1)
                        for lv in range(LEVELS):
                            act.wait_ge(s["lv_diff"], n_(LEVELS, lv + 1))
                            act.activation(Dl[lv % 2], Dl[lv % 2], ACT.Exp).then_inc(s["lv_exp"], 1)
                        act.wait_ge(s["st_diff"], n_(1, 1))
                        incl, excl = Bx[:, :, 1:P + 1], Bx[:, :, 0:P]
                        act.activation(chunks3(Qh if dr == 0 else Kh), incl if dr == 0 else excl, ACT.Exp)
                        act.activation(Kh if dr == 0 else Qh, Dl[0], ACT.Exp)
                        act.activation(Fd, Bx[:, :, P:P + 1].rearrange("p c o -> p (c o)"), ACT.Exp
                                       ).then_inc(s["st_exp"], 1)
                        act.wait_ge(s["st_tr"], n_(1, 1))
                        act.activation(KhT, PS[0][:, 0:TOK], ACT.Copy).then_inc(s["st_kht"], 1)
                end(f"hg{l}")
                act.wait_ge(s["ro_ms"], l + 1)
                link(act.activation(rr[:, fb:, :], rr[:, fb:, :], ACT.Ln))
                act.activation(rr[:, fb:, :], rr[:, fb:, :], ACT.Exp, scale=-0.5).then_inc(s["ro_r"], 1)
                act.wait_ge(s["ro_garg"], l + 1)
                act.activation(gT[:, fb:, :], gT[:, fb:, :], ACT.Exp).then_inc(s["ro_g"], 1)
                end(f"readout{l}")
                project(range(5, 12))
                end(f"projB{l}")
                base = t.get("rope", 0)
                q12v = q12.rearrange("p (h t) -> p h t", t=TOK)
                k8v = k8.rearrange("p (h t) -> p h t", t=TOK)
                ps4 = bank[0].rearrange("p (m t) -> p m t", t=P)
                for b in range(NB):
                    act.wait_ge(s["rope_T"], base + b + 1)
                    ts = slice(b * P, (b + 1) * P)
                    for e in range(2):
                        act.activation(q12v[0:64, e:6:2, ts], ps4[64 * e:64 * e + 64, 0:3, :], ACT.Copy)
                        last = act.activation(k8v[0:64, e, ts], ps4[64 * e:64 * e + 64, 3, :], ACT.Copy)
                    last.then_inc(s["rope_used"], 1)
                t["rope"] = base + NB
                end(f"rope{l}")
                U = len(units(l))
                u0 = t.get("units", 1)
                for kv in range(SWA_KV):
                    with act.Fori(0, 3) as g:
                        attention("swa", l, g + kv * 3, g * U + (u0 + kv * 3 * U))
                with act.Fori(0, NAT_H) as h:
                    attention("nat", l, h, h * U + (u0 + 6 * U))
                t["units"] = u0 + 12 * U
                end(f"attn{l}")
                base = t.get("mixb", 0)
                for i, b in enumerate(range(fb, NB)):
                    act.wait_ge(s["mixT_done"], base + i + 1)
                    act.activation(mixT[:, 0:4, b * P:(b + 1) * P], bank[0].rearrange("p (k t) -> p k t", t=P),
                                   ACT.Copy).then_inc(s["mixT_used"], 1)
                t["mixb"] = base + NB - fb
                end(f"mixT{l}")
                end(f"mix{l}")
                for b0 in passes_of(l):
                    ps_ = t.get("pass", 0)
                    norm([b0, b0 + 1], 1, xp, hP)
                    end(f"pnorm{l}{b0}")
                    with act.Fori(0, 2) as i:
                        for n in range(8):
                            act.wait_ge(s["pq_done"], i * 8 + (16 * ps_ + n + 1))
                            act.activation(arena[:, bass.ds(i * (8 * PASS) + n * PASS, PASS)], bank[n % 4][:, 0:PASS],
                                           ACT.Copy).then_inc(s["pq_used"], 1)
                    end(f"pq{l}{b0}")
                    for tb in range(2):
                        act.wait_ge(s["s_done"], 2 * ps_ + tb + 1)
                        if tb:
                            act.wait_ge(s["sel_ready"], 2 * ps_ + 1)
                        act.activation(sc[:, 0:8, :], PS[0][:, :].rearrange("p (a b) -> p a b", b=P), ACT.Copy)
                        act.activation(sc[:, 8:16, :], PS[1][:, :].rearrange("p (a b) -> p a b", b=P), ACT.Copy
                                       ).then_inc(s["s_used"], 1)
                        act.wait_ge(s["gexp"], 2 * ps_ + tb + 1)
                        act.activation(bs, bs, ACT.Exp).then_inc(s["gready"], 1)
                    end(f"topk{l}{b0}")
                    gb = ps_ * (PASS // 4)
                    with act.Fori(0, PASS // 8) as i:
                        for g in range(2):
                            act.wait_ge(s["one_used"], i * 2 + (gb + g + 1))
                            act.activation(G[:, :, bass.ds(i * 8 + 4 * g, 4)],
                                           bank[5 + g].rearrange("p (t j) -> p j t", j=P), ACT.Copy
                                           ).then_inc(s["g_used"], 1)
                    end(f"gbuild{l}{b0}")
                    cb = ps_ * PK

                    def gelu(i, c, first):
                        act.wait_ge(s["hu_done"], i * SLOTS + (cb + c + 1))
                        if not first:
                            act.wait_ge(s["gated"], i * SLOTS + (cb + c - 1))
                        act.activation(gel[c % 2], bank[c % 2][:, 0:PASS], ACT.Gelu).then_inc(s["gelu_done"], 1)

                    for c in range(SLOTS):
                        gelu(0, c, c < 2)
                    with act.Fori(1, PK // SLOTS) as i:
                        for c in range(SLOTS):
                            gelu(i, c, False)
                    t["pass"] = ps_ + 1
                    end(f"gemm{l}{b0}")
                    end(f"pres{l}{b0}")
            base = t["norm"]
            for i in range(4):
                act.activation(yP, x[:, CB + i, :], ACT.Square, accum_out=ss[:, i % 2:i % 2 + 1]
                               ).then_inc(s["sq_done"], 1)
                act.wait_ge(s["var_ready"], base + i + 1)
                link(act.activation(rs[:, i % 2:i % 2 + 1], ss[:, i % 2:i % 2 + 1], ACT.Ln))
                act.activation(rs[:, i % 2:i % 2 + 1], rs[:, i % 2:i % 2 + 1], ACT.Exp, scale=-0.5
                               ).then_inc(s["rms_ready"], 1)

        @block.vector
        def _(dve):
            t = {"items": 0, "tiles": 0}
            end = staged(dve, t)
            link = Chain(dve, s["dve_chain"])

            def norm(blocks, nidx, bufs, dst):
                base = t.get("norm", 0)

                def pre(i):
                    n = base + i
                    c = slice(i % 2, i % 2 + 1)
                    dve.wait_ge(s["sq_done"], n + 1)
                    dve.tensor_scalar(ss[:, c], ss[:, c], 1.0 / D, EPS, ALU.mult, ALU.add).then_inc(s["var_ready"], 1)
                    dve.wait_ge(s["rms_ready"], n + 1)
                    dve.tensor_scalar(bufs[i % 2], x[:, blocks[i], :], rs[:, c], None, ALU.mult
                                      ).then_inc(s["xn_ready"], 1)

                pre(0)
                for i, b in enumerate(blocks):
                    if i + 1 < len(blocks):
                        pre(i + 1)
                    st = 1 if b < CB else 0
                    dve.wait_ge(s["xT_done"], base + i + 1)
                    for k in range(4, 8):
                        last = dve.tensor_scalar(dst[:, k, i * P:(i + 1) * P], bank[1][:, (k - 4) * P:(k - 3) * P],
                                                 modA[:, nidx, k, st:st + 1], modp[:, nidx * 16 + k, st:st + 1],
                                                 ALU.mult, ALU.add)
                    last.then_inc(s["hT_dve"], 1)
                t["norm"] = base + len(blocks)

            def project(tiles):
                its = items(tiles)
                for n, it in enumerate(its):
                    n += t["items"]
                    if n % 2:
                        dve.wait_ge(s["proj_done"], n + 1)
                        evacuate(dve.tensor_copy, it, bank[n % 4]).then_inc(s["ev_dve"], 1)
                t["items"] += len(its)

            def attention(kind, l, head, first, head_n, nat_n):
                us = units(l)

                dve.wait_ge(s["scores_done"], first)
                qoff = head * TOK if kind == "swa" else head * TOK + 6 * TOK
                if kind == "swa":
                    link(dve.tensor_copy(sinkst, sink[:, bass.ds(head, 1)]))
                dve.tensor_scalar(qst[0:64, :], q12[0:64, bass.ds(qoff, TOK)], HD ** -0.5, None, ALU.mult
                                  ).then_inc(s["q_staged"], 1)

                def pre(i):
                    j, w, c = us[i], width(kind, us[i]), slice(i % 2, i % 2 + 1)
                    S = PS[i % 2]
                    dve.wait_ge(s["scores_done"], first + (i + 1))
                    if kind == "swa" and j >= 0:
                        edges = ([(0, CTX)] if j >= 1 else []) + ([(1, CTX + (2 if j >= 1 else 1) * P)] if j < 3 else [])
                        for m, col in edges:
                            last = dve.tensor_tensor(S[:, col:col + P], S[:, col:col + P], swam[:, m, :], ALU.add)
                        link(last)
                    if kind == "nat" and j >= 0:
                        dve.wait_ge(s["bias_ready"], nat_n + (j + 1))
                        dve.tensor_tensor(S[:, CTX:CTX + 512], S[:, CTX:CTX + 512], biast[j % 2], ALU.add
                                          ).then_inc(s["bias_used"], 1)
                        dve.wait_ge(s["bias_used"], nat_n + (j + 1))
                    link(dve.tensor_reduce(mxs[:, c], S[:, 0:w], AX, ALU.max))
                    if kind == "swa":
                        op = dve.tensor_scalar(nm[:, c], mxs[:, c], sinkst, -1.0, ALU.max, ALU.mult)
                    else:
                        op = dve.tensor_scalar(nm[:, c], mxs[:, c], -1.0, None, ALU.mult)
                    op.then_inc(s["max_ready"], 1)

                def post(i):
                    j, c = us[i], slice(i % 2, i % 2 + 1)
                    dve.wait_ge(s["exp_done"], first + (i + 1))
                    if kind == "swa":
                        link(dve.tensor_tensor(den[:, c], rsum[:, c], esink[:, c], ALU.add))
                        link(dve.reciprocal(rden[:, c], den[:, c]))
                        col = head * 64 + 256
                    else:
                        link(dve.reciprocal(rden[:, c], rsum[:, c]))
                        col = head * 64 + (256 + 384)
                    dve.wait_ge(s["pv_done"], first + (i + 1))
                    dve.tensor_scalar(mix[:, j + 2, bass.ds(col, 64)], bank[6 + i % 2][:, 0:64], rden[:, c], None,
                                      ALU.mult).then_inc(s["norm_done"], 1)

                pre(0)
                for i in range(len(us)):
                    if i + 1 < len(us):
                        pre(i + 1)
                    post(i)

            def topk(count):
                low = -3.0e38
                for hp in range(16):
                    last = dve.max(tv[:, hp, 0:8], sc[:, hp, :])
                link(last)
                for hp in range(16):
                    dve.max_index(tiu[:, hp, 0:8], tv[:, hp, 0:8], sc[:, hp, :])
                    last = dve.match_replace(sc2[:, hp, :], tv[:, hp, 0:8], sc[:, hp, :], low)
                link(last)
                for hp in range(16):
                    last = dve.max(tv[:, hp, 8:16], sc2[:, hp, :])
                link(last)
                for hp in range(16):
                    last = dve.max_index(tiu[:, hp, 8:16], tv[:, hp, 8:16], sc2[:, hp, :])
                link(last)
                link(dve.tensor_copy(tif, tiu))
                tvh = tv.rearrange("p (h o) k -> p h o k", o=2)
                tfh = tif.rearrange("p (h o) k -> p h o k", o=2)
                full = [P, HEADS, TOPK, TOPK]
                link(dve.tensor_tensor(cand.rearrange("p h (a b) -> p h a b", a=TOPK),
                                       tvh[:, :, 0, :].unsqueeze(3).broadcast_to(full),
                                       tvh[:, :, 1, :].unsqueeze(2).broadcast_to(full), ALU.add))
                for h in range(HEADS):
                    last = dve.max(bs[:, h, 0:8], cand[:, h, :])
                link(last)
                for h in range(HEADS):
                    dve.max_index(pu[:, h, 0:8], bs[:, h, 0:8], cand[:, h, :])
                    last = dve.match_replace(cand2[:, h, :], bs[:, h, 0:8], cand[:, h, :], low)
                link(last)
                for h in range(HEADS):
                    last = dve.max(bs[:, h, 8:16], cand2[:, h, :])
                link(last)
                for h in range(HEADS):
                    last = dve.max_index(pu[:, h, 8:16], bs[:, h, 8:16], cand2[:, h, :])
                link(last)
                link(dve.tensor_copy(gs1, bs[:, :, 0]))
                dve.tensor_tensor(bs, bs, gs1.unsqueeze(2).broadcast_to([P, HEADS, TOPK]), ALU.subtract
                                  ).then_inc(s["gexp"], 1)
                link(dve.tensor_single_scalar(pa, pu, 4, ALU.logical_shift_right))
                link(dve.tensor_copy(paf, pa))
                link(dve.tensor_single_scalar(pa, pu, 15, ALU.bitwise_and))
                link(dve.tensor_copy(pbf, pa))
                for v, at in enumerate((paf, pbf)):
                    link(dve.tensor_tensor(eq, at.unsqueeze(3).broadcast_to(full),
                                           iota[:, 0:TOPK].unsqueeze(1).unsqueeze(1).broadcast_to(full), ALU.is_equal))
                    link(dve.tensor_tensor(eq, eq, tfh[:, :, v, :].unsqueeze(2).broadcast_to(full), ALU.mult))
                    link(dve.tensor_reduce(sel[:, v, :].rearrange("p (h k) -> p h k", k=TOPK), eq, AX, ALU.add))
                dve.wait_ge(s["gready"], count)
                link(dve.tensor_reduce(gs1, bs, AX, ALU.add))
                link(dve.reciprocal(gs1, gs1))
                dve.tensor_tensor(sel[:, 2, :].rearrange("p (h k) -> p h k", k=TOPK), bs,
                                  gs1.unsqueeze(2).broadcast_to([P, HEADS, TOPK]), ALU.mult).then_inc(s["sel_ready"], 1)

            def links_of(kind, l):
                us = units(l)
                return (kind == "swa") + sum(1 + (kind == "swa" and j >= 0) + (2 if kind == "swa" else 1) for j in us)

            for name in ("max_ready", "norm_done", "bias_used"):
                dve.nop().then_inc(s[name], 1)
            dve.wait_ge(s["consts_in"], 64)
            dve.tensor_scalar(sT[:, :, :], c0, -1.0, 80.0, ALU.mult, ALU.min).then_inc(s["set_v"], 1)
            link(dve.tensor_tensor(lbt[:, :, :, 0:1], lbx[:, :, :, 0:1], lbx[:, :, :, 1:2], ALU.max))
            dve.tensor_tensor(lbx, lbx, lbt[:, :, :, 0:1].broadcast_to([P, 2, 2, 2]), ALU.subtract
                              ).then_inc(s["set_v"], 1)
            dve.wait_ge(s["set_a"], 2)
            dve.tensor_tensor(lbt[:, :, :, 0:1], lbt[:, :, :, 0:1], lbt[:, :, :, 1:2], ALU.add).then_inc(s["set_v"], 1)
            link(dve.tensor_scalar(sT[:, :, :], sT[:, :, :], 1.0, None, ALU.add))
            link(dve.reciprocal(sT[:, :, :], sT[:, :, :]))
            dve.tensor_tensor(sT[:, :, :], sT[:, :, :], c0, ALU.mult).then_inc(s["silu_done"], 1)
            dve.wait_ge(s["set_a"], 3)
            dve.tensor_tensor(lbc[:, :, :, 0:1], lbx[:, :, :, 1:2], lbt[:, :, :, 1:2], ALU.subtract)
            link(dve.tensor_tensor(lbc[:, :, :, 1:2], lbx[:, :, :, 0:1], lbt[:, :, :, 1:2], ALU.subtract))
            dve.wait_ge(s["x_in"], 16 * NB)
            for l in range(DEPTH):
                fb = first_block(l)
                nb = NB - fb
                dve.wait_ge(s["layer_in"], 144 * (l + 1))
                dve.wait_ge(s["slot_free"], t["tiles"] + MOD_TILES)
                link(dve.tensor_tensor(modp[:, :, :], bank[0][:, 0:64].rearrange("p (n s) -> p n s", s=2), bT, ALU.add))
                for n in range(2):
                    link(dve.tensor_scalar(modA[:, n, :, :], modp[:, n * 16 + 8:n * 16 + 16, :], 1.0, None, ALU.add))
                    link(dve.tensor_tensor(modA[:, n, :, :], modA[:, n, :, :],
                                           nw[:, n, :].unsqueeze(2).broadcast_to([P, KD, 2]), ALU.mult))
                for h in range(2):
                    last = dve.tensor_tensor(grow[0:2, h * 1024:h * 1024 + 1024], PS[1 + h][0:2, :],
                                             brow[0:2, h * 1024:h * 1024 + 1024], ALU.add)
                last.then_inc(s["mod_done"], 1)
                end(f"mod{l}")
                norm(list(range(NB)), 0, xn, hT)
                end(f"norm{l}")
                project(range(0, 5))
                t["tiles"] += MOD_TILES + IN_TILES + OUT_TILES
                end(f"projA{l}")

                dve.memset(Bx[:, :, 0:1], 0.0)
                dve.memset(ones, 1.0)
                for i in range(2):
                    dve.memset(Qt[i], 0.0)
                    last = dve.memset(Kt[i], 0.0)
                link(last)
                per = 2 * (10 if l else 7) + 4
                with link.loop(2, per) as pr:
                    for dr in range(2):
                        def n_(per_dir, k):
                            return pr * (2 * per_dir) + (4 * l + dr) * per_dir + k

                        if dr == 0:
                            link(dve.tensor_copy(q_s, arena[:, bass.ds(pr * TOK + 12288, TOK)]))
                            dve.tensor_scalar(t_s, q_s, -1.0, 80.0, ALU.mult, ALU.min).then_inc(s["hg_qarg"], 1)
                            dve.wait_ge(s["hg_qexp"], pr + (2 * l + 1))
                            link(dve.tensor_scalar(t_s, t_s, 1.0, None, ALU.add))
                            link(dve.reciprocal(t_s, t_s))
                            link(dve.tensor_tensor(q_s, q_s, t_s, ALU.mult))
                        dve.tensor_copy(lbst[:, dr, :], small[:, bass.ds(pr * 2 + (92 + 4 * dr), 2)])
                        link(dve.tensor_copy(z_s, arena[:, bass.ds(pr * TOK + (12288 + (2 + 2 * dr) * TOK), TOK)]))
                        dve.scalar_tensor_tensor(out=t_s, in0=z_s, scalar=-1.0, in1=z_s, op0=ALU.mult, op1=ALU.min
                                                 ).then_inc(s["hg_absz"], 1)
                        dve.wait_ge(s["hg_lsig"], n_(1, 1))
                        link(dve.scalar_tensor_tensor(out=lf_s, in0=z_s, scalar=0.0, in1=t_s, op0=ALU.min,
                                                      op1=ALU.subtract))
                        dve.tensor_tensor(k_s, lf_s, z_s, ALU.subtract).then_inc(s["hg_karg"], 1)
                        if l:
                            lb, lm = lbst[:, dr, 0:1], lbst[:, dr, 1:2]
                            link(dve.tensor_scalar(lf_s, lf_s, lm, None, ALU.add))
                            link(dve.tensor_scalar(z_s, lf_s, lb, None, ALU.subtract))
                            dve.scalar_tensor_tensor(out=t_s, in0=z_s, scalar=-1.0, in1=z_s, op0=ALU.mult,
                                                     op1=ALU.min).then_inc(s["hg_mix"], 1)
                            dve.wait_ge(s["hg_mixed"], pr * 2 + (dr + 1))
                            link(dve.scalar_tensor_tensor(out=lf_s, in0=lf_s, scalar=lb, in1=t_s, op0=ALU.max,
                                                          op1=ALU.add))
                        dve.memset(Asc, 0.0)
                        for c in range(NB):
                            last = dve.tensor_tensor_scan(Bx[:, c, 1:P + 1], ones, lf_s[:, c * P:(c + 1) * P], 0.0,
                                                          ALU.mult, ALU.add)
                        last.then_inc(s["hg_qk"], 1)
                        dve.wait_ge(s["hg_qk"], n_(1, 1))
                        incl, excl = Bx[:, :, 1:P + 1], Bx[:, :, 0:P]

                        def diff(lv):
                            H = 1 << lv
                            if lv >= 2:
                                dve.wait_ge(s["lv_ops"], n_(LEVELS, lv - 1))
                            dl, drt = lv_halves(chunks3(Dl[lv % 2]), lv)
                            il, ir = lv_halves(incl, lv)
                            xl, xr = lv_halves(excl, lv)
                            ref = xr[:, :, :, 0:1].broadcast_to([P, NB, P // (2 * H), H])
                            dve.tensor_tensor(dl, ref, il if dr == 0 else xl, ALU.subtract)
                            dve.tensor_tensor(drt, ir if dr == 0 else xr, ref, ALU.subtract).then_inc(s["lv_diff"], 1)

                        def ops(lv):
                            dve.wait_ge(s["lv_exp"], n_(LEVELS, lv + 1))
                            if lv >= 2:
                                dve.wait_ge(s["lv_pe"], n_(LEVELS + 1, lv - 1))
                            if lv == 0:
                                dve.wait_ge(s["hg_k"], n_(1, 1))
                            qs, ks = (1, 0) if dr == 0 else (0, 1)
                            E = lv_halves(chunks3(Dl[lv % 2]), lv)
                            dve.tensor_tensor(lv_halves(chunks3(Qt[lv % 2]), lv)[qs], E[qs],
                                              lv_halves(chunks3(q_s), lv)[qs], ALU.mult)
                            dve.tensor_tensor(lv_halves(chunks3(Kt[lv % 2]), lv)[ks], E[ks],
                                              lv_halves(chunks3(k_s), lv)[ks], ALU.mult).then_inc(s["lv_ops"], 1)

                        def merge(lv):
                            dve.wait_ge(s["lv_pe"], n_(LEVELS + 1, lv + 1))
                            if lv >= 1:
                                dve.wait_ge(s["lv_used"], n_(LEVELS + 1, lv))
                            dve.memset(small[:, 159:160], 0.0)
                            for e in range(2):
                                last = dve.copy_predicated(
                                    Asc[:, e], masks[:, dr, lv, :].unsqueeze(1).broadcast_to([P, NB, P]),
                                    chunks3(PS[2 * (lv % 2) + e][:, 0:TOK]))
                            last.then_inc(s["lv_used"], 1)

                        diff(0)
                        for lv in range(LEVELS):
                            if lv + 1 < LEVELS:
                                diff(lv + 1)
                            ops(lv)
                            if lv >= 1:
                                merge(lv - 1)
                        merge(LEVELS - 1)
                        dve.wait_ge(s["lv_ops"], n_(LEVELS, LEVELS))
                        dve.tensor_tensor(chunks3(Dl[0]), Bx[:, :, P:P + 1].broadcast_to([P, NB, P]),
                                          incl if dr == 0 else excl, ALU.subtract).then_inc(s["st_diff"], 1)
                        merge(LEVELS)
                        dve.wait_ge(s["st_exp"], n_(1, 1))
                        dve.tensor_tensor(Qh, Qh, q_s, ALU.mult)
                        dve.tensor_tensor(Kh, Kh, k_s, ALU.mult).then_inc(s["st_ops"], 1)
                        dve.memset(Sh[:, 0, :], 0.0)
                        dve.wait_ge(s["st_u"], n_(1, 1))
                        u = chunks3(PS[1][:, 0:TOK])
                        dve.tensor_copy(Ub[0:64, :, :], u[0:64, :, 0:64])
                        link(dve.tensor_copy(Ub[64:128, :, :], u[64:128, :, 64:128]))
                        order = [0, 1, 2, 3, 4, 5] if dr == 0 else [1, 0, 5, 4, 3, 2]
                        for n in range(NB - 1):
                            c = order[n]
                            op = dve.scalar_tensor_tensor(out=Sh[:, n + 1, :], in0=Sh[:, n, :], scalar=Fd[:, c:c + 1],
                                                          in1=Ub[:, c, :], op0=ALU.mult, op1=ALU.add)
                            if n < NB - 2:
                                link(op)
                            else:
                                op.then_inc(s["st_hist"], 1)
                        dve.wait_ge(s["st_out"], n_(1, 1))
                        for e in range(2):
                            dst = mix[:, fb:, bass.ds(pr * P + 64 * e, 64)]
                            src = bank[4 + e][:, fb * 64:NB * 64].rearrange("p (c d) -> p c d", d=64)
                            if dr == 0:
                                last = dve.tensor_copy(dst, src)
                            else:
                                last = dve.tensor_tensor(dst, src, dst, ALU.add)
                        last.then_inc(s["st_saved"], 1)
                        dve.wait_ge(s["st_saved"], n_(1, 1))
                end(f"hg{l}")

                ho = mix[:, fb:, 0:256]
                g4 = gS[:, fb:, :].rearrange("p c (h d) -> p c h d", d=64)
                gin = hvg[:, fb:, 256:512]
                gt = gT[:, fb:, :]
                link(dve.tensor_tensor(gS[:, fb:, :], ho, ho, ALU.mult))
                link(dve.tensor_reduce(rr[:, fb:, :], g4, AX, ALU.add))
                dve.tensor_scalar(rr[:, fb:, :], rr[:, fb:, :], 1.0 / 64, EPS, ALU.mult, ALU.add).then_inc(s["ro_ms"], 1)
                dve.tensor_scalar(gt, gin, -1.0, 80.0, ALU.mult, ALU.min).then_inc(s["ro_garg"], 1)
                dve.wait_ge(s["ro_g"], l + 1)
                link(dve.tensor_scalar(gt, gt, 1.0, None, ALU.add))
                link(dve.reciprocal(gt, gt))
                link(dve.tensor_tensor(gt, gt, gin, ALU.mult))
                link(dve.tensor_tensor(gt, gt, hnw.unsqueeze(1).broadcast_to([P, nb, 256]), ALU.mult))
                dve.wait_ge(s["ro_r"], l + 1)
                for c in range(fb, NB):
                    h4 = mix[:, c, 0:256].rearrange("p (h d) -> p h d", d=64)
                    last = dve.tensor_tensor(h4, h4, rr[:, c, :].unsqueeze(2).broadcast_to([P, 4, 64]), ALU.mult)
                link(last)
                link(dve.tensor_tensor(ho, ho, gt, ALU.mult))
                end(f"readout{l}")
                project(range(5, 12))
                end(f"projB{l}")

                for j in range(4):
                    b = CB + j
                    def four(ap):
                        return ap.rearrange("p (g o i) -> p g o i", o=2, i=16)
                    def half(ap):
                        return ap.rearrange("p (h f i) -> p h f i", f=2, i=16)
                    xi = four(sqk[:, b, :])
                    x1, x2 = (xi[:, :, o, :].rearrange("p (h f) i -> p h f i", f=2) for o in range(2))
                    yo = four(rq)
                    y1, y2 = (yo[:, :, o, :].rearrange("p (h f) i -> p h f i", f=2) for o in range(2))
                    cs, sn = (tt[:, j, :].rearrange("p (f i) -> p f i", f=2).unsqueeze(1).broadcast_to([P, 8, 2, 16])
                              for tt in (cosT, sinT))
                    t1, t2 = half(rt[:, 0:256]), half(rt[:, 256:512])
                    dve.tensor_tensor(t1, x1, cs, ALU.mult)
                    link(dve.tensor_tensor(t2, x2, sn, ALU.mult))
                    if j:
                        dve.wait_ge(s["rope_T"], NB * l + b)
                    link(dve.tensor_tensor(y1, t1, t2, ALU.subtract))
                    dve.tensor_tensor(t1, x2, cs, ALU.mult)
                    link(dve.tensor_tensor(t2, x1, sn, ALU.mult))
                    dve.tensor_tensor(y2, t1, t2, ALU.add).then_inc(s["rope_ready"], 1)
                    dve.wait_ge(s["rope_ready"], 4 * l + j + 1)
                end(f"rope{l}")

                U = len(units(l))
                u0, n0 = t.get("units", 1), 4 * NAT_H * l + 1
                for kv in range(SWA_KV):
                    with link.loop(3, links_of("swa", l)) as g:
                        attention("swa", l, g + kv * 3, g * U + (u0 + kv * 3 * U), None, None)
                with link.loop(NAT_H, links_of("nat", l)) as h:
                    attention("nat", l, h, h * U + (u0 + 6 * U), None, h * 4 + n0)
                t["units"] = u0 + 12 * U
                end(f"attn{l}")
                base = t.get("mixb", 0)
                for i, b in enumerate(range(fb, NB)):
                    dve.wait_ge(s["mixT_done"], base + i + 1)
                    dve.tensor_copy(mixT[:, 4:8, b * P:(b + 1) * P], bank[1].rearrange("p (k t) -> p k t", t=P)
                                    ).then_inc(s["mixT_used"], 1)
                t["mixb"] = base + nb
                end(f"mixT{l}")
                dve.wait_ge(s["gate_in"], 16 * t.get("gate", 0) + 32)
                t["gate"] = t.get("gate", 0) + 2
                base = t.get("y", 0)
                for tl in range(OUT_TILES):
                    for i, b in enumerate(range(fb, NB)):
                        n = base + tl * nb + i
                        st = 1 if b < CB else 0
                        cols = slice(tl * TW, (tl + 1) * TW)
                        dve.wait_ge(s["y_done"], n + 1)
                        dve.tensor_tensor(ytmp, bank[n % 4][:, 0:TW], gateb[:, st, cols], ALU.mult
                                          ).then_inc(s["y_used"], 1)
                        dve.wait_ge(s["y_used"], n + 1)
                        link(dve.tensor_tensor(x[:, b, cols], x[:, b, cols], ytmp, ALU.add))
                t["y"] = base + OUT_TILES * nb
                end(f"mix{l}")

                for b0 in passes_of(l):
                    ps_ = t.get("pass", 0)
                    norm([b0, b0 + 1], 1, xp, hP)
                    t["tiles"] += WQ_TILES
                    end(f"pnorm{l}{b0}")
                    end(f"pq{l}{b0}")
                    for tb in range(2):
                        dve.wait_ge(s["s_used"], 2 * ps_ + tb + 1)
                        topk(2 * ps_ + tb + 1)
                        dve.wait_ge(s["selT_done"], 2 * ps_ + tb + 1)
                        dve.tensor_copy(kT[:, :, tb * P:(tb + 1) * P], bank[4][:, 0:384].rearrange("p (v t) -> p v t", v=3)
                                        ).then_inc(s["selT_used"], 1)
                    end(f"topk{l}{b0}")
                    gb = ps_ * (PASS // 4)

                    def one_hots(i, first):
                        for g in range(2):
                            if not first:
                                dve.wait_ge(s["one_used"], i * 2 + (gb + g - 1))
                            for q in range(4):
                                n = 4 * g + q
                                row, col, gate = (arena[:, bass.ds(i * 8 + (34816 + v * PASS + n), 1)] for v in range(3))
                                dve.tensor_scalar(oneA[:, n, :], iota[:, :], row, gate, ALU.is_equal, ALU.mult)
                                last = dve.tensor_scalar(oneB[:, n, :], iota[:, :], col, None, ALU.is_equal)
                            last.then_inc(s["one_ready"], 1)

                    one_hots(0, True)
                    with dve.Fori(1, PASS // 8) as i:
                        one_hots(i, False)
                    end(f"gbuild{l}{b0}")
                    cb = ps_ * PK
                    t0 = t["tiles"]

                    def gate(i, c, first):
                        dve.wait_ge(s["gelu_done"], i * SLOTS + (cb + c + 1))
                        if not first:
                            dve.wait_ge(s["slot_free"], i * SLOTS + (t0 + c - 1))
                        dve.tensor_tensor(gat[c % 2], gel[c % 2], arena[:, bass.ds(i * (SLOTS * PASS) + c * PASS, PASS)],
                                          ALU.mult).then_inc(s["gated"], 1)

                    for c in range(SLOTS):
                        gate(0, c, c < 2)
                    with dve.Fori(1, PK // SLOTS) as i:
                        for c in range(SLOTS):
                            gate(i, c, False)
                    t["tiles"] += PK
                    t["pass"] = ps_ + 1
                    end(f"gemm{l}{b0}")
                    t["gate"] += 1
                    dve.wait_ge(s["gate_in"], 16 * t["gate"])
                    for tb in range(2):
                        link(dve.tensor_tensor(yP, PS[2 + tb][:, :], gbP, ALU.mult))
                        link(dve.tensor_tensor(x[:, b0 + tb, :], x[:, b0 + tb, :], yP, ALU.add))
                    end(f"pres{l}{b0}")
            base = t["norm"]
            dve.wait_ge(s["nrm_in"], 16)
            for i in range(4):
                c = slice(i % 2, i % 2 + 1)
                dve.wait_ge(s["sq_done"], base + i + 1)
                dve.tensor_scalar(ss[:, c], ss[:, c], 1.0 / D, EPS, ALU.mult, ALU.add).then_inc(s["var_ready"], 1)
                dve.wait_ge(s["rms_ready"], base + i + 1)
                if i >= 2:
                    dve.wait_ge(s[f"fin_out{i % 2}"], 16)
                dve.scalar_tensor_tensor(out=xp[i % 2], in0=x[:, CB + i, :], scalar=rs[:, c], in1=gbP,
                                         op0=ALU.mult, op1=ALU.mult).then_inc(s["fin_ready"], 1)



def shape_tables():
    ident = np.eye(P, dtype=np.float32)
    iota = np.broadcast_to(np.arange(P, dtype=np.float32), (P, P)).copy()
    a = np.arange(P)
    s_, t_ = a[:, None], a[None, :]
    masks = np.zeros((P, 2, LEVELS + 1, P), np.uint8)
    for lv in range(LEVELS):
        H = 1 << lv
        same = (s_ // (2 * H)) == (t_ // (2 * H))
        masks[:, 0, lv] = same & (s_ % (2 * H) < H) & (t_ % (2 * H) >= H)
        masks[:, 1, lv] = same & (s_ % (2 * H) >= H) & (t_ % (2 * H) < H)
    masks[:, :, LEVELS] = (s_ == t_)[:, None, :]
    pos = np.arange(SEQ)
    inv = (10000.0 ** (-np.arange(16, dtype=np.float32) / 16)).astype(np.float32)
    ang = np.concatenate([(pos // GRID_W)[:, None].astype(np.float32) * inv,
                          (pos % GRID_W)[:, None].astype(np.float32) * inv], axis=1)
    rope = np.stack([np.cos(ang), np.sin(ang)]).astype(np.float32).reshape(2, 4, P, 32).transpose(2, 0, 1, 3)
    swam = np.stack([np.where(t_ >= s_, 0.0, NEG), np.where(t_ <= s_, 0.0, NEG)], axis=1).astype(np.float32)
    col = np.arange(GRID_W)
    start = np.clip(col - NAT_COLS // 2, 0, GRID_W - NAT_COLS)
    ok = (col[None, :] >= start[:, None]) & (col[None, :] < start[:, None] + NAT_COLS)
    natm = np.tile(np.where(ok, 0.0, NEG).astype(np.float32), (2, 1))
    return {"ident": ident, "iota": iota, "masks": masks.reshape(P, -1).view(np.float32).copy(),
            "rope": rope.reshape(P, 256).copy(), "swam": swam.reshape(P, 256).copy(), "natm": natm}


def tiles_of(w, width):
    n = w.shape[1] // width
    return w.reshape(KD, P, n, width).transpose(2, 1, 0, 3)


def lay_out(a):
    L = DEPTH
    A = {"x": a["x"][0], "ctx": a["ctx"][0]}
    A["c"] = np.stack([a["c"][0].reshape(KD, P).T, a["c_ctx"].reshape(KD, P).T], axis=2)
    A["lb"] = a["hgrn_lb_logits"].reshape(2, L, 2, P).transpose(3, 0, 2, 1)
    wcat, wq, ex, bT, nw, rpb, subk, bgate = [], [], [], [], [], [], [], []
    for l in range(L):
        wm = np.split(a["w_mod"][l], 6, axis=1)
        wm = np.concatenate([wm[i] for i in (0, 1, 3, 4, 2, 5)], axis=1)
        wi = a["w_in"][l]
        wi = np.concatenate([wi[:, 0:1920], wi[:, 2688:3072], wi[:, 1920:2688]], axis=1)
        wcat.append(np.concatenate([tiles_of(w, TW).reshape(-1, P, TILE_F) for w in (wm, wi, a["w_out"][l])]))
        wq.append(a["peer_wq"][l].reshape(KD, P, WQ_TILES, 2, P).transpose(2, 1, 3, 0, 4).reshape(WQ_TILES, P, TILE_F))
        u = a["peer_u"][l].reshape(P, PK, KD, P).transpose(1, 3, 2, 0).reshape(PK, P, D)
        v = a["peer_v"][l].reshape(P, PK, D).transpose(1, 0, 2)
        ex.append(np.concatenate([u, v], axis=2))
        bm = np.split(a["b_mod"][l], 6)
        bm_ = np.concatenate([bm[i].reshape(KD, P).T for i in (0, 1, 3, 4)], axis=1)
        bT.append(np.repeat(bm_[:, :, None], 2, axis=2).reshape(P, 64))
        bgate.append(np.concatenate([bm[2], bm[5]]))
        nw.append(np.concatenate([a["norm_mix_w"][l].reshape(KD, P).T, a["norm_ffn_w"][l].reshape(KD, P).T], axis=1))
        r = a["nat_rpb"][l]
        wide = np.zeros((NAT_H, 15, 127), r.dtype)
        wide[:, :, 48:79] = r
        rpb.append(np.stack([wide[:, :, 63 - c:127 - c] for c in range(GRID_W)], axis=1).reshape(NAT_H, GRID_W, 960))
        subk.append(a["peer_subkeys"][l].reshape(16, P, P).transpose(2, 0, 1).reshape(P, 2048))
    A["wcat"], A["wq"], A["experts"], A["bT"], A["nw"] = map(np.stack, (wcat, wq, ex, bT, nw))
    A["rpb"], A["subk"], A["bgate"] = map(np.stack, (rpb, subk, bgate))
    A["sink"], A["hnw"] = a["swa_sink"], a["hgrn_norm_w"]
    A["fnw"] = a["final_norm_w"].reshape(1, D)
    A.update(shape_tables())
    return {k: np.ascontiguousarray(v) for k, v in A.items()}


def declare(nc, arrays):
    d = {k: nc.dram_tensor(f"in_{k}", v.shape, mybir.dt.from_np(v.dtype), kind="ExternalInput").ap()
         for k, v in arrays.items()}
    d["gates"] = nc.dram_tensor("gates", (DEPTH, 2, 2 * D), F32).ap()
    return d


def kernel(**inputs):
    import concourse.bacc as bacc
    from concourse.bass_utils import run_bass_kernel_spmd

    arrays = lay_out({k: np.asarray(v) for k, v in inputs.items()})
    nc = bacc.Bacc("TRN2", target_bir_lowering=False, num_devices=1)
    d = declare(nc, arrays)
    out = nc.dram_tensor("out", (SEQ, D), F32, kind="ExternalOutput").ap()
    build(nc, d, out)
    r = run_bass_kernel_spmd(nc, [{f"in_{k}": v for k, v in arrays.items()}], core_ids=[0])
    return r.results[0]["out"].reshape(1, SEQ, D)
```

```python
import numpy as np
import concourse.bass as bass
from concourse import mybir
from contextlib import ExitStack, contextmanager

D = 1024
P = 128
KD = D // P
CTX, SEQ, DEPTH = 256, 512, 2
TOK = CTX + SEQ
NB = TOK // P
CB = CTX // P
GRID_W, GRID_H = 64, SEQ // 64
HD = 64
SWA_H, SWA_KV, NAT_H = 6, 2, 6
NAT_ROWS, NAT_COLS = 8, 16
HEADS, PK, NK, TOPK = 8, 128, 128, 16
TW = 256
SLOTS = 4
TILE_F = KD * TW
MOD_TILES, IN_TILES, OUT_TILES, WQ_TILES = 24, 12, 4, 8
PASS = 2 * P
LEVELS = 7
EPS = 1e-6
NEG = -1e30

F32 = mybir.dt.float32
F32R = mybir.dt.float32r
U32 = mybir.dt.uint32
U8 = mybir.dt.uint8
ALU = mybir.AluOpType
ACT = mybir.ActivationFunctionType
AX = mybir.AxisListType.X


def passes_of(layer):
    return range(0 if layer < DEPTH - 1 else CB, NB, 2)


def first_block(layer):
    return 0 if layer < DEPTH - 1 else CB


class Chain:

    def __init__(self, eng, sem):
        self.eng, self.sem, self.n, self.term = eng, sem, 0, 0

    def __call__(self, ins):
        ins.then_inc(self.sem, 1)
        self.n += 1
        self.eng.wait_ge(self.sem, self.term + self.n if not isinstance(self.term, int) else self.n + self.term)

    @contextmanager
    def loop(self, count, per):
        base, outer = self.n, self.term
        with self.eng.Fori(0, count) as i:
            self.term = i * per + outer
            yield i
            assert self.n - base == per, f"{self.n - base} links in a body of {per}"
        self.term, self.n = outer, base + count * per


def build(nc, d, out):
    with ExitStack() as ctx:
        def sb(name, shape, dt=F32):
            return ctx.enter_context(nc.sbuf_tensor(name, shape, dt))

        def sem(name):
            return ctx.enter_context(nc.semaphore(name))

        ring = sb("ring", [P, SLOTS, TILE_F])
        ident = sb("ident", [P, P])
        iota = sb("iota", [P, P])
        sT = sb("sT", [P, KD, 2])
        modp = sb("modp", [P, 4 * KD, 2])
        modA = sb("modA", [P, 2, KD, 2])
        small = sb("small", [P, 160])
        ARENA = 35264
        arena = sb("arena", [P, ARENA])
        hS = sb("hS", [P, 2, KD, PASS], F32R)
        wS = sb("wS", [P, 4, D], F32R)
        gS_ = sb("gS_", [P, 4, PASS], F32R)

        def view(start, *dims):
            size = int(np.prod(dims))
            assert start + size <= ARENA
            names = "abcde"[:len(dims)]
            spec = " ".join(names)
            flat = arena[:, start:start + size]
            if len(dims) == 1:
                return flat
            return flat.rearrange(f"p ({spec}) -> p {spec}", **dict(zip(names, dims)))

        bT = small[:, 0:64].rearrange("p (n s) -> p n s", s=2)
        nw = small[:, 64:64 + 16].rearrange("p (n k) -> p n k", n=2)
        ss = small[:, 80:82]
        rs = small[:, 82:84]
        lbx = small[:, 84:92].rearrange("p (d q l) -> p d q l", d=2, q=2)
        lbc = small[:, 92:100].rearrange("p (d q v) -> p d q v", d=2, q=2)
        lbt = small[:, 100:108].rearrange("p (d q l) -> p d q l", d=2, q=2)
        sink = small[:, 108:114]
        nm = small[:, 114:118]
        rsum = small[:, 118:122]
        esink = small[:, 146:150]
        rden = small[:, 150:154]
        lbst = small[:, 122:126].rearrange("p (d v) -> p d v", d=2)
        mxs = small[:, 126:130]
        den = small[:, 154:158]
        sinkst = small[:, 158:159]
        c0 = small[:, 130:146].rearrange("p (k s) -> p k s", s=2)

        hT = view(0, KD, TOK)
        mix = view(6144, NB, D)
        hgF = view(12288, 6, TOK)
        hvg = view(16896, NB, 512)
        W = 19968
        z_s, q_s, k_s, lf_s, t_s = (view(W + i * TOK, TOK) for i in range(5))
        Bx = view(W + 5 * TOK, NB, P + 1)
        W2 = W + 5 * TOK + NB * (P + 1)
        Dl = [view(W2 + i * TOK, TOK) for i in range(2)]
        Qt = [view(W2 + (2 + i) * TOK, TOK) for i in range(2)]
        Kt = [view(W2 + (4 + i) * TOK, TOK) for i in range(2)]
        Asc = view(W2 + 6 * TOK, 2, NB, P)
        Qh, Kh, KhT = (view(W2 + (8 + i) * TOK, TOK) for i in range(3))
        Ub = view(W2 + 11 * TOK, NB, 64)
        Sh = view(W2 + 11 * TOK + NB * 64, NB, 64)
        Fd = view(W2 + 12 * TOK, NB)
        ones = t_s[:, 0:P]
        xin = view(12288, NB, D)
        gS = view(W, NB, 256)
        gT = view(W + 1536, NB, 256)
        rr = view(W + 3072, NB, 4)
        CST = ARENA - 1344
        masks = arena[:, CST:CST + 512].bitcast(U8).rearrange("p (d l t) -> p d l t", d=2, l=LEVELS + 1)
        cosT = view(CST + 512, 4, 32)
        sinT = view(CST + 640, 4, 32)
        swam = view(CST + 768, 2, P)
        natm = view(CST + 1024, GRID_W)
        hnw = view(CST + 1088, 256)

        q12 = view(12288, 12 * TOK)
        k8 = view(21504, 8 * TOK)
        v8 = view(27648, NB, 512)
        sqk = view(30720, NB, 512)
        rq = view(0, 512)
        rt = view(512, 512)
        qst = view(30720, TOK)
        Pm = [view(i * TOK, TOK) for i in range(2)]
        PT = [view((2 + i) * TOK, TOK) for i in range(2)]
        biast = [view(4 * TOK + i * 512, 512) for i in range(2)]
        mixT = hT
        gateb = view(12288, 2, D)
        xw = view(14336, NB, D)
        ytmp = view(20480, TW)
        grow = view(0, 2048)
        brow = view(2048, 2048)
        xn = [view(6144 + i * D, D) for i in range(2)]

        G = view(0, PK, PASS)
        KT0 = 32768
        kT = view(KT0, 3, PASS)
        GD = 4
        wrows = wS.rearrange("p a b -> p (a b)")
        oneR = [wrows[:, 512 * g:512 * g + 512].rearrange("p (n c) -> p n c", c=P) for g in range(GD)]
        oneB = [wrows[:, 2048 + 512 * g:2560 + 512 * g].rearrange("p (n c) -> p n c", c=P) for g in range(GD)]
        oneA = [view(KT0 + 3 * PASS + 512 * g, 4, P) for g in range(2)]
        gel = [view(KT0 + i * PASS, PASS) for i in range(4)]
        hP = view(28672, KD, PASS)
        xp = [view(24576 + i * D, D) for i in range(2)]
        XL = 22528
        xl = view(XL, 2, D)
        xf = view(4096, 4, D)
        qP = view(0, 16, PASS)
        subk = view(4096, 16, P)
        sc = view(6144, 16, P)
        sc2 = view(8192, 16, P)
        cand = view(10240, HEADS, 256)
        cand2 = view(12288, HEADS, 256)
        eqs = [view(14336 + v * 2048, HEADS, TOPK, TOPK) for v in range(2)]
        tv = view(20480, 16, TOPK)
        tifs = [view(20736, 16, TOPK), view(18432, 16, TOPK)]
        tiu = arena[:, 20992:21248].bitcast(U32).rearrange("p (a b) -> p a b", a=16)
        bss = [view(21248, HEADS, TOPK), view(18688, HEADS, TOPK)]
        pu = arena[:, 21376:21504].bitcast(U32).rearrange("p (a b) -> p a b", a=HEADS)
        pa = arena[:, 21504:21632].bitcast(U32).rearrange("p (a b) -> p a b", a=HEADS)
        pafs = [view(21632, HEADS, TOPK), view(18816, HEADS, TOPK)]
        pbfs = [view(21760, HEADS, TOPK), view(18944, HEADS, TOPK)]
        sel = view(21888, 3, P)
        gs1 = view(22272, HEADS)
        gbP = view(0, D)
        yP = view(1024, D)
        xr = view(2048, 2, D)

        PS = [ctx.enter_context(nc.psum_tensor(f"PS{i}", [P, 1024], F32)) for i in range(4)]
        bank = [PS[i // 2][:, 512 * (i % 2):512 * (i % 2) + 512] for i in range(8)]

        s = {n: sem(n) for n in (
            "consts_in", "x_in", "x_ready", "x_stored", "xp_in", "xr_in", "xr_ready", "stage_end", "slot_free", "dve_chain", "act_chain",
            "layer_in", "mod_done", "gates_out", "gate_in", "silu_done",
            "sq_done", "var_ready", "rms_ready", "xn_ready", "xT_done", "hT_act", "hT_dve",
            "proj_done", "ev_act", "ev_dve",
            "hg_absz", "hg_lsig", "hg_mix", "hg_mixed", "hg_karg", "hg_k", "hg_qarg", "hg_qexp", "hg_qk",
            "lv_diff", "lv_exp", "lv_ops", "lv_pe", "lv_used", "st_diff", "st_exp", "st_ops", "st_tr", "st_kht",
            "st_u", "st_hist", "st_out", "st_saved", "ro_ms", "ro_r", "ro_garg", "ro_g",
            "rope_ready", "rope_T", "rope_used",
            "q_staged", "scores_done", "max_ready", "exp_done", "trans_done", "pt_ready", "pv_done", "norm_done",
            "bias_used", "bias_in0", "bias_in1", "bias_ready",
            "mixT_done", "mixT_used", "y_done", "y_used",
            "pq_done", "pq_used", "set_v", "set_a", "sub_in", "s_done", "s_used", "gexp", "gready", "sel_ready", "selT_done", "selT_used",
            "one_ready", "rows_ready", "eq_want", "eq_done", "u_hi", "u_lo", "v_hi", "h_hi", "gfull", "g_hi", "down_done", "one_used", "g_used", "hu_done", "gelu_done", "gated", "y_acc", "x_out", "fin_ready", "fin_out0", "fin_out1", "nrm_in")}
        w_ready = [sem(f"w_ready{i}") for i in range(SLOTS)]
        block = ctx.enter_context(nc.Block())
        N_STAGED = 4

        def stage_end(eng, tally, name):
            tally["stage"] = tally.get("stage", 0) + 1
            eng.drain().then_inc(s["stage_end"], 1)
            eng.wait_ge(s["stage_end"], N_STAGED * tally["stage"])


        def staged(eng, tally):
            def end(name):
                stage_end(eng, tally, name)
            return end

        @block.sync
        def _(sp):
            tally = {"tiles": 0}

            def stream(src, count):
                base = tally["tiles"]

                def four(i, first):
                    for sl in range(SLOTS):
                        if not first:
                            sp.wait_ge(s["slot_free"], i * SLOTS + (base + sl - SLOTS + 1))
                        sp.dma_start(ring[:, sl, :], src[bass.ds(i * SLOTS + sl, 1)].rearrange("o p f -> p (o f)")
                                     ).then_inc(w_ready[sl], 16)
                if base == 0:
                    four(0, True)
                    with sp.Fori(1, count // SLOTS) as i:
                        four(i, False)
                else:
                    with sp.Fori(0, count // SLOTS) as i:
                        four(i, False)
                tally["tiles"] += count

            for l in range(DEPTH):
                stream(d["wcat"][l], MOD_TILES + IN_TILES + OUT_TILES)
                for _ in passes_of(l):
                    stream(d["wq"][l], WQ_TILES)
                    stream(d["experts"][l], PK)

        @block.gpsimd
        def _(pool):
            t = {}
            end = staged(pool, t)

            def const(dst, src):
                pool.dma_start(dst, src).then_inc(s["consts_in"], 16)

            pool.nop().then_inc(s["bias_ready"], 1)
            for dst, src in ((ident[:, :], d["ident"]), (iota[:, :], d["iota"]), (c0, d["c"]), (lbx, d["lb"])):
                const(dst, src)

            def tokens(l, b):
                if l:
                    return d["xs"][b * P:(b + 1) * P, :]
                return d["ctx"][b * P:(b + 1) * P, :] if b < CB else d["x"][(b - CB) * P:(b - CB + 1) * P, :]

            stored = 0
            for l in range(DEPTH):
                if l:
                    pool.wait_ge(s["x_stored"], 16 * stored)
                for b in range(NB):
                    pool.dma_start(xin[:, b, :], tokens(l, b)).then_inc(s["x_in"], 16)
                for dst, src in ((bT, d["bT"][l]), (nw, d["nw"][l]),
                                 (brow[0:2, :], d["bgate"][l:l + 1, :].broadcast_to([2, 2048])),
                                 (sink, d["sink"][l:l + 1, :].broadcast_to([P, SWA_H])),
                                 (arena[:, CST:CST + 512], d["masks"]), (arena[:, CST + 512:CST + 768], d["rope"]),
                                 (arena[:, CST + 768:CST + 1024], d["swam"]), (natm, d["natm"]),
                                 (hnw, d["hnw"][l:l + 1, :].broadcast_to([P, 256]))):
                    pool.dma_start(dst, src).then_inc(s["layer_in"], 16)
                pool.wait_ge(s["mod_done"], l + 1)
                pool.dma_start(d["gates"][l], grow[0:2, :]).then_inc(s["gates_out"], 16)
                pool.wait_ge(s["gates_out"], 16 * (l + 1))
                end(f"mod{l}")
                end(f"norm{l}")
                end(f"projA{l}")
                end(f"hg{l}")
                end(f"readout{l}")
                end(f"projB{l}")
                end(f"rope{l}")
                U = 4 + (CB if first_block(l) == 0 else 0)
                nbase = t.get("nat", 0)

                def bias(h, qb, wait_value):
                    pool.wait_ge(s["bias_used"], wait_value)
                    for r2 in range(2):
                        x0 = NAT_ROWS - 1 - (2 * qb + r2)
                        pool.dma_start(biast[qb % 2][64 * r2:64 * r2 + 64, :],
                                       d["rpb"][l, bass.ds(h, 1), :, x0 * 64:(x0 + 8) * 64].rearrange("o c f -> (o c) f")
                                       ).then_inc(s[f"bias_in{qb % 2}"], 16)

                def masked(h, qb):
                    pool.wait_ge(s[f"bias_in{qb % 2}"], h * 64 + (32 * (qb // 2) + 32 + 16 * nbase))
                    bt = biast[qb % 2].rearrange("p (r c) -> p r c", c=GRID_W)
                    pool.tensor_tensor(bt, bt, natm.unsqueeze(1).broadcast_to([P, 8, GRID_W]), ALU.add
                                       ).then_inc(s["bias_ready"], 1)

                ub = t.get("bu", 1)
                with pool.Fori(0, NAT_H) as h:
                    for qb in range(4):
                        bias(h, qb, h * 4 + (ub + max(qb - 1, 0)))
                        masked(h, qb)
                t["bu"] = ub + 4 * NAT_H
                t["nat"] = nbase + 4 * NAT_H
                end(f"attn{l}")
                for st in range(2):
                    pool.dma_start(gateb[:, st, :], d["gates"][l, st:st + 1, 0:D].broadcast_to([P, D])
                                   ).then_inc(s["gate_in"], 16)
                for b in range(first_block(l), NB):
                    pool.dma_start(xw[:, b, :], tokens(l, b)).then_inc(s["gate_in"], 16)
                end(f"mixT{l}")
                yb = t.get("yb", 0)
                for i, b in enumerate(range(first_block(l), NB)):
                    pool.wait_ge(s["x_ready"], yb + i + 1)
                    pool.dma_start(d["xs"][b * P:(b + 1) * P, :], xw[:, b, :]).then_inc(s["x_stored"], 16)
                    stored += 1
                t["yb"] = yb + NB - first_block(l)
                pool.wait_ge(s["x_stored"], 16 * stored)
                end(f"mix{l}")

                def load_pass(b0):
                    for i in range(2):
                        pool.dma_start(xl[:, i, :], d["xs"][(b0 + i) * P:(b0 + i + 1) * P, :]).then_inc(s["xp_in"], 16)

                load_pass(passes_of(l)[0])
                for pn, b0 in enumerate(passes_of(l)):
                    ps_ = t.get("pass", 0)
                    pool.dma_start(subk, d["subk"][l]).then_inc(s["sub_in"], 16)
                    end(f"pnorm{l}{b0}")
                    end(f"pq{l}{b0}")
                    full = [P, HEADS, TOPK, TOPK]
                    for tb in range(2):
                        pool.wait_ge(s["eq_want"], 2 * ps_ + tb + 1)
                        tfh = tifs[tb].rearrange("p (h o) k -> p h o k", o=2)
                        for v in ((0, 1) if tb == 0 else (1,)):
                            last = pool.tensor_tensor(eqs[v], eqs[v], tfh[:, :, v, :].unsqueeze(2).broadcast_to(full),
                                                      ALU.mult)
                        last.then_inc(s["eq_done"], 1)
                    end(f"topk{l}{b0}")
                    gb = ps_ * (PASS // 4)

                    def gate_rows(i, first):
                        for g in range(GD):
                            pool.wait_ge(s["one_ready"], i * GD + (gb + g + 1))
                            if not first or g >= 2:
                                pool.wait_ge(s["rows_ready"], i * GD + (gb + g))
                                pool.wait_ge(s["one_used"], i * GD + (gb + g - 1))
                                pool.tensor_tensor(small[:, 159:160], small[:, 84:85], small[:, 84:85], ALU.add)
                            pool.tensor_tensor(oneA[g % 2], oneR[g].bitcast(F32),
                                               arena[:, bass.ds(i * (4 * GD) + (KT0 + 2 * PASS + 4 * g), 4)].unsqueeze(2)
                                               .broadcast_to([P, 4, P]), ALU.mult).then_inc(s["rows_ready"], 1)

                    gate_rows(0, True)
                    with pool.Fori(1, PASS // (4 * GD)) as i:
                        gate_rows(i, False)
                    end(f"gbuild{l}{b0}")
                    end(f"gemm{l}{b0}")
                    t["pass"] = ps_ + 1
                    st = 1 if b0 < CB else 0
                    pool.dma_start(gbP, d["gates"][l, st:st + 1, D:2 * D].broadcast_to([P, D])
                                   ).then_inc(s["gate_in"], 16)
                    for i in range(2):
                        pool.dma_start(xr[:, i, :], d["xs"][(b0 + i) * P:(b0 + i + 1) * P, :]).then_inc(s["gate_in"], 16)
                    if b0 + 2 < NB:
                        load_pass(b0 + 2)
                    for i in range(2):
                        pool.wait_ge(s["xr_ready"], 2 * ps_ + i + 1)
                        pool.dma_start(d["xs"][(b0 + i) * P:(b0 + i + 1) * P, :], xr[:, i, :]).then_inc(s["x_stored"], 16)
                        stored += 1
                    pool.wait_ge(s["x_stored"], 16 * stored)
                    end(f"pres{l}{b0}")
            pool.dma_start(gbP, d["fnw"].broadcast_to([P, D])).then_inc(s["nrm_in"], 16)
            for b in range(4):
                pool.dma_start(xf[:, b, :], d["xs"][(CB + b) * P:(CB + b + 1) * P, :]).then_inc(s["nrm_in"], 16)
            for b in range(4):
                pool.wait_ge(s["fin_ready"], b + 1)
                pool.dma_start(out[b * P:(b + 1) * P, :], xp[b % 2]).then_inc(s[f"fin_out{b % 2}"], 16)
            for b in range(2):
                pool.wait_ge(s[f"fin_out{b}"], 32)

        def pieces(kind, j):
            if j < 0:
                return [(0, 0, CTX)]
            lo, hi = (0, 4) if kind == "nat" else (max(0, j - 1), min(4, j + 2))
            n1 = min(2, hi - lo)
            res = [(0, 0, CTX), (CTX, CTX + lo * P, n1 * P)]
            if hi - lo > n1:
                res.append((CTX + n1 * P, CTX + (lo + n1) * P, (hi - lo - n1) * P))
            return res

        def units(l):
            return [-2, -1, 0, 1, 2, 3] if first_block(l) == 0 else [0, 1, 2, 3]

        def width(kind, j):
            return sum(n for _, _, n in pieces(kind, j))

        def key_blocks(kind, j):
            return [t0 // P + i for _, t0, n in pieces(kind, j) for i in range(n // P)]

        def items(tiles):
            res = []
            for t in tiles:
                if t < 3 or t >= 9:
                    res += [("feat", t, (m, h)) for m in range(2) for h in range(2)]
                else:
                    res += [("tok", t, b) for b in range(NB)]
            return res

        def evacuate(op, item, ps):
            kind, tl, part = item
            if kind == "tok":
                b = part
                dst = (hvg[:, b, (tl - 3) * TW:(tl - 2) * TW] if tl < 5 else
                       sqk[:, b, (tl - 5) * TW:(tl - 4) * TW] if tl < 7 else
                       v8[:, b, (tl - 7) * TW:(tl - 6) * TW])
                return op(dst, ps[:, 0:TW])
            m, h = part
            half = slice(h * 384, h * 384 + 384)
            if tl < 3:
                return op(hgF[:, 2 * tl + m, half], ps[:, 0:384])
            ft = 2 * (tl - 9) + m
            for e in range(2):
                if ft < 3:
                    base = (6 + 2 * ft + e) * TOK
                    dst = q12[0:64, base + h * 384:base + h * 384 + 384]
                else:
                    base = (2 + 2 * (ft - 3) + e) * TOK
                    dst = k8[0:64, base + h * 384:base + h * 384 + 384]
                last = op(dst, ps[64 * e:64 * e + 64, 0:384])
            return last

        def lv_halves(ap3, lv):
            H = 1 << lv
            v = ap3.rearrange("p c (b h) -> p c b h", h=2 * H)
            return v[:, :, :, 0:H], v[:, :, :, H:2 * H]

        def chunks3(ap):
            return ap.rearrange("p (c t) -> p c t", t=P)

        @block.tensor
        def _(pe):
            t = {"tiles": 0, "items": 0}
            end = staged(pe, t)

            def slot(sl):
                return ring[:, sl, :].rearrange("p (k c) -> p k c", k=KD)

            def tile_in(sl, i=0):
                pe.wait_ge(w_ready[sl], i * 16 + 16 * (t["tiles"] // SLOTS + 1))

            def project(tiles):
                its = items(tiles)
                for n, (kind, tl, part) in enumerate(its):
                    n += t["items"]
                    if n >= 4:
                        pe.wait_ge(s["ev_dve" if n % 2 else "ev_act"], (n - 4) // 2 + 1)
                    g = t["tiles"]
                    w = slot(g % SLOTS)
                    pe.wait_ge(w_ready[g % SLOTS], 16 * (g // SLOTS + 1))
                    for k in range(KD):
                        if kind == "feat":
                            m, h = part
                            mm = pe.matmul(bank[n % 4][:, 0:384], w[:, k, m * P:(m + 1) * P],
                                           hT[:, k, h * 384:h * 384 + 384], start=(k == 0), stop=(k == KD - 1))
                        else:
                            mm = pe.matmul(bank[n % 4][:, 0:TW], hT[:, k, part * P:(part + 1) * P], w[:, k, :],
                                           start=(k == 0), stop=(k == KD - 1))
                    mm.then_inc(s["proj_done"], 1)
                    if n - t["items"] + 1 == len(its) or its[n - t["items"] + 1][1] != tl:
                        pe.wait_ge(s["proj_done"], n + 1)
                        pe.nop().then_inc(s["slot_free"], 1)
                        t["tiles"] += 1
                t["items"] += len(its)

            def norm(nblk):
                base = t.get("norm", 0)
                for i in range(nblk):
                    n = base + i
                    pe.wait_ge(s["xn_ready"], n + 1)
                    if n >= 1:
                        pe.wait_ge(s["hT_act"], n)
                        pe.wait_ge(s["hT_dve"], n)
                    for k in range(KD):
                        mm = pe.transpose(bank[k // 4][:, (k % 4) * P:(k % 4 + 1) * P],
                                          t["xn"][i % 2][:, k * P:(k + 1) * P], ident[:, :])
                    mm.then_inc(s["xT_done"], 1)
                t["norm"] = base + nblk

            def attention(kind, l, head, first, last_g):
                us = units(l)
                def scores(i):
                    j = us[i]
                    if i == 0 or kind == "nat":
                        pe.wait_ge(s["rope_ready"], 4 * (l + 1))
                        pe.wait_ge(s["q_staged"], last_g)
                    if i >= 2:
                        pe.wait_ge(s["exp_done"], first + (i - 1))
                    for c, t0, n in pieces(kind, j):
                        if kind == "swa":
                            rhs = k8[0:64, (head // 3) * TOK + t0:(head // 3) * TOK + t0 + n]
                        else:
                            rhs = k8[0:64, bass.ds(head * TOK + (2 * TOK + t0), n)]
                        mm = pe.matmul(PS[i % 2][:, c:c + n], qst[0:64, (j + 2) * P:(j + 3) * P], rhs,
                                       start=True, stop=True)
                    mm.then_inc(s["scores_done"], 1)

                def trans(i):
                    pe.wait_ge(s["exp_done"], first + (i + 1))
                    if i >= 1:
                        pe.wait_ge(s["pt_ready"], first + i)
                    for c in range(width(kind, us[i]) // P):
                        mm = pe.transpose(PS[2][:, c * P:(c + 1) * P], Pm[i % 2][:, c * P:(c + 1) * P], ident[:, :])
                    mm.then_inc(s["trans_done"], 1)

                def values(i):
                    pe.wait_ge(s["pt_ready"], first + (i + 1))
                    pe.wait_ge(s["norm_done"], first + max(i - 1, 0))
                    kb = key_blocks(kind, us[i])
                    for c, b in enumerate(kb):
                        if kind == "swa":
                            rhs = v8[:, b, (head // 3) * 64:(head // 3) * 64 + 64]
                        else:
                            rhs = v8[:, b, bass.ds(head * 64 + 128, 64)]
                        mm = pe.matmul(bank[6 + i % 2][:, 0:64], PT[i % 2][:, c * P:(c + 1) * P], rhs,
                                       start=(c == 0), stop=(c == len(kb) - 1))
                    mm.then_inc(s["pv_done"], 1)

                n = len(us)
                scores(0)
                for i in range(n + 1):
                    if i + 1 < n:
                        scores(i + 1)
                    if i < n:
                        trans(i)
                    if i >= 1:
                        values(i - 1)

            for name in ("scores_done", "trans_done", "pv_done"):
                pe.nop().then_inc(s[name], 1)
            pe.wait_ge(s["consts_in"], 64)
            for l in range(DEPTH):
                fb = first_block(l)
                pe.wait_ge(s["silu_done"], 1)
                with pe.Fori(0, 4) as i:
                    for sl in range(SLOTS):
                        tile_in(sl, i)
                        for m in range(2):
                            for k in range(KD):
                                mm = pe.matmul(bank[0][:, bass.ds(i * 16 + (sl * 4 + m * 2), 2)],
                                               slot(sl)[:, k, m * P:(m + 1) * P], sT[:, k, :],
                                               start=(k == 0), stop=(k == KD - 1))
                        mm.then_inc(s["slot_free"], 1)
                t["tiles"] += 16
                for half in range(2):
                    for sl in range(SLOTS):
                        tile_in(sl)
                        c = sl * TW
                        for k in range(KD):
                            mm = pe.matmul(PS[1 + half][0:2, c:c + TW], sT[:, k, :],
                                           slot(sl)[:, k, :], start=(k == 0), stop=(k == KD - 1))
                        mm.then_inc(s["slot_free"], 1)
                    t["tiles"] += 4
                end(f"mod{l}")
                t["xn"] = xn
                norm(NB)
                end(f"norm{l}")
                project(range(0, 5))
                end(f"projA{l}")

                with pe.Fori(0, 2) as pr:
                    for dr in range(2):
                        def n_(per_dir, k):
                            return pr * (2 * per_dir) + (4 * l + dr) * per_dir + k

                        pe.wait_ge(s["hg_qk"], n_(1, 1))
                        pe.wait_ge(s["hg_k"], n_(1, 1))
                        for lv in range(LEVELS):
                            pe.wait_ge(s["lv_ops"], n_(LEVELS, lv + 1))
                            if lv >= 3:
                                pe.wait_ge(s["lv_used"], n_(LEVELS + 1, lv - 2))
                            for e in range(2):
                                qhalf = lv_halves(chunks3(Qt[lv % 2][64 * e:64 * e + 64, :]), lv)[1 - dr]
                                for c in range(NB):
                                    mm = pe.matmul(bank[2 * (lv % 3) + e][:, c * 64:(c + 1) * 64],
                                                   Kt[lv % 2][64 * e:64 * e + 64, c * P:(c + 1) * P],
                                                   qhalf[:, c], start=True, stop=True)
                            mm.then_inc(s["lv_pe"], 1)
                        pe.wait_ge(s["lv_used"], n_(LEVELS + 1, LEVELS - 1))
                        for e in range(2):
                            for c in range(NB):
                                mm = pe.matmul(PS[1 + e][:, c * P:(c + 1) * P], k_s[64 * e:64 * e + 64, c * P:(c + 1) * P],
                                               q_s[64 * e:64 * e + 64, c * P:(c + 1) * P], start=True, stop=True)
                        mm.then_inc(s["lv_pe"], 1)
                        pe.wait_ge(s["st_ops"], n_(1, 1))
                        pe.wait_ge(s["lv_used"], n_(LEVELS + 1, LEVELS + 1))
                        for c in range(NB):
                            mm = pe.transpose(PS[0][:, c * P:(c + 1) * P], Kh[:, c * P:(c + 1) * P], ident[:, :])
                        mm.then_inc(s["st_tr"], 1)
                        pe.wait_ge(s["st_kht"], n_(1, 1))
                        for c in range(NB):
                            mm = pe.matmul(PS[1][:, c * P:(c + 1) * P], KhT[:, c * P:(c + 1) * P],
                                           hvg[:, c, bass.ds(pr * P, P)], start=True, stop=True)
                        mm.then_inc(s["st_u"], 1)
                        pe.wait_ge(s["st_hist"], n_(1, 1))
                        order = [0, 1, 2, 3, 4, 5] if dr == 0 else [1, 0, 5, 4, 3, 2]
                        for e in range(2):
                            for n, c in enumerate(order):
                                if c < fb:
                                    continue
                                pe.matmul(bank[4 + e][:, c * 64:c * 64 + 64], Asc[:, e, c, :],
                                          hvg[:, c, bass.ds(pr * P + 64 * e, 64)], start=True, stop=False)
                                mm = pe.matmul(bank[4 + e][:, c * 64:c * 64 + 64],
                                               Qh[64 * e:64 * e + 64, c * P:(c + 1) * P],
                                               Sh[64 * e:64 * e + 64, n, :], start=False, stop=True)
                        mm.then_inc(s["st_out"], 1)
                        pe.wait_ge(s["st_saved"], n_(1, 1))
                end(f"hg{l}")
                end(f"readout{l}")
                project(range(5, 12))
                end(f"projB{l}")
                base = t.get("rope", 0)
                for b in range(NB):
                    n = base + b
                    if b >= CB:
                        pe.wait_ge(s["rope_ready"], 4 * l + b - CB + 1)
                    if n >= 1:
                        pe.wait_ge(s["rope_used"], n)
                    src = sqk[:, b, :] if b < CB else rq
                    for m in range(4):
                        mm = pe.transpose(bank[0][:, m * P:(m + 1) * P], src[:, m * P:(m + 1) * P], ident[:, :])
                    mm.then_inc(s["rope_T"], 1)
                t["rope"] = base + NB
                end(f"rope{l}")
                U = len(units(l))
                u0, h0 = t.get("units", 1), t.get("heads", 0)
                for kv in range(SWA_KV):
                    with pe.Fori(0, 3) as g:
                        attention("swa", l, kv * 3, g * U + (u0 + kv * 3 * U), g + (h0 + kv * 3 + 1))
                with pe.Fori(0, NAT_H) as h:
                    attention("nat", l, h, h * U + (u0 + 6 * U), h + (h0 + 7))
                t["units"], t["heads"] = u0 + 12 * U, h0 + 12
                end(f"attn{l}")
                base = t.get("mixb", 0)
                for i, b in enumerate(range(fb, NB)):
                    n = base + i
                    if n >= 1:
                        pe.wait_ge(s["mixT_used"], 2 * n)
                    for k in range(KD):
                        mm = pe.transpose(bank[k // 4][:, (k % 4) * P:(k % 4 + 1) * P],
                                          mix[:, b, k * P:(k + 1) * P], ident[:, :])
                    mm.then_inc(s["mixT_done"], 1)
                t["mixb"] = base + NB - fb
                end(f"mixT{l}")
                base = t.get("y", 0)
                for sl in range(SLOTS):
                    tile_in(sl)
                for i, b in enumerate(range(fb, NB)):
                    for tl in range(OUT_TILES):
                        n = base + i * OUT_TILES + tl
                        if n >= 4:
                            pe.wait_ge(s["y_used"], n - 3)
                        for k in range(KD):
                            mm = pe.matmul(bank[n % 4][:, 0:TW], mixT[:, k, b * P:(b + 1) * P],
                                           slot(tl)[:, k, :], start=(k == 0), stop=(k == KD - 1))
                        mm.then_inc(s["y_done"], 1)
                pe.wait_ge(s["y_done"], n + 1)
                pe.nop().then_inc(s["slot_free"], 4)
                t["tiles"] += 4
                t["y"] = base + OUT_TILES * (NB - fb)
                end(f"mix{l}")

                for b0 in passes_of(l):
                    t["xn"] = xp
                    norm(2)
                    end(f"pnorm{l}{b0}")
                    ps_ = t.get("pass", 0)
                    qb = 16 * ps_
                    with pe.Fori(0, WQ_TILES // SLOTS) as i:
                        for sl in range(SLOTS):
                            tile_in(sl, i)
                            w = ring[:, sl, :].rearrange("p (m k c) -> p m k c", m=2, k=KD)
                            for m in range(2):
                                n = sl * 2 + m
                                if n >= 4:
                                    pe.wait_ge(s["pq_used"], i * 8 + (qb + n - 3))
                                for k in range(KD):
                                    mm = pe.matmul(bank[n % 4][:, 0:PASS], w[:, m, k, :], hP[:, k, :],
                                                   start=(k == 0), stop=(k == KD - 1))
                                mm.then_inc(s["pq_done"], 1)
                            pe.wait_ge(s["pq_done"], i * 8 + (qb + sl * 2 + 2))
                            pe.nop().then_inc(s["slot_free"], 1)
                        pe.wait_ge(s["pq_used"], i * 8 + (qb + 8))
                    t["tiles"] += WQ_TILES
                    end(f"pq{l}{b0}")
                    pe.wait_ge(s["sub_in"], 16 * (ps_ + 1))
                    for tb in range(2):
                        if tb:
                            pe.wait_ge(s["s_used"], 2 * ps_ + 1)
                        for hp in range(16):
                            mm = pe.matmul(bank[hp // 4][:, (hp % 4) * P:(hp % 4 + 1) * P],
                                           qP[:, hp, tb * P:(tb + 1) * P], subk[:, hp, :], start=True, stop=True)
                        mm.then_inc(s["s_done"], 1)
                    for tb in range(2):
                        pe.wait_ge(s["sel_ready"], 2 * ps_ + tb + 1)
                        if tb:
                            pe.wait_ge(s["selT_used"], 2 * ps_ + 1)
                        for v in range(3):
                            mm = pe.transpose(bank[4][:, v * P:(v + 1) * P], sel[:, v, :], ident[:, :])
                        mm.then_inc(s["selT_done"], 1)
                    end(f"topk{l}{b0}")
                    gb = ps_ * (PASS // 4)

                    def gates_of(i, first):
                        for g in range(GD):
                            pe.wait_ge(s["rows_ready"], i * GD + (gb + g + 1))
                            if not first:
                                pe.wait_ge(s["g_used"], i * GD + (gb + g + 1 - GD))
                            for q in range(4):
                                mm = pe.matmul(bank[4 + g][:, q * P:(q + 1) * P], oneA[g % 2][:, q, :],
                                               oneB[g][:, q, :].bitcast(F32), start=True, stop=True)
                            mm.then_inc(s["one_used"], 1)

                    gates_of(0, True)
                    with pe.Fori(1, PASS // (4 * GD)) as i:
                        gates_of(i, False)
                    end(f"gbuild{l}{b0}")

                    cbase = ps_ * PK

                    def up(i, c, sl):
                        pe.wait_ge(s["u_hi"], i * SLOTS + (cbase + c + 1))
                        if not (isinstance(i, int) and i == 0 and c < 2):
                            pe.wait_ge(s["gelu_done"], i * SLOTS + (cbase + c - 1))
                        for part, (w, h) in enumerate(((0, 0), (0, 1), (1, 0))):
                            if w:
                                pe.wait_ge(s["u_lo"], i * SLOTS + (cbase + c + 1))
                            u = wS[:, w, :].rearrange("p (k e) -> p k e", k=KD)
                            for k in range(KD):
                                mm = pe.matmul(bank[c % 2][:, 0:PASS], u[:, k, :], hS[:, h, k, :],
                                               start=(part == 0 and k == 0), stop=(part == 2 and k == KD - 1))
                        mm.then_inc(s["hu_done"], 1)

                    def down(i, c, sl, start=False, stop=False):
                        pe.wait_ge(s["gated"], i * SLOTS + (cbase + c + 1))
                        pe.wait_ge(s["v_hi"], i * SLOTS + (cbase + c + 1))
                        for part, (g, v) in enumerate(((0, 0), (1, 0), (0, 1))):
                            if v:
                                pe.wait_ge(s["slot_free"], i * SLOTS + (t["tiles"] + c + 1))
                            for tb in range(2):
                                for h in range(2):
                                    mm = pe.matmul(bank[4 + 2 * tb + h],
                                                   gS_[:, 2 * (c % 2) + g, tb * P:(tb + 1) * P],
                                                   wS[:, 2 + v, 512 * h:512 * h + 512],
                                                   start=(start and part == 0), stop=(stop and part == 2))
                        mm.then_inc(s["down_done"], 1)

                    def group(i, first, last):
                        for sl in range(SLOTS):
                            if sl < SLOTS - 1:
                                up(i, sl + 1, sl + 1)
                            elif not last:
                                up(i + 1, 0, 0)
                            down(i, sl, sl, first and sl == 0, last and sl == SLOTS - 1)

                    up(0, 0, 0)
                    group(0, True, False)
                    with pe.Fori(1, PK // SLOTS - 1) as i:
                        group(i, False, False)
                    group(PK // SLOTS - 1, False, True)
                    t["tiles"] += PK
                    t["pass"] = ps_ + 1
                    end(f"gemm{l}{b0}")
                    end(f"pres{l}{b0}")

        @block.scalar
        def _(act):
            t = {"items": 0, "tiles": 0}
            end = staged(act, t)
            link = Chain(act, s["act_chain"])

            def norm(blocks, src, nidx, bufs, dst):
                base = t.get("norm", 0)

                def pre(i):
                    n = base + i
                    if i >= 2:
                        act.wait_ge(s["xT_done"], n - 1)
                    act.activation(bufs[i % 2], src[:, i, :], ACT.Square,
                                   accum_out=ss[:, i % 2:i % 2 + 1]).then_inc(s["sq_done"], 1)
                    act.wait_ge(s["var_ready"], n + 1)
                    link(act.activation(rs[:, i % 2:i % 2 + 1], ss[:, i % 2:i % 2 + 1], ACT.Ln))
                    act.activation(rs[:, i % 2:i % 2 + 1], rs[:, i % 2:i % 2 + 1], ACT.Exp, scale=-0.5
                                   ).then_inc(s["rms_ready"], 1)

                pre(0)
                for i, b in enumerate(blocks):
                    if i + 1 < len(blocks):
                        pre(i + 1)
                    st = 1 if b < CB else 0
                    act.wait_ge(s["xT_done"], base + i + 1)
                    for k in range(4):
                        last = act.activation(dst[:, k, i * P:(i + 1) * P], bank[0][:, k * P:(k + 1) * P], ACT.Identity,
                                              scale=modA[:, nidx, k, st:st + 1], bias=modp[:, nidx * 16 + k, st:st + 1])
                    last.then_inc(s["hT_act"], 1)
                t["norm"] = base + len(blocks)
                if dst is hP:
                    act.wait_ge(s["hT_act"], t["norm"])
                    act.wait_ge(s["hT_dve"], t["norm"])
                    act.activation(hS[:, 0], hP, ACT.Copy).then_inc(s["h_hi"], 1)

            def project(tiles):
                its = items(tiles)
                for n, it in enumerate(its):
                    n += t["items"]
                    if n % 2 == 0:
                        act.wait_ge(s["proj_done"], n + 1)
                        evacuate(lambda dd, ss_: act.activation(dd, ss_, ACT.Copy), it, bank[n % 4]
                                 ).then_inc(s["ev_act"], 1)
                t["items"] += len(its)

            def attention(kind, l, head, first):
                us = units(l)

                def exps(i):
                    w = width(kind, us[i])
                    act.wait_ge(s["max_ready"], first + (i + 1))
                    act.wait_ge(s["norm_done"], first + max(i - 3, 0))
                    if i >= 2:
                        act.wait_ge(s["trans_done"], first + (i - 1))
                    if kind == "swa":
                        act.activation(esink[:, i % 4:i % 4 + 1], sinkst, ACT.Exp, bias=nm[:, i % 4:i % 4 + 1])
                    act.activation(Pm[i % 2][:, 0:w], PS[i % 2][:, 0:w], ACT.Exp, bias=nm[:, i % 4:i % 4 + 1],
                                   accum_out=rsum[:, i % 4:i % 4 + 1]).then_inc(s["exp_done"], 1)

                def evac(i):
                    w = width(kind, us[i])
                    act.wait_ge(s["trans_done"], first + (i + 1))
                    act.wait_ge(s["pv_done"], first + max(i - 1, 0))
                    act.activation(PT[i % 2][:, 0:w], PS[2][:, 0:w], ACT.Copy).then_inc(s["pt_ready"], 1)

                exps(0)
                for i in range(len(us)):
                    evac(i)
                    if i + 1 < len(us):
                        exps(i + 1)

            for name in ("exp_done", "pt_ready"):
                act.nop().then_inc(s[name], 1)
            act.wait_ge(s["set_v"], 2)
            act.activation(sT[:, :, :], sT[:, :, :], ACT.Exp).then_inc(s["set_a"], 1)
            act.activation(lbt, lbx, ACT.Exp).then_inc(s["set_a"], 1)
            act.wait_ge(s["set_v"], 3)
            act.activation(lbt[:, :, :, 1:2], lbt[:, :, :, 0:1], ACT.Ln).then_inc(s["set_a"], 1)
            for l in range(DEPTH):
                fb = first_block(l)
                end(f"mod{l}")
                act.wait_ge(s["x_in"], 16 * NB * (l + 1))
                norm(list(range(NB)), xin, 0, xn, hT)
                end(f"norm{l}")
                project(range(0, 5))
                end(f"projA{l}")
                with link.loop(2, 4 if l else 2) as pr:
                    for dr in range(2):
                        def n_(per_dir, k):
                            return pr * (2 * per_dir) + (4 * l + dr) * per_dir + k

                        if dr == 0:
                            act.wait_ge(s["hg_qarg"], pr + (2 * l + 1))
                            act.activation(t_s, t_s, ACT.Exp).then_inc(s["hg_qexp"], 1)
                        act.wait_ge(s["hg_absz"], n_(1, 1))
                        link(act.activation(t_s, t_s, ACT.Exp))
                        act.activation(t_s, t_s, ACT.Ln, bias=1.0).then_inc(s["hg_lsig"], 1)
                        act.wait_ge(s["hg_karg"], n_(1, 1))
                        act.activation(k_s, k_s, ACT.Exp, bias=lbst[:, dr, 1:2] if l else 0.0).then_inc(s["hg_k"], 1)
                        if l:
                            act.wait_ge(s["hg_mix"], pr * 2 + (dr + 1))
                            link(act.activation(t_s, t_s, ACT.Exp))
                            act.activation(t_s, t_s, ACT.Ln, bias=1.0).then_inc(s["hg_mixed"], 1)
                        for lv in range(LEVELS):
                            act.wait_ge(s["lv_diff"], n_(LEVELS, lv + 1))
                            act.activation(Dl[lv % 2], Dl[lv % 2], ACT.Exp).then_inc(s["lv_exp"], 1)
                        act.wait_ge(s["st_diff"], n_(1, 1))
                        incl, excl = Bx[:, :, 1:P + 1], Bx[:, :, 0:P]
                        act.activation(chunks3(Qh if dr == 0 else Kh), incl if dr == 0 else excl, ACT.Exp)
                        act.activation(Kh if dr == 0 else Qh, Dl[0], ACT.Exp)
                        act.activation(Fd, Bx[:, :, P:P + 1].rearrange("p c o -> p (c o)"), ACT.Exp
                                       ).then_inc(s["st_exp"], 1)
                        act.wait_ge(s["st_tr"], n_(1, 1))
                        act.activation(KhT, PS[0][:, 0:TOK], ACT.Copy).then_inc(s["st_kht"], 1)
                end(f"hg{l}")
                act.wait_ge(s["ro_ms"], l + 1)
                link(act.activation(rr[:, fb:, :], rr[:, fb:, :], ACT.Ln))
                act.activation(rr[:, fb:, :], rr[:, fb:, :], ACT.Exp, scale=-0.5).then_inc(s["ro_r"], 1)
                act.wait_ge(s["ro_garg"], l + 1)
                act.activation(gT[:, fb:, :], gT[:, fb:, :], ACT.Exp).then_inc(s["ro_g"], 1)
                end(f"readout{l}")
                project(range(5, 12))
                end(f"projB{l}")
                base = t.get("rope", 0)
                q12v = q12.rearrange("p (h t) -> p h t", t=TOK)
                k8v = k8.rearrange("p (h t) -> p h t", t=TOK)
                ps4 = bank[0].rearrange("p (m t) -> p m t", t=P)
                for b in range(NB):
                    act.wait_ge(s["rope_T"], base + b + 1)
                    ts = slice(b * P, (b + 1) * P)
                    for e in range(2):
                        act.activation(q12v[0:64, e:6:2, ts], ps4[64 * e:64 * e + 64, 0:3, :], ACT.Copy)
                        last = act.activation(k8v[0:64, e, ts], ps4[64 * e:64 * e + 64, 3, :], ACT.Copy)
                    last.then_inc(s["rope_used"], 1)
                t["rope"] = base + NB
                end(f"rope{l}")
                U = len(units(l))
                u0 = t.get("units", 1)
                for kv in range(SWA_KV):
                    with act.Fori(0, 3) as g:
                        attention("swa", l, g + kv * 3, g * U + (u0 + kv * 3 * U))
                with act.Fori(0, NAT_H) as h:
                    attention("nat", l, h, h * U + (u0 + 6 * U))
                t["units"] = u0 + 12 * U
                end(f"attn{l}")
                base = t.get("mixb", 0)
                for i, b in enumerate(range(fb, NB)):
                    act.wait_ge(s["mixT_done"], base + i + 1)
                    act.activation(mixT[:, 0:4, b * P:(b + 1) * P], bank[0].rearrange("p (k t) -> p k t", t=P),
                                   ACT.Copy).then_inc(s["mixT_used"], 1)
                t["mixb"] = base + NB - fb
                end(f"mixT{l}")
                t["tiles"] += MOD_TILES + IN_TILES + OUT_TILES
                end(f"mix{l}")
                for b0 in passes_of(l):
                    ps_ = t.get("pass", 0)
                    act.wait_ge(s["xp_in"], 32 * (ps_ + 1))
                    norm([b0, b0 + 1], xl, 1, xp, hP)
                    end(f"pnorm{l}{b0}")
                    with act.Fori(0, 2) as i:
                        for n in range(8):
                            act.wait_ge(s["pq_done"], i * 8 + (16 * ps_ + n + 1))
                            act.activation(arena[:, bass.ds(i * (8 * PASS) + n * PASS, PASS)], bank[n % 4][:, 0:PASS],
                                           ACT.Copy).then_inc(s["pq_used"], 1)
                    t["tiles"] += WQ_TILES
                    end(f"pq{l}{b0}")
                    for tb in range(2):
                        act.wait_ge(s["s_done"], 2 * ps_ + tb + 1)
                        if tb:
                            act.wait_ge(s["gexp"], 2 * ps_ + 1)
                        act.activation(sc[:, 0:8, :], PS[0][:, :].rearrange("p (a b) -> p a b", b=P), ACT.Copy)
                        act.activation(sc[:, 8:16, :], PS[1][:, :].rearrange("p (a b) -> p a b", b=P), ACT.Copy
                                       ).then_inc(s["s_used"], 1)
                        act.wait_ge(s["gexp"], 2 * ps_ + tb + 1)
                        act.activation(bss[tb], bss[tb], ACT.Exp).then_inc(s["gready"], 1)
                    end(f"topk{l}{b0}")
                    gb = ps_ * (PASS // 4)
                    with act.Fori(0, PASS // (4 * GD)) as i:
                        for g in range(GD):
                            act.wait_ge(s["one_used"], i * GD + (gb + g + 1))
                            act.activation(G[:, :, bass.ds(i * (4 * GD) + 4 * g, 4)],
                                           bank[4 + g].rearrange("p (t j) -> p j t", j=P), ACT.Copy
                                           ).then_inc(s["g_used"], 1)
                    end(f"gbuild{l}{b0}")
                    cb = ps_ * PK

                    t0 = t["tiles"]

                    def u_high(i, c, first=False):
                        sl = c % SLOTS
                        act.wait_ge(w_ready[sl], (i + c // SLOTS) * 16 + 16 * (t0 // SLOTS + 1))
                        if not first:
                            act.wait_ge(s["hu_done"], i * SLOTS + (cb + c))
                        act.activation(wS[:, 0, :], ring[:, sl, 0:D], ACT.Copy).then_inc(s["u_hi"], 1)

                    def step(i, c, first=False, last=False):
                        act.wait_ge(s["hu_done"], i * SLOTS + (cb + c + 1))
                        if not last:
                            u_high(i, c + 1)
                        if not (first and c < 2):
                            act.wait_ge(s["gated"], i * SLOTS + (cb + c - 1))
                        act.activation(gel[c % 2], bank[c % 2][:, 0:PASS], ACT.Gelu).then_inc(s["gelu_done"], 1)
                        act.wait_ge(s["gfull"], i * SLOTS + (cb + c + 1))
                        act.activation(gS_[:, 2 * (c % 2), :], gel[2 + c % 2], ACT.Copy).then_inc(s["g_hi"], 1)
                        if not (first and c == 0):
                            act.wait_ge(s["down_done"], i * SLOTS + (cb + c))
                        act.activation(wS[:, 2, :], ring[:, c, D:2 * D], ACT.Copy).then_inc(s["v_hi"], 1)

                    u_high(0, 0, True)
                    for c in range(SLOTS):
                        step(0, c, True)
                    with act.Fori(1, PK // SLOTS - 1) as i:
                        for c in range(SLOTS):
                            step(i, c)
                    for c in range(SLOTS):
                        step(PK // SLOTS - 1, c, last=(c == SLOTS - 1))
                    t["tiles"] += PK
                    t["pass"] = ps_ + 1
                    end(f"gemm{l}{b0}")
                    end(f"pres{l}{b0}")
            base = t["norm"]
            act.wait_ge(s["nrm_in"], 80)
            for i in range(4):
                act.activation(yP, xf[:, i, :], ACT.Square, accum_out=ss[:, i % 2:i % 2 + 1]
                               ).then_inc(s["sq_done"], 1)
                act.wait_ge(s["var_ready"], base + i + 1)
                link(act.activation(rs[:, i % 2:i % 2 + 1], ss[:, i % 2:i % 2 + 1], ACT.Ln))
                act.activation(rs[:, i % 2:i % 2 + 1], rs[:, i % 2:i % 2 + 1], ACT.Exp, scale=-0.5
                               ).then_inc(s["rms_ready"], 1)

        @block.vector
        def _(dve):
            t = {"items": 0, "tiles": 0}
            end = staged(dve, t)
            link = Chain(dve, s["dve_chain"])

            def norm(blocks, src, nidx, bufs, dst):
                base = t.get("norm", 0)

                def pre(i):
                    n = base + i
                    c = slice(i % 2, i % 2 + 1)
                    dve.wait_ge(s["sq_done"], n + 1)
                    dve.tensor_scalar(ss[:, c], ss[:, c], 1.0 / D, EPS, ALU.mult, ALU.add).then_inc(s["var_ready"], 1)
                    dve.wait_ge(s["rms_ready"], n + 1)
                    dve.tensor_scalar(bufs[i % 2], src[:, i, :], rs[:, c], None, ALU.mult
                                      ).then_inc(s["xn_ready"], 1)

                pre(0)
                for i, b in enumerate(blocks):
                    if i + 1 < len(blocks):
                        pre(i + 1)
                    st = 1 if b < CB else 0
                    dve.wait_ge(s["xT_done"], base + i + 1)
                    for k in range(4, 8):
                        last = dve.tensor_scalar(dst[:, k, i * P:(i + 1) * P], bank[1][:, (k - 4) * P:(k - 3) * P],
                                                 modA[:, nidx, k, st:st + 1], modp[:, nidx * 16 + k, st:st + 1],
                                                 ALU.mult, ALU.add)
                    last.then_inc(s["hT_dve"], 1)
                t["norm"] = base + len(blocks)
                if dst is hP:
                    dve.wait_ge(s["hT_act"], t["norm"])
                    dve.wait_ge(s["h_hi"], t.get("pass", 0) + 1)
                    dve.tensor_tensor(hS[:, 1], hP, hS[:, 0].bitcast(F32), ALU.subtract)

            def project(tiles):
                its = items(tiles)
                for n, it in enumerate(its):
                    n += t["items"]
                    if n % 2:
                        dve.wait_ge(s["proj_done"], n + 1)
                        evacuate(dve.tensor_copy, it, bank[n % 4]).then_inc(s["ev_dve"], 1)
                t["items"] += len(its)

            def attention(kind, l, head, first, head_n, nat_n):
                us = units(l)

                dve.wait_ge(s["scores_done"], first)
                qoff = head * TOK if kind == "swa" else head * TOK + 6 * TOK
                if kind == "swa":
                    link(dve.tensor_copy(sinkst, sink[:, bass.ds(head, 1)]))
                dve.tensor_scalar(qst[0:64, :], q12[0:64, bass.ds(qoff, TOK)], HD ** -0.5, None, ALU.mult
                                  ).then_inc(s["q_staged"], 1)

                def pre(i):
                    j, w, c = us[i], width(kind, us[i]), slice(i % 4, i % 4 + 1)
                    S = PS[i % 2]
                    dve.wait_ge(s["scores_done"], first + (i + 1))
                    if kind == "swa" and j >= 0:
                        edges = ([(0, CTX)] if j >= 1 else []) + ([(1, CTX + (2 if j >= 1 else 1) * P)] if j < 3 else [])
                        for m, col in edges:
                            last = dve.tensor_tensor(S[:, col:col + P], S[:, col:col + P], swam[:, m, :], ALU.add)
                        link(last)
                    if kind == "nat" and j >= 0:
                        dve.wait_ge(s["bias_ready"], nat_n + (j + 1))
                        dve.tensor_tensor(S[:, CTX:CTX + 512], S[:, CTX:CTX + 512], biast[j % 2], ALU.add
                                          ).then_inc(s["bias_used"], 1)
                        dve.wait_ge(s["bias_used"], nat_n + (j + 1))
                    link(dve.tensor_reduce(mxs[:, c], S[:, 0:w], AX, ALU.max))
                    if kind == "swa":
                        op = dve.tensor_scalar(nm[:, c], mxs[:, c], sinkst, -1.0, ALU.max, ALU.mult)
                    else:
                        op = dve.tensor_scalar(nm[:, c], mxs[:, c], -1.0, None, ALU.mult)
                    op.then_inc(s["max_ready"], 1)

                def post(i):
                    j, c = us[i], slice(i % 4, i % 4 + 1)
                    dve.wait_ge(s["exp_done"], first + (i + 1))
                    if kind == "swa":
                        link(dve.tensor_tensor(den[:, c], rsum[:, c], esink[:, c], ALU.add))
                        link(dve.reciprocal(rden[:, c], den[:, c]))
                        col = head * 64 + 256
                    else:
                        link(dve.reciprocal(rden[:, c], rsum[:, c]))
                        col = head * 64 + (256 + 384)
                    dve.wait_ge(s["pv_done"], first + (i + 1))
                    dve.tensor_scalar(mix[:, j + 2, bass.ds(col, 64)], bank[6 + i % 2][:, 0:64], rden[:, c], None,
                                      ALU.mult).then_inc(s["norm_done"], 1)

                pre(0)
                for i in range(len(us) + 1):
                    if i + 1 < len(us):
                        pre(i + 1)
                    if i:
                        post(i - 1)

            def topk(tb):
                tif, bs, paf, pbf = tifs[tb], bss[tb], pafs[tb], pbfs[tb]
                low = -3.0e38
                for hp in range(16):
                    last = dve.max(tv[:, hp, 0:8], sc[:, hp, :])
                link(last)
                for hp in range(16):
                    dve.max_index(tiu[:, hp, 0:8], tv[:, hp, 0:8], sc[:, hp, :])
                    last = dve.match_replace(sc2[:, hp, :], tv[:, hp, 0:8], sc[:, hp, :], low)
                link(last)
                for hp in range(16):
                    last = dve.max(tv[:, hp, 8:16], sc2[:, hp, :])
                link(last)
                for hp in range(16):
                    last = dve.max_index(tiu[:, hp, 8:16], tv[:, hp, 8:16], sc2[:, hp, :])
                link(last)
                link(dve.tensor_copy(tif, tiu))
                tvh = tv.rearrange("p (h o) k -> p h o k", o=2)
                full = [P, HEADS, TOPK, TOPK]
                link(dve.tensor_tensor(cand.rearrange("p h (a b) -> p h a b", a=TOPK),
                                       tvh[:, :, 0, :].unsqueeze(3).broadcast_to(full),
                                       tvh[:, :, 1, :].unsqueeze(2).broadcast_to(full), ALU.add))
                for h in range(HEADS):
                    last = dve.max(bs[:, h, 0:8], cand[:, h, :])
                link(last)
                for h in range(HEADS):
                    dve.max_index(pu[:, h, 0:8], bs[:, h, 0:8], cand[:, h, :])
                    last = dve.match_replace(cand2[:, h, :], bs[:, h, 0:8], cand[:, h, :], low)
                link(last)
                for h in range(HEADS):
                    last = dve.max(bs[:, h, 8:16], cand2[:, h, :])
                link(last)
                for h in range(HEADS):
                    last = dve.max_index(pu[:, h, 8:16], bs[:, h, 8:16], cand2[:, h, :])
                link(last)
                link(dve.tensor_single_scalar(pa, pu, 4, ALU.logical_shift_right))
                link(dve.tensor_copy(paf, pa))
                link(dve.tensor_single_scalar(pa, pu, 15, ALU.bitwise_and))
                link(dve.tensor_copy(pbf, pa))
                if tb == 0:
                    one_hot_lists(tb, 2 * t.get("pass", 0) + tb + 1)
                link(dve.tensor_copy(gs1, bs[:, :, 0]))
                dve.tensor_tensor(bs, bs, gs1.unsqueeze(2).broadcast_to([P, HEADS, TOPK]), ALU.subtract
                                  ).then_inc(s["gexp"], 1)
                dve.wait_ge(s["gexp"], 2 * t.get("pass", 0) + tb + 1)

            def one_hot_lists(tb, count):
                full = [P, HEADS, TOPK, TOPK]
                for v, at in ((0, pafs[tb]), (1, pbfs[tb])):
                    last = dve.tensor_tensor(eqs[v], at.unsqueeze(3).broadcast_to(full),
                                             iota[:, 0:TOPK].unsqueeze(1).unsqueeze(1).broadcast_to(full), ALU.is_equal)
                last.then_inc(s["eq_want"], 1)
                dve.wait_ge(s["eq_want"], count)

            def select(tb, count):
                bs = bss[tb]
                full = [P, HEADS, TOPK, TOPK]
                dve.wait_ge(s["gready"], count)
                link(dve.tensor_reduce(gs1, bs, AX, ALU.add))
                link(dve.reciprocal(gs1, gs1))
                link(dve.tensor_tensor(sel[:, 2, :].rearrange("p (h k) -> p h k", k=TOPK), bs,
                                       gs1.unsqueeze(2).broadcast_to([P, HEADS, TOPK]), ALU.mult))
                if tb:
                    tfh = tifs[tb].rearrange("p (h o) k -> p h o k", o=2)
                    one_hot_lists(tb, count)
                    link(dve.tensor_tensor(eqs[0], eqs[0], tfh[:, :, 0, :].unsqueeze(2).broadcast_to(full), ALU.mult))
                dve.wait_ge(s["eq_done"], count)
                dve.tensor_reduce(sel[:, 0, :].rearrange("p (h k) -> p h k", k=TOPK), eqs[0], AX, ALU.add)
                dve.tensor_reduce(sel[:, 1, :].rearrange("p (h k) -> p h k", k=TOPK), eqs[1], AX, ALU.add
                                  ).then_inc(s["sel_ready"], 1)
                dve.wait_ge(s["sel_ready"], count)

            def links_of(kind, l):
                us = units(l)
                return (kind == "swa") + sum(1 + (kind == "swa" and j >= 0) + (2 if kind == "swa" else 1) for j in us)

            for name in ("max_ready", "norm_done", "bias_used"):
                dve.nop().then_inc(s[name], 1)
            dve.wait_ge(s["consts_in"], 64)
            dve.tensor_scalar(sT[:, :, :], c0, -1.0, 80.0, ALU.mult, ALU.min).then_inc(s["set_v"], 1)
            link(dve.tensor_tensor(lbt[:, :, :, 0:1], lbx[:, :, :, 0:1], lbx[:, :, :, 1:2], ALU.max))
            dve.tensor_tensor(lbx, lbx, lbt[:, :, :, 0:1].broadcast_to([P, 2, 2, 2]), ALU.subtract
                              ).then_inc(s["set_v"], 1)
            dve.wait_ge(s["set_a"], 2)
            dve.tensor_tensor(lbt[:, :, :, 0:1], lbt[:, :, :, 0:1], lbt[:, :, :, 1:2], ALU.add).then_inc(s["set_v"], 1)
            link(dve.tensor_scalar(sT[:, :, :], sT[:, :, :], 1.0, None, ALU.add))
            link(dve.reciprocal(sT[:, :, :], sT[:, :, :]))
            dve.tensor_tensor(sT[:, :, :], sT[:, :, :], c0, ALU.mult).then_inc(s["silu_done"], 1)
            dve.wait_ge(s["set_a"], 3)
            dve.tensor_tensor(lbc[:, :, :, 0:1], lbx[:, :, :, 1:2], lbt[:, :, :, 1:2], ALU.subtract)
            link(dve.tensor_tensor(lbc[:, :, :, 1:2], lbx[:, :, :, 0:1], lbt[:, :, :, 1:2], ALU.subtract))
            for l in range(DEPTH):
                fb = first_block(l)
                nb = NB - fb
                dve.wait_ge(s["layer_in"], 144 * (l + 1))
                dve.wait_ge(s["slot_free"], t["tiles"] + MOD_TILES)
                link(dve.tensor_tensor(modp[:, :, :], bank[0][:, 0:64].rearrange("p (n s) -> p n s", s=2), bT, ALU.add))
                for n in range(2):
                    link(dve.tensor_scalar(modA[:, n, :, :], modp[:, n * 16 + 8:n * 16 + 16, :], 1.0, None, ALU.add))
                    link(dve.tensor_tensor(modA[:, n, :, :], modA[:, n, :, :],
                                           nw[:, n, :].unsqueeze(2).broadcast_to([P, KD, 2]), ALU.mult))
                for h in range(2):
                    last = dve.tensor_tensor(grow[0:2, h * 1024:h * 1024 + 1024], PS[1 + h][0:2, :],
                                             brow[0:2, h * 1024:h * 1024 + 1024], ALU.add)
                last.then_inc(s["mod_done"], 1)
                end(f"mod{l}")
                norm(list(range(NB)), xin, 0, xn, hT)
                end(f"norm{l}")
                project(range(0, 5))
                t["tiles"] += MOD_TILES + IN_TILES + OUT_TILES
                end(f"projA{l}")

                dve.memset(Bx[:, :, 0:1], 0.0)
                for i in range(2):
                    dve.memset(Qt[i], 0.0)
                    last = dve.memset(Kt[i], 0.0)
                link(last)
                per = 2 * (11 if l else 8) + 4
                with link.loop(2, per) as pr:
                    for dr in range(2):
                        def n_(per_dir, k):
                            return pr * (2 * per_dir) + (4 * l + dr) * per_dir + k

                        if dr == 0:
                            link(dve.tensor_copy(q_s, arena[:, bass.ds(pr * TOK + 12288, TOK)]))
                            dve.tensor_scalar(t_s, q_s, -1.0, 80.0, ALU.mult, ALU.min).then_inc(s["hg_qarg"], 1)
                            dve.wait_ge(s["hg_qexp"], pr + (2 * l + 1))
                            link(dve.tensor_scalar(t_s, t_s, 1.0, None, ALU.add))
                            link(dve.reciprocal(t_s, t_s))
                            link(dve.tensor_tensor(q_s, q_s, t_s, ALU.mult))
                        dve.tensor_copy(lbst[:, dr, :], small[:, bass.ds(pr * 2 + (92 + 4 * dr), 2)])
                        link(dve.tensor_copy(z_s, arena[:, bass.ds(pr * TOK + (12288 + (2 + 2 * dr) * TOK), TOK)]))
                        dve.scalar_tensor_tensor(out=t_s, in0=z_s, scalar=-1.0, in1=z_s, op0=ALU.mult, op1=ALU.min
                                                 ).then_inc(s["hg_absz"], 1)
                        dve.wait_ge(s["hg_lsig"], n_(1, 1))
                        link(dve.scalar_tensor_tensor(out=lf_s, in0=z_s, scalar=0.0, in1=t_s, op0=ALU.min,
                                                      op1=ALU.subtract))
                        dve.tensor_tensor(k_s, lf_s, z_s, ALU.subtract).then_inc(s["hg_karg"], 1)
                        if l:
                            lb, lm = lbst[:, dr, 0:1], lbst[:, dr, 1:2]
                            link(dve.tensor_scalar(lf_s, lf_s, lm, None, ALU.add))
                            link(dve.tensor_scalar(z_s, lf_s, lb, None, ALU.subtract))
                            dve.scalar_tensor_tensor(out=t_s, in0=z_s, scalar=-1.0, in1=z_s, op0=ALU.mult,
                                                     op1=ALU.min).then_inc(s["hg_mix"], 1)
                            dve.wait_ge(s["hg_mixed"], pr * 2 + (dr + 1))
                            link(dve.scalar_tensor_tensor(out=lf_s, in0=lf_s, scalar=lb, in1=t_s, op0=ALU.max,
                                                          op1=ALU.add))
                        dve.memset(Asc, 0.0)
                        link(dve.memset(ones, 1.0))
                        for c in range(NB):
                            last = dve.tensor_tensor_scan(Bx[:, c, 1:P + 1], ones, lf_s[:, c * P:(c + 1) * P], 0.0,
                                                          ALU.mult, ALU.add)
                        last.then_inc(s["hg_qk"], 1)
                        dve.wait_ge(s["hg_qk"], n_(1, 1))
                        incl, excl = Bx[:, :, 1:P + 1], Bx[:, :, 0:P]

                        def diff(lv):
                            H = 1 << lv
                            if lv >= 2:
                                dve.wait_ge(s["lv_ops"], n_(LEVELS, lv - 1))
                            dl, drt = lv_halves(chunks3(Dl[lv % 2]), lv)
                            il, ir = lv_halves(incl, lv)
                            xl, xr = lv_halves(excl, lv)
                            ref = xr[:, :, :, 0:1].broadcast_to([P, NB, P // (2 * H), H])
                            dve.tensor_tensor(dl, ref, il if dr == 0 else xl, ALU.subtract)
                            dve.tensor_tensor(drt, ir if dr == 0 else xr, ref, ALU.subtract).then_inc(s["lv_diff"], 1)

                        def ops(lv):
                            dve.wait_ge(s["lv_exp"], n_(LEVELS, lv + 1))
                            if lv >= 2:
                                dve.wait_ge(s["lv_pe"], n_(LEVELS + 1, lv - 1))
                            if lv == 0:
                                dve.wait_ge(s["hg_k"], n_(1, 1))
                            qs, ks = (1, 0) if dr == 0 else (0, 1)
                            E = lv_halves(chunks3(Dl[lv % 2]), lv)
                            dve.tensor_tensor(lv_halves(chunks3(Qt[lv % 2]), lv)[qs], E[qs],
                                              lv_halves(chunks3(q_s), lv)[qs], ALU.mult)
                            dve.tensor_tensor(lv_halves(chunks3(Kt[lv % 2]), lv)[ks], E[ks],
                                              lv_halves(chunks3(k_s), lv)[ks], ALU.mult).then_inc(s["lv_ops"], 1)

                        def merge(lv):
                            dve.wait_ge(s["lv_pe"], n_(LEVELS + 1, lv + 1))
                            if lv >= 1:
                                dve.wait_ge(s["lv_used"], n_(LEVELS + 1, lv))
                            dve.memset(small[:, 159:160], 0.0)
                            for e in range(2):
                                if lv < LEVELS:
                                    dst = lv_halves(Asc[:, e], lv)[1 - dr]
                                    mk = lv_halves(masks[:, dr, lv:lv + 1, :], lv)[1 - dr].broadcast_to(
                                        [P, NB, P >> (lv + 1), 1 << lv])
                                    src = bank[2 * (lv % 3) + e][:, 0:NB * 64].rearrange(
                                        "p (c b h) -> p c b h", c=NB, h=1 << lv)
                                else:
                                    dst = Asc[:, e]
                                    mk = masks[:, dr, lv, :].unsqueeze(1).broadcast_to([P, NB, P])
                                    src = chunks3(PS[1 + e][:, 0:TOK])
                                last = dve.copy_predicated(dst, mk, src)
                            last.then_inc(s["lv_used"], 1)

                        diff(0)
                        for lv in range(LEVELS):
                            if lv + 1 < LEVELS:
                                diff(lv + 1)
                            ops(lv)
                            if lv >= 1:
                                merge(lv - 1)
                        merge(LEVELS - 1)
                        dve.wait_ge(s["lv_ops"], n_(LEVELS, LEVELS))
                        dve.tensor_tensor(chunks3(Dl[0]), Bx[:, :, P:P + 1].broadcast_to([P, NB, P]),
                                          incl if dr == 0 else excl, ALU.subtract).then_inc(s["st_diff"], 1)
                        merge(LEVELS)
                        dve.wait_ge(s["st_exp"], n_(1, 1))
                        dve.tensor_tensor(Qh, Qh, q_s, ALU.mult)
                        dve.tensor_tensor(Kh, Kh, k_s, ALU.mult).then_inc(s["st_ops"], 1)
                        dve.memset(Sh[:, 0, :], 0.0)
                        dve.wait_ge(s["st_u"], n_(1, 1))
                        u = chunks3(PS[1][:, 0:TOK])
                        dve.tensor_copy(Ub[0:64, :, :], u[0:64, :, 0:64])
                        link(dve.tensor_copy(Ub[64:128, :, :], u[64:128, :, 64:128]))
                        order = [0, 1, 2, 3, 4, 5] if dr == 0 else [1, 0, 5, 4, 3, 2]
                        for n in range(NB - 1):
                            c = order[n]
                            op = dve.scalar_tensor_tensor(out=Sh[:, n + 1, :], in0=Sh[:, n, :], scalar=Fd[:, c:c + 1],
                                                          in1=Ub[:, c, :], op0=ALU.mult, op1=ALU.add)
                            if n < NB - 2:
                                link(op)
                            else:
                                op.then_inc(s["st_hist"], 1)
                        dve.wait_ge(s["st_out"], n_(1, 1))
                        for e in range(2):
                            dst = mix[:, fb:, bass.ds(pr * P + 64 * e, 64)]
                            src = bank[4 + e][:, fb * 64:NB * 64].rearrange("p (c d) -> p c d", d=64)
                            if dr == 0:
                                last = dve.tensor_copy(dst, src)
                            else:
                                last = dve.tensor_tensor(dst, src, dst, ALU.add)
                        last.then_inc(s["st_saved"], 1)
                        dve.wait_ge(s["st_saved"], n_(1, 1))
                end(f"hg{l}")

                ho = mix[:, fb:, 0:256]
                g4 = gS[:, fb:, :].rearrange("p c (h d) -> p c h d", d=64)
                gin = hvg[:, fb:, 256:512]
                gt = gT[:, fb:, :]
                link(dve.tensor_tensor(gS[:, fb:, :], ho, ho, ALU.mult))
                link(dve.tensor_reduce(rr[:, fb:, :], g4, AX, ALU.add))
                dve.tensor_scalar(rr[:, fb:, :], rr[:, fb:, :], 1.0 / 64, EPS, ALU.mult, ALU.add).then_inc(s["ro_ms"], 1)
                dve.tensor_scalar(gt, gin, -1.0, 80.0, ALU.mult, ALU.min).then_inc(s["ro_garg"], 1)
                dve.wait_ge(s["ro_g"], l + 1)
                link(dve.tensor_scalar(gt, gt, 1.0, None, ALU.add))
                link(dve.reciprocal(gt, gt))
                link(dve.tensor_tensor(gt, gt, gin, ALU.mult))
                link(dve.tensor_tensor(gt, gt, hnw.unsqueeze(1).broadcast_to([P, nb, 256]), ALU.mult))
                dve.wait_ge(s["ro_r"], l + 1)
                for c in range(fb, NB):
                    h4 = mix[:, c, 0:256].rearrange("p (h d) -> p h d", d=64)
                    last = dve.tensor_tensor(h4, h4, rr[:, c, :].unsqueeze(2).broadcast_to([P, 4, 64]), ALU.mult)
                link(last)
                link(dve.tensor_tensor(ho, ho, gt, ALU.mult))
                end(f"readout{l}")
                project(range(5, 12))
                end(f"projB{l}")

                for j in range(4):
                    b = CB + j
                    def four(ap):
                        return ap.rearrange("p (g o i) -> p g o i", o=2, i=16)
                    def half(ap):
                        return ap.rearrange("p (h f i) -> p h f i", f=2, i=16)
                    xi = four(sqk[:, b, :])
                    x1, x2 = (xi[:, :, o, :].rearrange("p (h f) i -> p h f i", f=2) for o in range(2))
                    yo = four(rq)
                    y1, y2 = (yo[:, :, o, :].rearrange("p (h f) i -> p h f i", f=2) for o in range(2))
                    cs, sn = (tt[:, j, :].rearrange("p (f i) -> p f i", f=2).unsqueeze(1).broadcast_to([P, 8, 2, 16])
                              for tt in (cosT, sinT))
                    t1, t2 = half(rt[:, 0:256]), half(rt[:, 256:512])
                    dve.tensor_tensor(t1, x1, cs, ALU.mult)
                    link(dve.tensor_tensor(t2, x2, sn, ALU.mult))
                    if j:
                        dve.wait_ge(s["rope_T"], NB * l + b)
                    link(dve.tensor_tensor(y1, t1, t2, ALU.subtract))
                    dve.tensor_tensor(t1, x2, cs, ALU.mult)
                    link(dve.tensor_tensor(t2, x1, sn, ALU.mult))
                    dve.tensor_tensor(y2, t1, t2, ALU.add).then_inc(s["rope_ready"], 1)
                    dve.wait_ge(s["rope_ready"], 4 * l + j + 1)
                end(f"rope{l}")

                U = len(units(l))
                u0, n0 = t.get("units", 1), 4 * NAT_H * l + 1
                for kv in range(SWA_KV):
                    with link.loop(3, links_of("swa", l)) as g:
                        attention("swa", l, g + kv * 3, g * U + (u0 + kv * 3 * U), None, None)
                with link.loop(NAT_H, links_of("nat", l)) as h:
                    attention("nat", l, h, h * U + (u0 + 6 * U), None, h * 4 + n0)
                t["units"] = u0 + 12 * U
                end(f"attn{l}")
                base = t.get("mixb", 0)
                for i, b in enumerate(range(fb, NB)):
                    dve.wait_ge(s["mixT_done"], base + i + 1)
                    dve.tensor_copy(mixT[:, 4:8, b * P:(b + 1) * P], bank[1].rearrange("p (k t) -> p k t", t=P)
                                    ).then_inc(s["mixT_used"], 1)
                t["mixb"] = base + nb
                end(f"mixT{l}")
                t["gate"] = t.get("gate", 0) + 2 + nb
                dve.wait_ge(s["gate_in"], 16 * t["gate"])
                base = t.get("y", 0)
                for i, b in enumerate(range(fb, NB)):
                    for tl in range(OUT_TILES):
                        n = base + i * OUT_TILES + tl
                        st = 1 if b < CB else 0
                        cols = slice(tl * TW, (tl + 1) * TW)
                        dve.wait_ge(s["y_done"], n + 1)
                        dve.tensor_tensor(ytmp, bank[n % 4][:, 0:TW], gateb[:, st, cols], ALU.mult
                                          ).then_inc(s["y_used"], 1)
                        dve.wait_ge(s["y_used"], n + 1)
                        link(dve.tensor_tensor(xw[:, b, cols], xw[:, b, cols], ytmp, ALU.add))
                    dve.nop().then_inc(s["x_ready"], 1)
                t["y"] = base + OUT_TILES * nb
                end(f"mix{l}")

                for b0 in passes_of(l):
                    ps_ = t.get("pass", 0)
                    norm([b0, b0 + 1], xl, 1, xp, hP)
                    t["tiles"] += WQ_TILES
                    end(f"pnorm{l}{b0}")
                    end(f"pq{l}{b0}")
                    for tb in range(2):
                        dve.wait_ge(s["s_used"], 2 * ps_ + tb + 1)
                        topk(tb)
                    for tb in range(2):
                        if tb:
                            dve.wait_ge(s["selT_done"], 2 * ps_ + 1)
                        select(tb, 2 * ps_ + tb + 1)
                        dve.wait_ge(s["selT_done"], 2 * ps_ + tb + 1)
                        dve.tensor_copy(kT[:, :, tb * P:(tb + 1) * P], bank[4][:, 0:384].rearrange("p (v t) -> p v t", v=3)
                                        ).then_inc(s["selT_used"], 1)
                    end(f"topk{l}{b0}")
                    gb = ps_ * (PASS // 4)

                    def one_hots(i, first):
                        for g in range(GD):
                            for v, dst in ((0, oneR), (1, oneB)):
                                if not first:
                                    dve.wait_ge(s["one_used" if v else "rows_ready"], i * GD + (gb + g + 1 - GD))
                                at = arena[:, bass.ds(i * (4 * GD) + (KT0 + v * PASS + 4 * g), 4)]
                                last = dve.tensor_tensor(dst[g], iota[:, :].unsqueeze(1).broadcast_to([P, 4, P]),
                                                         at.unsqueeze(2).broadcast_to([P, 4, P]), ALU.is_equal)
                            last.then_inc(s["one_ready"], 1)

                    one_hots(0, True)
                    with dve.Fori(1, PASS // (4 * GD)) as i:
                        one_hots(i, False)
                    end(f"gbuild{l}{b0}")
                    cb = ps_ * PK
                    t0 = t["tiles"]

                    def u_low(i, c):
                        dve.wait_ge(s["u_hi"], i * SLOTS + (cb + c + 1))
                        dve.tensor_tensor(wS[:, 1, :], ring[:, c % SLOTS, 0:D], wS[:, 0, :].bitcast(F32), ALU.subtract
                                          ).then_inc(s["u_lo"], 1)

                    def step(i, c, first=False, last=False):
                        if not last:
                            u_low(i, c + 1)
                        dve.wait_ge(s["gelu_done"], i * SLOTS + (cb + c + 1))
                        if not (first and c < 2):
                            dve.wait_ge(s["gated"], i * SLOTS + (cb + c - 1))
                        dve.tensor_tensor(gel[2 + c % 2], gel[c % 2], arena[:, bass.ds(i * (SLOTS * PASS) + c * PASS, PASS)],
                                          ALU.mult).then_inc(s["gfull"], 1)
                        dve.wait_ge(s["g_hi"], i * SLOTS + (cb + c + 1))
                        dve.tensor_tensor(gS_[:, 2 * (c % 2) + 1, :], gel[2 + c % 2], gS_[:, 2 * (c % 2), :].bitcast(F32),
                                          ALU.subtract).then_inc(s["gated"], 1)
                        dve.wait_ge(s["v_hi"], i * SLOTS + (cb + c + 1))
                        dve.tensor_tensor(wS[:, 3, :], ring[:, c, D:2 * D], wS[:, 2, :].bitcast(F32), ALU.subtract
                                          ).then_inc(s["slot_free"], 1)

                    u_low(0, 0)
                    for c in range(SLOTS):
                        step(0, c, True)
                    with dve.Fori(1, PK // SLOTS - 1) as i:
                        for c in range(SLOTS):
                            step(i, c)
                    for c in range(SLOTS):
                        step(PK // SLOTS - 1, c, last=(c == SLOTS - 1))
                    t["tiles"] += PK
                    t["pass"] = ps_ + 1
                    end(f"gemm{l}{b0}")
                    t["gate"] += 3
                    dve.wait_ge(s["gate_in"], 16 * t["gate"])
                    for tb in range(2):
                        link(dve.tensor_tensor(yP, PS[2 + tb][:, :], gbP, ALU.mult))
                        dve.tensor_tensor(xr[:, tb, :], xr[:, tb, :], yP, ALU.add).then_inc(s["xr_ready"], 1)
                        dve.wait_ge(s["xr_ready"], 2 * ps_ + tb + 1)
                    end(f"pres{l}{b0}")
            base = t["norm"]
            dve.wait_ge(s["nrm_in"], 80)
            for i in range(4):
                c = slice(i % 2, i % 2 + 1)
                dve.wait_ge(s["sq_done"], base + i + 1)
                dve.tensor_scalar(ss[:, c], ss[:, c], 1.0 / D, EPS, ALU.mult, ALU.add).then_inc(s["var_ready"], 1)
                dve.wait_ge(s["rms_ready"], base + i + 1)
                if i >= 2:
                    dve.wait_ge(s[f"fin_out{i % 2}"], 16)
                dve.scalar_tensor_tensor(out=xp[i % 2], in0=xf[:, i, :], scalar=rs[:, c], in1=gbP,
                                         op0=ALU.mult, op1=ALU.mult).then_inc(s["fin_ready"], 1)



def shape_tables():
    ident = np.eye(P, dtype=np.float32)
    iota = np.broadcast_to(np.arange(P, dtype=np.float32), (P, P)).copy()
    a = np.arange(P)
    s_, t_ = a[:, None], a[None, :]
    masks = np.zeros((P, 2, LEVELS + 1, P), np.uint8)
    for lv in range(LEVELS):
        H = 1 << lv
        same = (s_ // (2 * H)) == (t_ // (2 * H))
        masks[:, 0, lv] = same & (s_ % (2 * H) < H) & (t_ % (2 * H) >= H)
        masks[:, 1, lv] = same & (s_ % (2 * H) >= H) & (t_ % (2 * H) < H)
    masks[:, :, LEVELS] = (s_ == t_)[:, None, :]
    pos = np.arange(SEQ)
    inv = (10000.0 ** (-np.arange(16, dtype=np.float32) / 16)).astype(np.float32)
    ang = np.concatenate([(pos // GRID_W)[:, None].astype(np.float32) * inv,
                          (pos % GRID_W)[:, None].astype(np.float32) * inv], axis=1)
    rope = np.stack([np.cos(ang), np.sin(ang)]).astype(np.float32).reshape(2, 4, P, 32).transpose(2, 0, 1, 3)
    swam = np.stack([np.where(t_ >= s_, 0.0, NEG), np.where(t_ <= s_, 0.0, NEG)], axis=1).astype(np.float32)
    col = np.arange(GRID_W)
    start = np.clip(col - NAT_COLS // 2, 0, GRID_W - NAT_COLS)
    ok = (col[None, :] >= start[:, None]) & (col[None, :] < start[:, None] + NAT_COLS)
    natm = np.tile(np.where(ok, 0.0, NEG).astype(np.float32), (2, 1))
    return {"ident": ident, "iota": iota, "masks": masks.reshape(P, -1).view(np.float32).copy(),
            "rope": rope.reshape(P, 256).copy(), "swam": swam.reshape(P, 256).copy(), "natm": natm}


def tiles_of(w, width):
    n = w.shape[1] // width
    return w.reshape(KD, P, n, width).transpose(2, 1, 0, 3)


def lay_out(a):
    L = DEPTH
    A = {"x": a["x"][0], "ctx": a["ctx"][0]}
    A["c"] = np.stack([a["c"][0].reshape(KD, P).T, a["c_ctx"].reshape(KD, P).T], axis=2)
    A["lb"] = a["hgrn_lb_logits"].reshape(2, L, 2, P).transpose(3, 0, 2, 1)
    wcat, wq, ex, bT, nw, rpb, subk, bgate = [], [], [], [], [], [], [], []
    for l in range(L):
        wm = np.split(a["w_mod"][l], 6, axis=1)
        wm = np.concatenate([wm[i] for i in (0, 1, 3, 4, 2, 5)], axis=1)
        wi = a["w_in"][l]
        wi = np.concatenate([wi[:, 0:1920], wi[:, 2688:3072], wi[:, 1920:2688]], axis=1)
        wcat.append(np.concatenate([tiles_of(w, TW).reshape(-1, P, TILE_F) for w in (wm, wi, a["w_out"][l])]))
        wq.append(a["peer_wq"][l].reshape(KD, P, WQ_TILES, 2, P).transpose(2, 1, 3, 0, 4).reshape(WQ_TILES, P, TILE_F))
        u = a["peer_u"][l].reshape(P, PK, KD, P).transpose(1, 3, 2, 0).reshape(PK, P, D)
        v = a["peer_v"][l].reshape(P, PK, D).transpose(1, 0, 2)
        ex.append(np.concatenate([u, v], axis=2))
        bm = np.split(a["b_mod"][l], 6)
        bm_ = np.concatenate([bm[i].reshape(KD, P).T for i in (0, 1, 3, 4)], axis=1)
        bT.append(np.repeat(bm_[:, :, None], 2, axis=2).reshape(P, 64))
        bgate.append(np.concatenate([bm[2], bm[5]]))
        nw.append(np.concatenate([a["norm_mix_w"][l].reshape(KD, P).T, a["norm_ffn_w"][l].reshape(KD, P).T], axis=1))
        r = a["nat_rpb"][l]
        wide = np.zeros((NAT_H, 15, 127), r.dtype)
        wide[:, :, 48:79] = r
        rpb.append(np.stack([wide[:, :, 63 - c:127 - c] for c in range(GRID_W)], axis=1).reshape(NAT_H, GRID_W, 960))
        subk.append(a["peer_subkeys"][l].reshape(16, P, P).transpose(2, 0, 1).reshape(P, 2048))
    A["wcat"], A["wq"], A["experts"], A["bT"], A["nw"] = map(np.stack, (wcat, wq, ex, bT, nw))
    A["rpb"], A["subk"], A["bgate"] = map(np.stack, (rpb, subk, bgate))
    A["sink"], A["hnw"] = a["swa_sink"], a["hgrn_norm_w"]
    A["fnw"] = a["final_norm_w"].reshape(1, D)
    A.update(shape_tables())
    return {k: np.ascontiguousarray(v) for k, v in A.items()}


def declare(nc, arrays):
    d = {k: nc.dram_tensor(f"in_{k}", v.shape, mybir.dt.from_np(v.dtype), kind="ExternalInput").ap()
         for k, v in arrays.items()}
    d["xs"] = nc.dram_tensor("xs", (TOK, D), F32).ap()
    d["gates"] = nc.dram_tensor("gates", (DEPTH, 2, 2 * D), F32).ap()
    return d


def kernel(**inputs):
    import concourse.bacc as bacc
    from concourse.bass_utils import run_bass_kernel_spmd

    arrays = lay_out({k: np.asarray(v) for k, v in inputs.items()})
    nc = bacc.Bacc("TRN2", target_bir_lowering=False, num_devices=1)
    d = declare(nc, arrays)
    out = nc.dram_tensor("out", (SEQ, D), F32, kind="ExternalOutput").ap()
    build(nc, d, out)
    r = run_bass_kernel_spmd(nc, [{f"in_{k}": v for k, v in arrays.items()}], core_ids=[0])
    return r.results[0]["out"].reshape(1, SEQ, D)
```

```python
import numpy as np
import concourse.bass as bass
from concourse import mybir
from contextlib import ExitStack, contextmanager

D = 1024
P = 128
KD = D // P
CTX, SEQ, DEPTH = 256, 512, 2
TOK = CTX + SEQ
NB = TOK // P
CB = CTX // P
GRID_W, GRID_H = 64, SEQ // 64
HD = 64
SWA_H, SWA_KV, NAT_H = 6, 2, 6
NAT_ROWS, NAT_COLS = 8, 16
HEADS, PK, NK, TOPK = 8, 128, 128, 16
TW = 256
SLOTS = 4
TILE_F = KD * TW
MOD_TILES, IN_TILES, OUT_TILES, WQ_TILES = 24, 12, 4, 8
PASS = 2 * P
LEVELS = 7
EPS = 1e-6
NEG = -1e30

F32 = mybir.dt.float32
F32R = mybir.dt.float32r
U32 = mybir.dt.uint32
U8 = mybir.dt.uint8
ALU = mybir.AluOpType
ACT = mybir.ActivationFunctionType
AX = mybir.AxisListType.X


def passes_of(layer):
    return range(0 if layer < DEPTH - 1 else CB, NB, 2)


def first_block(layer):
    return 0 if layer < DEPTH - 1 else CB


class Chain:

    def __init__(self, eng, sem):
        self.eng, self.sem, self.n, self.term = eng, sem, 0, 0

    def __call__(self, ins):
        ins.then_inc(self.sem, 1)
        self.n += 1
        self.eng.wait_ge(self.sem, self.term + self.n if not isinstance(self.term, int) else self.n + self.term)

    @contextmanager
    def loop(self, count, per):
        base, outer = self.n, self.term
        with self.eng.Fori(0, count) as i:
            self.term = i * per + outer
            yield i
            assert self.n - base == per, f"{self.n - base} links in a body of {per}"
        self.term, self.n = outer, base + count * per


def build(nc, d, out):
    with ExitStack() as ctx:
        def sb(name, shape, dt=F32):
            return ctx.enter_context(nc.sbuf_tensor(name, shape, dt))

        def sem(name):
            return ctx.enter_context(nc.semaphore(name))

        ring = sb("ring", [P, SLOTS, TILE_F])
        ident = sb("ident", [P, P])
        iota = sb("iota", [P, P])
        sT = sb("sT", [P, KD, 2])
        modp = sb("modp", [P, 4 * KD, 2])
        modA = sb("modA", [P, 2, KD, 2])
        small = sb("small", [P, 160])
        ARENA = 35264
        arena = sb("arena", [P, ARENA])
        hS = sb("hS", [P, 2, KD, PASS], F32R)
        wS = sb("wS", [P, 4, D], F32R)
        gS_ = sb("gS_", [P, 4, PASS], F32R)

        def view(start, *dims):
            size = int(np.prod(dims))
            assert start + size <= ARENA
            names = "abcde"[:len(dims)]
            spec = " ".join(names)
            flat = arena[:, start:start + size]
            if len(dims) == 1:
                return flat
            return flat.rearrange(f"p ({spec}) -> p {spec}", **dict(zip(names, dims)))

        bT = small[:, 0:64].rearrange("p (n s) -> p n s", s=2)
        nw = small[:, 64:64 + 16].rearrange("p (n k) -> p n k", n=2)
        ss = small[:, 130:136]
        rs = small[:, 136:142]
        lbx = small[:, 84:92].rearrange("p (d q l) -> p d q l", d=2, q=2)
        lbc = small[:, 92:100].rearrange("p (d q v) -> p d q v", d=2, q=2)
        lbt = small[:, 100:108].rearrange("p (d q l) -> p d q l", d=2, q=2)
        sink = small[:, 108:114]
        nm = small[:, 114:118]
        rsum = small[:, 118:122]
        esink = small[:, 146:150]
        rden = small[:, 150:154]
        lbst = small[:, 122:126].rearrange("p (d v) -> p d v", d=2)
        mxs = small[:, 126:130]
        den = small[:, 154:158]
        sinkst = small[:, 158:159]
        c0 = small[:, 130:146].rearrange("p (k s) -> p k s", s=2)

        hT = view(0, KD, TOK)
        mix = view(6144, NB, D)
        hgF = view(12288, 6, TOK)
        hvg = view(16896, NB, 512)
        W = 19968
        z_s, q_s, k_s, lf_s, t_s = (view(W + i * TOK, TOK) for i in range(5))
        Bx = view(W + 5 * TOK, NB, P + 1)
        W2 = W + 5 * TOK + NB * (P + 1)
        Dl = [view(W2 + i * TOK, TOK) for i in range(2)]
        Qt = [view(W2 + (2 + i) * TOK, TOK) for i in range(2)]
        Kt = [view(W2 + (4 + i) * TOK, TOK) for i in range(2)]
        Asc = view(W2 + 6 * TOK, 2, NB, P)
        Qh, Kh, KhT = (view(W2 + (8 + i) * TOK, TOK) for i in range(3))
        Ub = view(W2 + 11 * TOK, NB, 64)
        Sh = view(W2 + 11 * TOK + NB * 64, NB, 64)
        Fd = view(W2 + 12 * TOK, NB)
        ones = t_s[:, 0:P]
        xin = view(12288, NB, D)
        gS = view(W, NB, 256)
        gT = view(W + 1536, NB, 256)
        rr = view(W + 3072, NB, 4)
        CST = ARENA - 1344
        masks = arena[:, CST:CST + 512].bitcast(U8).rearrange("p (d l t) -> p d l t", d=2, l=LEVELS + 1)
        cosT = view(CST + 512, 4, 32)
        sinT = view(CST + 640, 4, 32)
        swam = view(CST + 768, 2, P)
        natm = view(CST + 1024, GRID_W)
        hnw = view(CST + 1088, 256)

        Q12 = 12288
        q12 = view(Q12, 12 * TOK)
        k8 = view(21504, 8 * TOK)
        v8 = view(27648, NB, 512)
        sqk = view(30720, NB, 512)
        rq = view(0, 512)
        rt = view(512, 512)
        qst = view(30720, TOK)
        Pm = [view(i * TOK, TOK) for i in range(2)]
        PT = [view((2 + i) * TOK, TOK) for i in range(2)]
        biast = [view(4 * TOK + i * 512, 512) for i in range(2)]
        mixT = hT
        gateb = view(12288, 2, D)
        xw = view(14336, NB, D)
        ytmp = view(20480, TW)
        grow = view(0, 2048)
        brow = view(2048, 2048)
        ROWS = 18432
        rows = view(ROWS, MOD_TILES * TW)
        xn = [view(6144 + i * D, D) for i in range(2)]

        G = view(0, PK, PASS)
        KT0 = 32768
        kT = view(KT0, 3, PASS)
        GD = 4
        wrows = wS.rearrange("p a b -> p (a b)")
        oneR = [wrows[:, 512 * g:512 * g + 512].rearrange("p (n c) -> p n c", c=P) for g in range(GD)]
        oneB = [wrows[:, 2048 + 512 * g:2560 + 512 * g].rearrange("p (n c) -> p n c", c=P) for g in range(GD)]
        oneA = [view(KT0 + 3 * PASS + 512 * g, 4, P) for g in range(2)]
        gel = [view(KT0 + i * PASS, PASS) for i in range(4)]
        hP = view(28672, KD, PASS)
        xp = [view(24576 + i * D, D) for i in range(2)]
        XL = 22528
        xl = view(XL, 2, D)
        xf = view(4096, 4, D)
        qP = view(0, 8, PASS)
        sc2 = [view(2048 + i * 512, 4, P) for i in range(2)]
        SUBK = 4096
        subk = view(SUBK, 16, P)
        SC = 6144
        sc = view(SC, HEADS, 4, P)
        cand = view(10240, 4, 256)
        cand2 = view(12288, 4, 256)
        eqs = [[[view(o + (2 * tb + v) * 1024, 4, TOPK, TOPK) for v in range(2)] for tb in range(2)] for o in (14336, 24576)]
        tvs = [view(20480, 16, TOPK), view(3072, 16, TOPK)]
        tifs = [view(20736, 16, TOPK), view(18432, 16, TOPK)]
        tius = [arena[:, o:o + 256].bitcast(U32).rearrange("p (a b) -> p a b", a=16) for o in (20992, 3328)]
        bss = [view(21248, HEADS, TOPK), view(18688, HEADS, TOPK)]
        pus = [arena[:, o:o + 128].bitcast(U32).rearrange("p (a b) -> p a b", a=HEADS) for o in (21376, 19072)]
        pas = [[arena[:, o:o + 128].bitcast(U32).rearrange("p (a b) -> p a b", a=HEADS)
                for o in (19712 + 256 * tb, 19840 + 256 * tb)] for tb in range(2)]
        HALF = HEADS // 2
        pafs = [view(21632, HEADS, TOPK), view(18816, HEADS, TOPK)]
        pbfs = [view(21760, HEADS, TOPK), view(18944, HEADS, TOPK)]
        sels = [view(21888, 3, P), view(19328, 3, P)]
        gsums = [view(22272 + HEADS * tb, HEADS) for tb in range(2)]
        gbP = view(0, D)
        yP = view(1024, D)
        xr = view(2048, 2, D)

        PS = [ctx.enter_context(nc.psum_tensor(f"PS{i}", [P, 1024], F32)) for i in range(4)]
        bank = [PS[i // 2][:, 512 * (i % 2):512 * (i % 2) + 512] for i in range(8)]

        s = {n: sem(n) for n in (
            "consts_in", "x_in", "x_ready", "x_stored", "xp_in", "xr_ready", "stage_end", "slot_free",
            "dve_chain", "act_chain", "layer_in", "row_taken", "modT_done", "mod_done", "gates_out", "gate_in",
            "silu_done", "sq_done", "var_ready", "rms_ready", "xn_ready", "xT_done", "hT_act", "hT_dve",
            "proj_done", "ev_act", "ev_dve", "hg_absz", "hg_lsig", "hg_mix", "hg_mixed", "hg_karg", "hg_k",
            "hg_qarg", "hg_qexp", "hg_qk", "lv_diff", "lv_exp", "lv_ops", "lv_pe", "lv_used", "st_diff",
            "st_exp", "st_ops", "st_tr", "st_kht", "st_u", "st_hist", "st_out", "st_saved", "ro_ms", "ro_r",
            "ro_garg", "ro_g", "rope_ready", "rope_T", "rope_used", "q_staged", "scores_done", "max_ready",
            "exp_done", "trans_done", "pt_ready", "pv_done", "norm_done", "bias_used", "bias_in0", "bias_in1",
            "bias_ready", "mixT_done", "mixT_used", "y_done", "y_used", "pq_done", "pq_used", "set_v", "set_a",
            "sub_in", "s_done", "s_used", "gexp", "gready", "sel_ready", "selT_done", "one_ready",
            "rows_ready", "eq_want", "eq_done", "u_hi", "u_lo", "v_hi", "h_hi", "gfull", "g_hi", "down_done",
            "one_used", "g_used", "hu_done", "gelu_done", "gated", "fin_ready", "fin_out0", "fin_out1",
            "nrm_in")}
        w_ready = [sem(f"w_ready{i}") for i in range(SLOTS)]
        block = ctx.enter_context(nc.Block())
        N_STAGED = 4

        def stage_end(eng, tally, name):
            tally["stage"] = tally.get("stage", 0) + 1
            eng.drain().then_inc(s["stage_end"], 1)
            eng.wait_ge(s["stage_end"], N_STAGED * tally["stage"])


        def staged(eng, tally):
            def end(name):
                stage_end(eng, tally, name)
            return end

        @block.sync
        def _(sp):
            tally = {"tiles": 0}

            def stream(src, count):
                base = tally["tiles"]

                def four(i, first):
                    for sl in range(SLOTS):
                        if not first:
                            sp.wait_ge(s["slot_free"], i * SLOTS + (base + sl - SLOTS + 1))
                        sp.dma_start(ring[:, sl, :], src[bass.ds(i * SLOTS + sl, 1)].rearrange("o p f -> p (o f)")
                                     ).then_inc(w_ready[sl], 16)
                if base == 0:
                    four(0, True)
                    with sp.Fori(1, count // SLOTS) as i:
                        four(i, False)
                else:
                    with sp.Fori(0, count // SLOTS) as i:
                        four(i, False)
                tally["tiles"] += count

            for l in range(DEPTH):
                stream(d["wcat"][l], MOD_TILES + IN_TILES + OUT_TILES)
                for _ in passes_of(l):
                    stream(d["wq"][l], WQ_TILES)
                    stream(d["experts"][l], PK)

        @block.gpsimd
        def _(pool):
            t = {}
            end = staged(pool, t)

            def const(dst, src):
                pool.dma_start(dst, src).then_inc(s["consts_in"], 16)

            pool.nop().then_inc(s["bias_ready"], 1)
            for dst, src in ((ident[:, :], d["ident"]), (iota[:, :], d["iota"]), (c0, d["c"]), (lbx, d["lb"])):
                const(dst, src)

            def tokens(l, b):
                if l:
                    return d["xs"][b * P:(b + 1) * P, :]
                return d["ctx"][b * P:(b + 1) * P, :] if b < CB else d["x"][(b - CB) * P:(b - CB + 1) * P, :]

            stored = 0
            for l in range(DEPTH):
                if l:
                    pool.wait_ge(s["x_stored"], 16 * stored)
                for b in range(NB):
                    pool.dma_start(xin[:, b, :], tokens(l, b)).then_inc(s["x_in"], 16)
                for dst, src in ((bT, d["bT"][l]), (nw, d["nw"][l]),
                                 (brow[0:2, :], d["bgate"][l:l + 1, :].broadcast_to([2, 2048])),
                                 (sink, d["sink"][l:l + 1, :].broadcast_to([P, SWA_H])),
                                 (arena[:, CST:CST + 512], d["masks"]), (arena[:, CST + 512:CST + 768], d["rope"]),
                                 (arena[:, CST + 768:CST + 1024], d["swam"]), (natm, d["natm"]),
                                 (hnw, d["hnw"][l:l + 1, :].broadcast_to([P, 256]))):
                    pool.dma_start(dst, src).then_inc(s["layer_in"], 16)
                pool.wait_ge(s["mod_done"], l + 1)
                pool.dma_start(d["gates"][l], grow[0:2, :]).then_inc(s["gates_out"], 16)
                pool.wait_ge(s["gates_out"], 16 * (l + 1))
                end(f"mod{l}")
                end(f"norm{l}")
                end(f"projA{l}")
                end(f"hg{l}")
                end(f"readout{l}")
                end(f"projB{l}")
                end(f"rope{l}")
                U = 4 + (CB if first_block(l) == 0 else 0)
                nbase = t.get("nat", 0)

                def bias(h, qb, wait_value):
                    pool.wait_ge(s["bias_used"], wait_value)
                    for r2 in range(2):
                        x0 = NAT_ROWS - 1 - (2 * qb + r2)
                        pool.dma_start(biast[qb % 2][64 * r2:64 * r2 + 64, :],
                                       d["rpb"][l, bass.ds(h, 1), :, x0 * 64:(x0 + 8) * 64].rearrange("o c f -> (o c) f")
                                       ).then_inc(s[f"bias_in{qb % 2}"], 16)

                def masked(h, qb):
                    pool.wait_ge(s[f"bias_in{qb % 2}"], h * 64 + (32 * (qb // 2) + 32 + 16 * nbase))
                    bt = biast[qb % 2].rearrange("p (r c) -> p r c", c=GRID_W)
                    pool.tensor_tensor(bt, bt, natm.unsqueeze(1).broadcast_to([P, 8, GRID_W]), ALU.add
                                       ).then_inc(s["bias_ready"], 1)

                ub = t.get("bu", 1)
                with pool.Fori(0, NAT_H) as h:
                    for qb in range(4):
                        bias(h, qb, h * 4 + (ub + max(qb - 1, 0)))
                        masked(h, qb)
                t["bu"] = ub + 4 * NAT_H
                t["nat"] = nbase + 4 * NAT_H
                end(f"attn{l}")
                for st in range(2):
                    pool.dma_start(gateb[:, st, :], d["gates"][l, st:st + 1, 0:D].broadcast_to([P, D])
                                   ).then_inc(s["gate_in"], 16)
                for b in range(first_block(l), NB):
                    pool.dma_start(xw[:, b, :], tokens(l, b)).then_inc(s["gate_in"], 16)
                end(f"mixT{l}")
                yb = t.get("yb", 0)
                for i, b in enumerate(range(first_block(l), NB)):
                    pool.wait_ge(s["x_ready"], yb + i + 1)
                    pool.dma_start(d["xs"][b * P:(b + 1) * P, :], xw[:, b, :]).then_inc(s["x_stored"], 16)
                    stored += 1
                t["yb"] = yb + NB - first_block(l)
                pool.wait_ge(s["x_stored"], 16 * stored)
                end(f"mix{l}")

                def load_pass(b0):
                    for i in range(2):
                        pool.dma_start(xl[:, i, :], d["xs"][(b0 + i) * P:(b0 + i + 1) * P, :]).then_inc(s["xp_in"], 16)

                load_pass(passes_of(l)[0])
                for pn, b0 in enumerate(passes_of(l)):
                    ps_ = t.get("pass", 0)
                    if pn == 0:
                        pool.dma_start(subk, d["subk"][l]).then_inc(s["sub_in"], 16)
                    pool.wait_ge(s["x_stored"], 16 * stored)
                    end(f"pnorm{l}{b0}")
                    full = [P, HALF, TOPK, TOPK]
                    for hf in range(2):
                        pool.wait_ge(s["eq_want"], 2 * ps_ + hf + 1)
                        for tb in range(2):
                            tfh = tifs[tb].rearrange("p (h o) k -> p h o k", o=2)[:, HALF * hf:HALF * (hf + 1)]
                            for v in ((0, 1) if hf == 0 else (1,)):
                                eq = eqs[hf][tb][v]
                                last = pool.tensor_tensor(eq, eq, tfh[:, :, v, :].unsqueeze(2).broadcast_to(full), ALU.mult)
                        last.then_inc(s["eq_done"], 1)
                    end(f"topk{l}{b0}")
                    gb = ps_ * (PASS // 4)

                    def gate_rows(i, first):
                        for g in range(GD):
                            pool.wait_ge(s["one_ready"], i * GD + (gb + g + 1))
                            if not first or g >= 2:
                                pool.wait_ge(s["rows_ready"], i * GD + (gb + g))
                                pool.wait_ge(s["one_used"], i * GD + (gb + g - 1))
                                pool.tensor_tensor(small[:, 159:160], small[:, 84:85], small[:, 84:85], ALU.add)
                            pool.tensor_tensor(oneA[g % 2], oneR[g].bitcast(F32),
                                               arena[:, bass.ds(i * (4 * GD) + (KT0 + 2 * PASS + 4 * g), 4)].unsqueeze(2)
                                               .broadcast_to([P, 4, P]), ALU.mult).then_inc(s["rows_ready"], 1)

                    gate_rows(0, True)
                    with pool.Fori(1, PASS // (4 * GD)) as i:
                        gate_rows(i, False)
                    end(f"gbuild{l}{b0}")
                    pool.wait_ge(s["gfull"], (ps_ + 1) * PK - SLOTS * 2)
                    t["pass"] = ps_ + 1
                    st = 1 if b0 < CB else 0
                    pool.dma_start(gbP, d["gates"][l, st:st + 1, D:2 * D].broadcast_to([P, D])
                                   ).then_inc(s["gate_in"], 16)
                    for i in range(2):
                        pool.dma_start(xr[:, i, :], d["xs"][(b0 + i) * P:(b0 + i + 1) * P, :]).then_inc(s["gate_in"], 16)
                    if b0 + 2 < NB:
                        pool.dma_start(subk, d["subk"][l]).then_inc(s["sub_in"], 16)
                        load_pass(b0 + 2)
                    end(f"gemm{l}{b0}")
                    for i in range(2):
                        pool.wait_ge(s["xr_ready"], 2 * ps_ + i + 1)
                        pool.dma_start(d["xs"][(b0 + i) * P:(b0 + i + 1) * P, :], xr[:, i, :]).then_inc(s["x_stored"], 16)
                        stored += 1
                    if b0 + 2 >= NB:
                        pool.wait_ge(s["x_stored"], 16 * stored)
                    end(f"pres{l}{b0}")
            pool.dma_start(gbP, d["fnw"].broadcast_to([P, D])).then_inc(s["nrm_in"], 16)
            for b in range(4):
                pool.dma_start(xf[:, b, :], d["xs"][(CB + b) * P:(CB + b + 1) * P, :]).then_inc(s["nrm_in"], 16)
            for b in range(4):
                pool.wait_ge(s["fin_ready"], b + 1)
                pool.dma_start(out[b * P:(b + 1) * P, :], xp[b % 2]).then_inc(s[f"fin_out{b % 2}"], 16)
            for b in range(2):
                pool.wait_ge(s[f"fin_out{b}"], 32)

        def pieces(kind, j):
            if j < 0:
                return [(0, 0, CTX)]
            lo, hi = (0, 4) if kind == "nat" else (max(0, j - 1), min(4, j + 2))
            n1 = min(2, hi - lo)
            res = [(0, 0, CTX), (CTX, CTX + lo * P, n1 * P)]
            if hi - lo > n1:
                res.append((CTX + n1 * P, CTX + (lo + n1) * P, (hi - lo - n1) * P))
            return res

        def units(l):
            return [-2, -1, 0, 1, 2, 3] if first_block(l) == 0 else [0, 1, 2, 3]

        def width(kind, j):
            return sum(n for _, _, n in pieces(kind, j))

        def key_blocks(kind, j):
            return [t0 // P + i for _, t0, n in pieces(kind, j) for i in range(n // P)]

        def items(tiles):
            res = []
            for t in tiles:
                if t < 3 or t >= 9:
                    res += [("feat", t, (m, h)) for m in range(2) for h in range(2)]
                else:
                    res += [("tok", t, b) for b in range(NB)]
            return res

        def evacuate(op, item, ps):
            kind, tl, part = item
            if kind == "tok":
                b = part
                dst = (hvg[:, b, (tl - 3) * TW:(tl - 2) * TW] if tl < 5 else
                       sqk[:, b, (tl - 5) * TW:(tl - 4) * TW] if tl < 7 else
                       v8[:, b, (tl - 7) * TW:(tl - 6) * TW])
                return op(dst, ps[:, 0:TW])
            m, h = part
            half = slice(h * 384, h * 384 + 384)
            if tl < 3:
                return op(hgF[:, 2 * tl + m, half], ps[:, 0:384])
            ft = 2 * (tl - 9) + m
            for e in range(2):
                if ft < 3:
                    base = (6 + 2 * ft + e) * TOK
                    dst = q12[0:64, base + h * 384:base + h * 384 + 384]
                else:
                    base = (2 + 2 * (ft - 3) + e) * TOK
                    dst = k8[0:64, base + h * 384:base + h * 384 + 384]
                last = op(dst, ps[64 * e:64 * e + 64, 0:384])
            return last

        def lv_halves(ap3, lv):
            H = 1 << lv
            v = ap3.rearrange("p c (b h) -> p c b h", h=2 * H)
            return v[:, :, :, 0:H], v[:, :, :, H:2 * H]

        def chunks3(ap):
            return ap.rearrange("p (c t) -> p c t", t=P)

        @block.tensor
        def _(pe):
            t = {"tiles": 0, "items": 0}
            end = staged(pe, t)

            def slot(sl):
                return ring[:, sl, :].rearrange("p (k c) -> p k c", k=KD)

            def tile_in(sl, i=0):
                pe.wait_ge(w_ready[sl], i * 16 + 16 * (t["tiles"] // SLOTS + 1))

            def project(tiles):
                its = items(tiles)
                for n, (kind, tl, part) in enumerate(its):
                    n += t["items"]
                    if n >= 4:
                        pe.wait_ge(s["ev_dve" if n % 2 else "ev_act"], (n - 4) // 2 + 1)
                    g = t["tiles"]
                    w = slot(g % SLOTS)
                    pe.wait_ge(w_ready[g % SLOTS], 16 * (g // SLOTS + 1))
                    for k in range(KD):
                        if kind == "feat":
                            m, h = part
                            mm = pe.matmul(bank[n % 4][:, 0:384], w[:, k, m * P:(m + 1) * P],
                                           hT[:, k, h * 384:h * 384 + 384], start=(k == 0), stop=(k == KD - 1))
                        else:
                            mm = pe.matmul(bank[n % 4][:, 0:TW], hT[:, k, part * P:(part + 1) * P], w[:, k, :],
                                           start=(k == 0), stop=(k == KD - 1))
                    mm.then_inc(s["proj_done"], 1)
                    if n - t["items"] + 1 == len(its) or its[n - t["items"] + 1][1] != tl:
                        pe.wait_ge(s["proj_done"], n + 1)
                        pe.nop().then_inc(s["slot_free"], 1)
                        t["tiles"] += 1
                t["items"] += len(its)

            def norm(nblk):
                base = t.get("norm", 0)
                for i in range(nblk):
                    n = base + i
                    pe.wait_ge(s["xn_ready"], n + 1)
                    if n >= 2:
                        pe.wait_ge(s["hT_act"], n - 1)
                        pe.wait_ge(s["hT_dve"], n - 1)
                    for k in range(KD):
                        mm = pe.transpose(bank[2 * (n % 2) + k // 4][:, (k % 4) * P:(k % 4 + 1) * P],
                                          t["xn"][i % 2][:, k * P:(k + 1) * P], ident[:, :])
                    mm.then_inc(s["xT_done"], 1)
                t["norm"] = base + nblk

            def attention(kind, l, head, first, last_g):
                us = units(l)
                def scores(i):
                    j = us[i]
                    if i == 0 or kind == "nat":
                        pe.wait_ge(s["rope_ready"], 4 * (l + 1))
                        pe.wait_ge(s["q_staged"], last_g)
                    if i >= 2:
                        pe.wait_ge(s["exp_done"], first + (i - 1))
                    for c, t0, n in pieces(kind, j):
                        if kind == "swa":
                            rhs = k8[0:64, (head // 3) * TOK + t0:(head // 3) * TOK + t0 + n]
                        else:
                            rhs = k8[0:64, bass.ds(head * TOK + (2 * TOK + t0), n)]
                        mm = pe.matmul(PS[i % 2][:, c:c + n], qst[0:64, (j + 2) * P:(j + 3) * P], rhs,
                                       start=True, stop=True)
                    mm.then_inc(s["scores_done"], 1)

                def trans(i):
                    pe.wait_ge(s["exp_done"], first + (i + 1))
                    if i >= 1:
                        pe.wait_ge(s["pt_ready"], first + i)
                    for c in range(width(kind, us[i]) // P):
                        mm = pe.transpose(PS[2][:, c * P:(c + 1) * P], Pm[i % 2][:, c * P:(c + 1) * P], ident[:, :])
                    mm.then_inc(s["trans_done"], 1)

                def values(i):
                    pe.wait_ge(s["pt_ready"], first + (i + 1))
                    pe.wait_ge(s["norm_done"], first + max(i - 1, 0))
                    kb = key_blocks(kind, us[i])
                    for c, b in enumerate(kb):
                        if kind == "swa":
                            rhs = v8[:, b, (head // 3) * 64:(head // 3) * 64 + 64]
                        else:
                            rhs = v8[:, b, bass.ds(head * 64 + 128, 64)]
                        mm = pe.matmul(bank[6 + i % 2][:, 0:64], PT[i % 2][:, c * P:(c + 1) * P], rhs,
                                       start=(c == 0), stop=(c == len(kb) - 1))
                    mm.then_inc(s["pv_done"], 1)

                n = len(us)
                scores(0)
                for i in range(n + 1):
                    if i + 1 < n:
                        scores(i + 1)
                    if i < n:
                        trans(i)
                    if i >= 1:
                        values(i - 1)

            for name in ("scores_done", "trans_done", "pv_done"):
                pe.nop().then_inc(s[name], 1)
            pe.wait_ge(s["consts_in"], 64)
            for l in range(DEPTH):
                fb = first_block(l)
                mb = MOD_TILES // SLOTS * l
                pe.wait_ge(s["silu_done"], 1)
                with pe.Fori(0, MOD_TILES // 8) as i:
                    for r in range(2):
                        pe.wait_ge(s["row_taken"], i * 2 + (mb + r + 1))
                        for sl in range(SLOTS):
                            pe.wait_ge(w_ready[sl], i * 32 + 16 * (t["tiles"] // SLOTS + r + 1))
                            for k in range(KD):
                                mm = pe.matmul(PS[r][0:2, sl * TW:(sl + 1) * TW], sT[:, k, :],
                                               slot(sl)[:, k, :], start=(k == 0), stop=(k == KD - 1))
                            mm.then_inc(s["slot_free"], 1)
                t["tiles"] += MOD_TILES
                pe.wait_ge(s["row_taken"], mb + 8)
                for n in range(32):
                    mm = pe.transpose(bank[4][:, 2 * n:2 * n + 2], rows[0:2, n * P:(n + 1) * P], ident[0:2, 0:2])
                mm.then_inc(s["modT_done"], 1)
                end(f"mod{l}")
                t["xn"] = xn
                norm(NB)
                end(f"norm{l}")
                project(range(0, 5))
                end(f"projA{l}")

                with pe.Fori(0, 2) as pr:
                    for dr in range(2):
                        def n_(per_dir, k):
                            return pr * (2 * per_dir) + (4 * l + dr) * per_dir + k

                        pe.wait_ge(s["hg_qk"], n_(1, 1))
                        pe.wait_ge(s["hg_k"], n_(1, 1))
                        for e in range(2):
                            for c in range(NB):
                                mm = pe.matmul(PS[1 + e][:, c * P:(c + 1) * P], k_s[64 * e:64 * e + 64, c * P:(c + 1) * P],
                                               q_s[64 * e:64 * e + 64, c * P:(c + 1) * P], start=True, stop=True)
                        mm.then_inc(s["lv_pe"], 1)
                        for lv in range(LEVELS):
                            pe.wait_ge(s["lv_ops"], n_(LEVELS, lv + 1))
                            if lv >= 1:
                                pe.wait_ge(s["lv_used"], n_(LEVELS + 1, max(1, lv - 1)))
                            for c in range(NB):
                                mm = pe.matmul(PS[lv % 3][:, c * P:(c + 1) * P], Kt[lv % 2][:, c * P:(c + 1) * P],
                                               Qt[lv % 2][:, c * P:(c + 1) * P], start=True, stop=True)
                            mm.then_inc(s["lv_pe"], 1)
                        pe.wait_ge(s["st_ops"], n_(1, 1))
                        pe.wait_ge(s["lv_used"], n_(LEVELS + 1, LEVELS + 1))
                        for c in range(NB):
                            mm = pe.transpose(PS[0][:, c * P:(c + 1) * P], Kh[:, c * P:(c + 1) * P], ident[:, :])
                        mm.then_inc(s["st_tr"], 1)
                        pe.wait_ge(s["st_kht"], n_(1, 1))
                        for c in range(NB):
                            mm = pe.matmul(PS[1][:, c * P:(c + 1) * P], KhT[:, c * P:(c + 1) * P],
                                           hvg[:, c, bass.ds(pr * P, P)], start=True, stop=True)
                        mm.then_inc(s["st_u"], 1)
                        pe.wait_ge(s["st_hist"], n_(1, 1))
                        order = [0, 1, 2, 3, 4, 5] if dr == 0 else [1, 0, 5, 4, 3, 2]
                        for e in range(2):
                            for n, c in enumerate(order):
                                if c < fb:
                                    continue
                                pe.matmul(bank[4 + e][:, c * 64:c * 64 + 64], Asc[:, e, c, :],
                                          hvg[:, c, bass.ds(pr * P + 64 * e, 64)], start=True, stop=False)
                                mm = pe.matmul(bank[4 + e][:, c * 64:c * 64 + 64],
                                               Qh[64 * e:64 * e + 64, c * P:(c + 1) * P],
                                               Sh[64 * e:64 * e + 64, n, :], start=False, stop=True)
                        mm.then_inc(s["st_out"], 1)
                        pe.wait_ge(s["st_saved"], n_(1, 1))
                end(f"hg{l}")
                end(f"readout{l}")
                project(range(5, 12))
                end(f"projB{l}")
                base = t.get("rope", 0)
                for b in range(NB):
                    n = base + b
                    if b >= CB:
                        pe.wait_ge(s["rope_ready"], 4 * l + b - CB + 1)
                    if n >= 1:
                        pe.wait_ge(s["rope_used"], n)
                    src = sqk[:, b, :] if b < CB else rq
                    for m in range(4):
                        mm = pe.transpose(bank[0][:, m * P:(m + 1) * P], src[:, m * P:(m + 1) * P], ident[:, :])
                    mm.then_inc(s["rope_T"], 1)
                t["rope"] = base + NB
                end(f"rope{l}")
                U = len(units(l))
                u0, h0 = t.get("units", 1), t.get("heads", 0)
                for kv in range(SWA_KV):
                    with pe.Fori(0, 3) as g:
                        attention("swa", l, kv * 3, g * U + (u0 + kv * 3 * U), g + (h0 + kv * 3 + 1))
                with pe.Fori(0, NAT_H) as h:
                    attention("nat", l, h, h * U + (u0 + 6 * U), h + (h0 + 7))
                t["units"], t["heads"] = u0 + 12 * U, h0 + 13
                end(f"attn{l}")
                base = t.get("mixb", 0)
                for i, b in enumerate(range(fb, NB)):
                    n = base + i
                    if n >= 1:
                        pe.wait_ge(s["mixT_used"], 2 * n)
                    for k in range(KD):
                        mm = pe.transpose(bank[k // 4][:, (k % 4) * P:(k % 4 + 1) * P],
                                          mix[:, b, k * P:(k + 1) * P], ident[:, :])
                    mm.then_inc(s["mixT_done"], 1)
                t["mixb"] = base + NB - fb
                end(f"mixT{l}")
                base = t.get("y", 0)
                for sl in range(SLOTS):
                    tile_in(sl)
                for i, b in enumerate(range(fb, NB)):
                    for tl in range(OUT_TILES):
                        n = base + i * OUT_TILES + tl
                        if n >= 4:
                            pe.wait_ge(s["y_used"], n - 3)
                        for k in range(KD):
                            mm = pe.matmul(bank[n % 4][:, 0:TW], mixT[:, k, b * P:(b + 1) * P],
                                           slot(tl)[:, k, :], start=(k == 0), stop=(k == KD - 1))
                        mm.then_inc(s["y_done"], 1)
                pe.wait_ge(s["y_done"], n + 1)
                pe.nop().then_inc(s["slot_free"], 4)
                t["tiles"] += 4
                t["y"] = base + OUT_TILES * (NB - fb)
                end(f"mix{l}")

                for b0 in passes_of(l):
                    t["xn"] = xp
                    norm(2)
                    end(f"pnorm{l}{b0}")
                    ps_ = t.get("pass", 0)
                    qb = 16 * ps_
                    pe.wait_ge(s["sub_in"], 16 * (ps_ + 1))
                    with pe.Fori(0, WQ_TILES // SLOTS) as i:
                        def scores_of(h):
                            pe.wait_ge(s["pq_used"], i * 8 + (qb + 2 * h + 2))
                            if h >= 2:
                                pe.wait_ge(s["s_used"], i * 4 + (8 * ps_ + h - 1))
                            for tb in range(2):
                                for o in range(2):
                                    mm = pe.matmul(bank[4 + h % 2][:, (2 * tb + o) * P:(2 * tb + o + 1) * P],
                                                   qP[:, 2 * h + o, tb * P:(tb + 1) * P],
                                                   arena[:, bass.ds(i * (8 * P) + (SUBK + (2 * h + o) * P), P)],
                                                   start=True, stop=True)
                            mm.then_inc(s["s_done"], 1)

                        for sl in range(SLOTS):
                            tile_in(sl, i)
                            w = ring[:, sl, :].rearrange("p (m k c) -> p m k c", m=2, k=KD)
                            for m in range(2):
                                n = sl * 2 + m
                                if n >= 4:
                                    pe.wait_ge(s["pq_used"], i * 8 + (qb + n - 3))
                                for k in range(KD):
                                    mm = pe.matmul(bank[n % 4][:, 0:PASS], w[:, m, k, :], hP[:, k, :],
                                                   start=(k == 0), stop=(k == KD - 1))
                                mm.then_inc(s["pq_done"], 1)
                                if sl and m == 0:
                                    scores_of(sl - 1)
                            pe.wait_ge(s["pq_done"], i * 8 + (qb + sl * 2 + 2))
                            pe.nop().then_inc(s["slot_free"], 1)
                        scores_of(SLOTS - 1)
                        pe.wait_ge(s["pq_used"], i * 8 + (qb + 8))
                        pe.wait_ge(s["s_done"], i * 4 + (8 * ps_ + 4))
                        pe.wait_ge(s["s_used"], i * 4 + (8 * ps_ + 4))
                    t["tiles"] += WQ_TILES
                    for tb in range(2):
                        pe.wait_ge(s["sel_ready"], 2 * ps_ + tb + 1)
                        for v in range(3):
                            mm = pe.transpose(bank[4 + tb][:, v * P:(v + 1) * P], sels[tb][:, v, :], ident[:, :])
                        mm.then_inc(s["selT_done"], 1)
                    end(f"topk{l}{b0}")
                    gb = ps_ * (PASS // 4)

                    def gates_of(i, first):
                        for g in range(GD):
                            pe.wait_ge(s["rows_ready"], i * GD + (gb + g + 1))
                            if not first:
                                pe.wait_ge(s["g_used"], i * GD + (gb + g + 1 - GD))
                            for q in range(4):
                                mm = pe.matmul(bank[4 + g][:, q * P:(q + 1) * P], oneA[g % 2][:, q, :],
                                               oneB[g][:, q, :].bitcast(F32), start=True, stop=True)
                            mm.then_inc(s["one_used"], 1)

                    gates_of(0, True)
                    with pe.Fori(1, PASS // (4 * GD)) as i:
                        gates_of(i, False)
                    end(f"gbuild{l}{b0}")

                    cbase = ps_ * PK

                    def up(i, c, sl):
                        pe.wait_ge(s["u_hi"], i * SLOTS + (cbase + c + 1))
                        if not (isinstance(i, int) and i == 0 and c < 2):
                            pe.wait_ge(s["gelu_done"], i * SLOTS + (cbase + c - 1))
                        for part, (w, h) in enumerate(((0, 0), (0, 1), (1, 0))):
                            if w:
                                pe.wait_ge(s["u_lo"], i * SLOTS + (cbase + c + 1))
                            u = wS[:, w, :].rearrange("p (k e) -> p k e", k=KD)
                            for k in range(KD):
                                mm = pe.matmul(bank[c % 2][:, 0:PASS], u[:, k, :], hS[:, h, k, :],
                                               start=(part == 0 and k == 0), stop=(part == 2 and k == KD - 1))
                        mm.then_inc(s["hu_done"], 1)

                    def down(i, c, sl, start=False, stop=False):
                        pe.wait_ge(s["gated"], i * SLOTS + (cbase + c + 1))
                        pe.wait_ge(s["v_hi"], i * SLOTS + (cbase + c + 1))
                        for part, (g, v) in enumerate(((0, 0), (1, 0), (0, 1))):
                            if v:
                                pe.wait_ge(s["slot_free"], i * SLOTS + (t["tiles"] + c + 1))
                            for tb in range(2):
                                for h in range(2):
                                    mm = pe.matmul(bank[4 + 2 * tb + h],
                                                   gS_[:, 2 * (c % 2) + g, tb * P:(tb + 1) * P],
                                                   wS[:, 2 + v, 512 * h:512 * h + 512],
                                                   start=(start and part == 0), stop=(stop and part == 2))
                        mm.then_inc(s["down_done"], 1)

                    def group(i, first, last):
                        for sl in range(SLOTS):
                            if sl < SLOTS - 1:
                                up(i, sl + 1, sl + 1)
                            elif not last:
                                up(i + 1, 0, 0)
                            down(i, sl, sl, first and sl == 0, last and sl == SLOTS - 1)

                    up(0, 0, 0)
                    group(0, True, False)
                    with pe.Fori(1, PK // SLOTS - 1) as i:
                        group(i, False, False)
                    group(PK // SLOTS - 1, False, True)
                    t["tiles"] += PK
                    t["pass"] = ps_ + 1
                    end(f"gemm{l}{b0}")
                    end(f"pres{l}{b0}")

        @block.scalar
        def _(act):
            t = {"items": 0, "tiles": 0}
            end = staged(act, t)
            link = Chain(act, s["act_chain"])

            def norm(blocks, src, nidx, bufs, dst):
                base = t.get("norm", 0)
                n = len(blocks)
                for i in range(n):
                    if i >= 2:
                        act.wait_ge(s["sq_done"], base + i - 1)
                    act.activation(bufs[i % 2], src[:, i, :], ACT.Square, accum_out=ss[:, i:i + 1]
                                   ).then_inc(s["sq_done"], 1)
                t["var"] = t.get("var", 0) + 1
                act.wait_ge(s["var_ready"], t["var"])
                link(act.activation(rs[:, 0:n], ss[:, 0:n], ACT.Ln))
                act.activation(rs[:, 0:n], rs[:, 0:n], ACT.Exp, scale=-0.5).then_inc(s["rms_ready"], 1)
                for i, b in enumerate(blocks):
                    st = 1 if b < CB else 0
                    act.wait_ge(s["xT_done"], base + i + 1)
                    for k in range(4):
                        last = act.activation(dst[:, k, i * P:(i + 1) * P], bank[2 * ((base + i) % 2)][:, k * P:(k + 1) * P], ACT.Identity,
                                              scale=modA[:, nidx, k, st:st + 1], bias=modp[:, nidx * 16 + k, st:st + 1])
                    last.then_inc(s["hT_act"], 1)
                t["norm"] = base + len(blocks)
                if dst is hP:
                    act.wait_ge(s["hT_act"], t["norm"])
                    act.wait_ge(s["hT_dve"], t["norm"])
                    act.activation(hS[:, 0], hP, ACT.Copy).then_inc(s["h_hi"], 1)

            def project(tiles):
                its = items(tiles)
                for n, it in enumerate(its):
                    n += t["items"]
                    if n % 2 == 0:
                        act.wait_ge(s["proj_done"], n + 1)
                        evacuate(lambda dd, ss_: act.activation(dd, ss_, ACT.Copy), it, bank[n % 4]
                                 ).then_inc(s["ev_act"], 1)
                t["items"] += len(its)

            def attention(kind, l, head, first):
                us = units(l)

                def exps(i):
                    w = width(kind, us[i])
                    act.wait_ge(s["max_ready"], first + (i + 1))
                    act.wait_ge(s["norm_done"], first + max(i - 3, 0))
                    if i >= 2:
                        act.wait_ge(s["trans_done"], first + (i - 1))
                    if kind == "swa":
                        act.activation(esink[:, i % 4:i % 4 + 1], sinkst, ACT.Exp, bias=nm[:, i % 4:i % 4 + 1])
                    act.activation(Pm[i % 2][:, 0:w], PS[i % 2][:, 0:w], ACT.Exp, bias=nm[:, i % 4:i % 4 + 1],
                                   accum_out=rsum[:, i % 4:i % 4 + 1]).then_inc(s["exp_done"], 1)

                def evac(i):
                    w = width(kind, us[i])
                    act.wait_ge(s["trans_done"], first + (i + 1))
                    act.wait_ge(s["pv_done"], first + max(i - 1, 0))
                    act.activation(PT[i % 2][:, 0:w], PS[2][:, 0:w], ACT.Copy).then_inc(s["pt_ready"], 1)

                exps(0)
                for i in range(len(us)):
                    evac(i)
                    if i + 1 < len(us):
                        exps(i + 1)

            for name in ("exp_done", "pt_ready"):
                act.nop().then_inc(s[name], 1)
            act.wait_ge(s["set_v"], 2)
            act.activation(sT[:, :, :], sT[:, :, :], ACT.Exp).then_inc(s["set_a"], 1)
            act.activation(lbt, lbx, ACT.Exp).then_inc(s["set_a"], 1)
            act.wait_ge(s["set_v"], 3)
            act.activation(lbt[:, :, :, 1:2], lbt[:, :, :, 0:1], ACT.Ln).then_inc(s["set_a"], 1)
            for l in range(DEPTH):
                fb = first_block(l)
                end(f"mod{l}")
                act.wait_ge(s["x_in"], 16 * NB * (l + 1))
                norm(list(range(NB)), xin, 0, xn, hT)
                end(f"norm{l}")
                project(range(0, 5))
                end(f"projA{l}")
                with link.loop(2, 4 if l else 2) as pr:
                    for dr in range(2):
                        def n_(per_dir, k):
                            return pr * (2 * per_dir) + (4 * l + dr) * per_dir + k

                        if dr == 0:
                            act.wait_ge(s["hg_qarg"], pr + (2 * l + 1))
                            act.activation(Qh, Qh, ACT.Exp).then_inc(s["hg_qexp"], 1)
                        act.wait_ge(s["hg_absz"], n_(1, 1))
                        link(act.activation(t_s, t_s, ACT.Exp))
                        act.activation(t_s, t_s, ACT.Ln, bias=1.0).then_inc(s["hg_lsig"], 1)
                        act.wait_ge(s["hg_karg"], n_(1, 1))
                        act.activation(k_s, k_s, ACT.Exp, bias=lbst[:, dr, 1:2] if l else 0.0).then_inc(s["hg_k"], 1)
                        if l:
                            act.wait_ge(s["hg_mix"], pr * 2 + (dr + 1))
                            link(act.activation(t_s, t_s, ACT.Exp))
                            act.activation(t_s, t_s, ACT.Ln, bias=1.0).then_inc(s["hg_mixed"], 1)
                        for lv in range(LEVELS):
                            act.wait_ge(s["lv_diff"], n_(LEVELS, lv + 1))
                            act.activation(Dl[lv % 2], Dl[lv % 2], ACT.Exp).then_inc(s["lv_exp"], 1)
                        act.wait_ge(s["st_diff"], n_(1, 1))
                        incl, excl = Bx[:, :, 1:P + 1], Bx[:, :, 0:P]
                        act.activation(chunks3(Qh if dr == 0 else Kh), incl if dr == 0 else excl, ACT.Exp)
                        act.activation(Kh if dr == 0 else Qh, Dl[0], ACT.Exp)
                        act.activation(Fd, Bx[:, :, P:P + 1].rearrange("p c o -> p (c o)"), ACT.Exp
                                       ).then_inc(s["st_exp"], 1)
                        act.wait_ge(s["st_tr"], n_(1, 1))
                        act.activation(KhT, PS[0][:, 0:TOK], ACT.Copy).then_inc(s["st_kht"], 1)
                end(f"hg{l}")
                act.wait_ge(s["ro_ms"], l + 1)
                link(act.activation(rr[:, fb:, :], rr[:, fb:, :], ACT.Ln))
                act.activation(rr[:, fb:, :], rr[:, fb:, :], ACT.Exp, scale=-0.5).then_inc(s["ro_r"], 1)
                act.wait_ge(s["ro_garg"], l + 1)
                act.activation(gT[:, fb:, :], gT[:, fb:, :], ACT.Exp).then_inc(s["ro_g"], 1)
                end(f"readout{l}")
                project(range(5, 12))
                end(f"projB{l}")
                base = t.get("rope", 0)
                q12v = q12.rearrange("p (h t) -> p h t", t=TOK)
                k8v = k8.rearrange("p (h t) -> p h t", t=TOK)
                ps4 = bank[0].rearrange("p (m t) -> p m t", t=P)
                for b in range(NB):
                    act.wait_ge(s["rope_T"], base + b + 1)
                    ts = slice(b * P, (b + 1) * P)
                    for e in range(2):
                        act.activation(q12v[0:64, e:6:2, ts], ps4[64 * e:64 * e + 64, 0:3, :], ACT.Copy)
                        last = act.activation(k8v[0:64, e, ts], ps4[64 * e:64 * e + 64, 3, :], ACT.Copy)
                    last.then_inc(s["rope_used"], 1)
                t["rope"] = base + NB
                end(f"rope{l}")
                U = len(units(l))
                u0 = t.get("units", 1)
                for kv in range(SWA_KV):
                    with act.Fori(0, 3) as g:
                        attention("swa", l, g + kv * 3, g * U + (u0 + kv * 3 * U))
                with act.Fori(0, NAT_H) as h:
                    attention("nat", l, h, h * U + (u0 + 6 * U))
                t["units"] = u0 + 12 * U
                end(f"attn{l}")
                base = t.get("mixb", 0)
                for i, b in enumerate(range(fb, NB)):
                    act.wait_ge(s["mixT_done"], base + i + 1)
                    act.activation(mixT[:, 0:4, b * P:(b + 1) * P], bank[0].rearrange("p (k t) -> p k t", t=P),
                                   ACT.Copy).then_inc(s["mixT_used"], 1)
                t["mixb"] = base + NB - fb
                end(f"mixT{l}")
                t["tiles"] += MOD_TILES + IN_TILES + OUT_TILES
                end(f"mix{l}")
                for b0 in passes_of(l):
                    ps_ = t.get("pass", 0)
                    act.wait_ge(s["xp_in"], 32 * (ps_ + 1))
                    norm([b0, b0 + 1], xl, 1, xp, hP)
                    end(f"pnorm{l}{b0}")
                    with act.Fori(0, 2) as i:
                        def take_scores(h):
                            act.wait_ge(s["s_done"], i * 4 + (8 * ps_ + h + 1))
                            act.activation(arena[:, bass.ds(i * 2048 + (SC + 512 * h), 512)], bank[4 + h % 2], ACT.Copy
                                           ).then_inc(s["s_used"], 1)

                        for n in range(8):
                            act.wait_ge(s["pq_done"], i * 8 + (16 * ps_ + n + 1))
                            act.activation(qP[:, n, :], bank[n % 4][:, 0:PASS], ACT.Copy).then_inc(s["pq_used"], 1)
                            if n >= 2 and n % 2 == 0:
                                take_scores(n // 2 - 1)
                        take_scores(3)
                    t["tiles"] += WQ_TILES
                    for tb in range(2):
                        act.wait_ge(s["gexp"], 2 * ps_ + tb + 1)
                        act.activation(bss[tb], bss[tb], ACT.Exp).then_inc(s["gready"], 1)
                    end(f"topk{l}{b0}")
                    gb = ps_ * (PASS // 4)
                    with act.Fori(0, PASS // (4 * GD)) as i:
                        for g in range(GD):
                            act.wait_ge(s["one_used"], i * GD + (gb + g + 1))
                            act.activation(G[:, :, bass.ds(i * (4 * GD) + 4 * g, 4)],
                                           bank[4 + g].rearrange("p (t j) -> p j t", j=P), ACT.Copy
                                           ).then_inc(s["g_used"], 1)
                    end(f"gbuild{l}{b0}")
                    cb = ps_ * PK

                    t0 = t["tiles"]

                    def u_high(i, c, first=False):
                        sl = c % SLOTS
                        act.wait_ge(w_ready[sl], (i + c // SLOTS) * 16 + 16 * (t0 // SLOTS + 1))
                        if not first:
                            act.wait_ge(s["hu_done"], i * SLOTS + (cb + c))
                        act.activation(wS[:, 0, :], ring[:, sl, 0:D], ACT.Copy).then_inc(s["u_hi"], 1)

                    def step(i, c, first=False, last=False):
                        act.wait_ge(s["hu_done"], i * SLOTS + (cb + c + 1))
                        if not last:
                            u_high(i, c + 1)
                        if not (first and c < 2):
                            act.wait_ge(s["gated"], i * SLOTS + (cb + c - 1))
                        act.activation(gel[c % 2], bank[c % 2][:, 0:PASS], ACT.Gelu).then_inc(s["gelu_done"], 1)
                        act.wait_ge(s["gfull"], i * SLOTS + (cb + c + 1))
                        act.activation(gS_[:, 2 * (c % 2), :], gel[2 + c % 2], ACT.Copy).then_inc(s["g_hi"], 1)
                        if not (first and c == 0):
                            act.wait_ge(s["down_done"], i * SLOTS + (cb + c))
                        act.activation(wS[:, 2, :], ring[:, c, D:2 * D], ACT.Copy).then_inc(s["v_hi"], 1)

                    u_high(0, 0, True)
                    for c in range(SLOTS):
                        step(0, c, True)
                    with act.Fori(1, PK // SLOTS - 1) as i:
                        for c in range(SLOTS):
                            step(i, c)
                    for c in range(SLOTS):
                        step(PK // SLOTS - 1, c, last=(c == SLOTS - 1))
                    t["tiles"] += PK
                    t["pass"] = ps_ + 1
                    end(f"gemm{l}{b0}")
                    end(f"pres{l}{b0}")
            base = t["norm"]
            act.wait_ge(s["nrm_in"], 80)
            for i in range(4):
                if i >= 2:
                    act.wait_ge(s["sq_done"], base + i - 1)
                act.activation(xp[i % 2], xf[:, i, :], ACT.Square, accum_out=ss[:, i:i + 1]
                               ).then_inc(s["sq_done"], 1)
            act.wait_ge(s["var_ready"], t["var"] + 1)
            link(act.activation(rs[:, 0:4], ss[:, 0:4], ACT.Ln))
            act.activation(rs[:, 0:4], rs[:, 0:4], ACT.Exp, scale=-0.5).then_inc(s["rms_ready"], 1)

        @block.vector
        def _(dve):
            t = {"items": 0, "tiles": 0}
            end = staged(dve, t)
            link = Chain(dve, s["dve_chain"])

            def norm(blocks, src, nidx, bufs, dst):
                base = t.get("norm", 0)

                n = len(blocks)
                t["var"] = t.get("var", 0) + 1
                dve.wait_ge(s["sq_done"], base + n)
                dve.tensor_scalar(ss[:, 0:n], ss[:, 0:n], 1.0 / D, EPS, ALU.mult, ALU.add).then_inc(s["var_ready"], 1)
                dve.wait_ge(s["rms_ready"], t["var"])

                def pre(i):
                    if i >= 2:
                        dve.wait_ge(s["xT_done"], base + i - 1)
                    dve.tensor_scalar(bufs[i % 2], src[:, i, :], rs[:, i:i + 1], None, ALU.mult
                                      ).then_inc(s["xn_ready"], 1)

                pre(0)
                for i, b in enumerate(blocks):
                    if i + 1 < len(blocks):
                        pre(i + 1)
                    st = 1 if b < CB else 0
                    dve.wait_ge(s["xT_done"], base + i + 1)
                    for k in range(4, 8):
                        last = dve.tensor_scalar(dst[:, k, i * P:(i + 1) * P],
                                                 bank[2 * ((base + i) % 2) + 1][:, (k - 4) * P:(k - 3) * P],
                                                 modA[:, nidx, k, st:st + 1], modp[:, nidx * 16 + k, st:st + 1],
                                                 ALU.mult, ALU.add)
                    last.then_inc(s["hT_dve"], 1)
                t["norm"] = base + len(blocks)
                if dst is hP:
                    dve.wait_ge(s["hT_act"], t["norm"])
                    dve.wait_ge(s["h_hi"], t.get("pass", 0) + 1)
                    dve.tensor_tensor(hS[:, 1], hP, hS[:, 0].bitcast(F32), ALU.subtract)

            def project(tiles):
                its = items(tiles)
                for n, it in enumerate(its):
                    n += t["items"]
                    if n % 2:
                        dve.wait_ge(s["proj_done"], n + 1)
                        evacuate(dve.tensor_copy, it, bank[n % 4]).then_inc(s["ev_dve"], 1)
                t["items"] += len(its)

            def stage_queries(src):
                dve.tensor_scalar(qst[0:64, :], src, HD ** -0.5, None, ALU.mult).then_inc(s["q_staged"], 1)

            def attention(kind, l, head, first, nat_n):
                us = units(l)

                if kind == "nat":
                    after = head * TOK + 7 * TOK
                else:
                    after = head * TOK + TOK
                if kind == "swa":
                    link(dve.tensor_copy(sinkst, sink[:, bass.ds(head, 1)]))

                def pre(i):
                    j, w, c = us[i], width(kind, us[i]), slice(i % 4, i % 4 + 1)
                    S = PS[i % 2]
                    dve.wait_ge(s["scores_done"], first + (i + 1))
                    if kind == "swa" and j >= 0:
                        edges = ([(0, CTX)] if j >= 1 else []) + ([(1, CTX + (2 if j >= 1 else 1) * P)] if j < 3 else [])
                        for m, col in edges:
                            last = dve.tensor_tensor(S[:, col:col + P], S[:, col:col + P], swam[:, m, :], ALU.add)
                        link(last)
                    if kind == "nat" and j >= 0:
                        dve.wait_ge(s["bias_ready"], nat_n + (j + 1))
                        dve.tensor_tensor(S[:, CTX:CTX + 512], S[:, CTX:CTX + 512], biast[j % 2], ALU.add
                                          ).then_inc(s["bias_used"], 1)
                        dve.wait_ge(s["bias_used"], nat_n + (j + 1))
                    link(dve.tensor_reduce(mxs[:, c], S[:, 0:w], AX, ALU.max))
                    if kind == "swa":
                        op = dve.tensor_scalar(nm[:, c], mxs[:, c], sinkst, -1.0, ALU.max, ALU.mult)
                    else:
                        op = dve.tensor_scalar(nm[:, c], mxs[:, c], -1.0, None, ALU.mult)
                    op.then_inc(s["max_ready"], 1)

                def post(i):
                    j, c = us[i], slice(i % 4, i % 4 + 1)
                    dve.wait_ge(s["exp_done"], first + (i + 1))
                    if kind == "swa":
                        link(dve.tensor_tensor(den[:, c], rsum[:, c], esink[:, c], ALU.add))
                        link(dve.reciprocal(rden[:, c], den[:, c]))
                        col = head * 64 + 256
                    else:
                        link(dve.reciprocal(rden[:, c], rsum[:, c]))
                        col = head * 64 + (256 + 384)
                    dve.wait_ge(s["pv_done"], first + (i + 1))
                    dve.tensor_scalar(mix[:, j + 2, bass.ds(col, 64)], bank[6 + i % 2][:, 0:64], rden[:, c], None,
                                      ALU.mult).then_inc(s["norm_done"], 1)

                pre(0)
                for i in range(len(us) + 1):
                    if i + 1 < len(us):
                        pre(i + 1)
                    if i == len(us) - 2:
                        stage_queries(arena[0:64, bass.ds(after + Q12, TOK)])
                    if i:
                        post(i - 1)

            def head_lists(h, count):
                low = -3.0e38
                dve.wait_ge(s["s_used"], count)
                each = [(sc[:, h, 2 * tb + o, :], sc2[h % 2][:, 2 * tb + o, :], tvs[tb][:, 2 * h + o, :],
                         tius[tb][:, 2 * h + o, :]) for tb in range(2) for o in range(2)]
                for a, b, v, n in each:
                    last = dve.max(v[:, 0:8], a)
                link(last)
                for a, b, v, n in each:
                    dve.max_index(n[:, 0:8], v[:, 0:8], a)
                    last = dve.match_replace(b, v[:, 0:8], a, low)
                link(last)
                for a, b, v, n in each:
                    last = dve.max(v[:, 8:16], b)
                link(last)
                for a, b, v, n in each:
                    dve.max_index(n[:, 8:16], v[:, 8:16], b)
                full = [P, TOPK, TOPK]
                for tb in range(2):
                    last = dve.tensor_tensor(cand[:, 2 * (h % 2) + tb, :].rearrange("p (a b) -> p a b", a=TOPK),
                                             tvs[tb][:, 2 * h, :].unsqueeze(2).broadcast_to(full),
                                             tvs[tb][:, 2 * h + 1, :].unsqueeze(1).broadcast_to(full), ALU.add)
                link(last)
                each = [(cand[:, 2 * (h % 2) + tb, :], cand2[:, 2 * (h % 2) + tb, :], bss[tb][:, h, :], pus[tb][:, h, :])
                        for tb in range(2)]
                for a, b, v, n in each:
                    last = dve.max(v[:, 0:8], a)
                link(last)
                for a, b, v, n in each:
                    dve.max_index(n[:, 0:8], v[:, 0:8], a)
                    last = dve.match_replace(b, v[:, 0:8], a, low)
                link(last)
                for a, b, v, n in each:
                    last = dve.max(v[:, 8:16], b)
                link(last)
                for a, b, v, n in each:
                    last = dve.max_index(n[:, 8:16], v[:, 8:16], b)
                link(last)

            def positions(hf, count):
                hs, hps = slice(HALF * hf, HALF * (hf + 1)), slice(2 * HALF * hf, 2 * HALF * (hf + 1))
                for tb in range(2):
                    dve.tensor_copy(tifs[tb][:, hps], tius[tb][:, hps])
                    dve.tensor_single_scalar(pas[tb][0][:, hs], pus[tb][:, hs], 4, ALU.logical_shift_right)
                    last = dve.tensor_single_scalar(pas[tb][1][:, hs], pus[tb][:, hs], 15, ALU.bitwise_and)
                link(last)
                for tb in range(2):
                    dve.tensor_copy(pafs[tb][:, hs], pas[tb][0][:, hs])
                    last = dve.tensor_copy(pbfs[tb][:, hs], pas[tb][1][:, hs])
                link(last)
                full = [P, HALF, TOPK, TOPK]
                for tb in range(2):
                    for v, at in ((0, pafs[tb]), (1, pbfs[tb])):
                        last = dve.tensor_tensor(eqs[hf][tb][v], at[:, hs].unsqueeze(3).broadcast_to(full),
                                                 iota[:, 0:TOPK].unsqueeze(1).unsqueeze(1).broadcast_to(full), ALU.is_equal)
                last.then_inc(s["eq_want"], 1)
                dve.wait_ge(s["eq_want"], count)

            def by_head(tb, v):
                return sels[tb][:, v, :].rearrange("p (h k) -> p h k", k=TOPK)

            def look_up(hf, tb, v):
                return dve.tensor_reduce(by_head(tb, v)[:, HALF * hf:HALF * (hf + 1)], eqs[hf][tb][v], AX, ALU.add)

            def retrieve(ps_):
                for h in range(HEADS):
                    head_lists(h, 8 * ps_ + h + 1)
                    if h == HALF - 1:
                        positions(0, 2 * ps_ + 1)
                for tb in range(2):
                    last = dve.tensor_copy(gsums[tb], bss[tb][:, :, 0])
                link(last)
                wide = [P, HEADS, TOPK]
                for tb in range(2):
                    dve.tensor_tensor(bss[tb], bss[tb], gsums[tb].unsqueeze(2).broadcast_to(wide), ALU.subtract
                                      ).then_inc(s["gexp"], 1)
                dve.wait_ge(s["gexp"], 2 * ps_ + 2)
                positions(1, 2 * ps_ + 2)
                for tb in range(2):
                    tfh = tifs[tb].rearrange("p (h o) k -> p h o k", o=2)[:, HALF:]
                    last = dve.tensor_tensor(eqs[1][tb][0], eqs[1][tb][0],
                                             tfh[:, :, 0, :].unsqueeze(2).broadcast_to([P, HALF, TOPK, TOPK]), ALU.mult)
                link(last)
                dve.wait_ge(s["gready"], 2 * ps_ + 2)
                for tb in range(2):
                    last = dve.tensor_reduce(gsums[tb], bss[tb], AX, ALU.add)
                link(last)
                for tb in range(2):
                    last = dve.reciprocal(gsums[tb], gsums[tb])
                link(last)
                for tb in range(2):
                    dve.tensor_tensor(by_head(tb, 2), bss[tb], gsums[tb].unsqueeze(2).broadcast_to(wide), ALU.mult)
                dve.wait_ge(s["eq_done"], 2 * ps_ + 1)
                for tb in range(2):
                    look_up(1, tb, 0)
                    look_up(0, tb, 0)
                    look_up(0, tb, 1)
                dve.wait_ge(s["eq_done"], 2 * ps_ + 2)
                for tb in range(2):
                    look_up(1, tb, 1).then_inc(s["sel_ready"], 1)

            def links_of(kind, l):
                us = units(l)
                return (kind == "swa") + sum(1 + (kind == "swa" and j >= 0) + (2 if kind == "swa" else 1) for j in us)

            for name in ("max_ready", "norm_done", "bias_used"):
                dve.nop().then_inc(s[name], 1)
            dve.wait_ge(s["consts_in"], 64)
            dve.tensor_scalar(sT[:, :, :], c0, -1.0, 80.0, ALU.mult, ALU.min).then_inc(s["set_v"], 1)
            link(dve.tensor_tensor(lbt[:, :, :, 0:1], lbx[:, :, :, 0:1], lbx[:, :, :, 1:2], ALU.max))
            dve.tensor_tensor(lbx, lbx, lbt[:, :, :, 0:1].broadcast_to([P, 2, 2, 2]), ALU.subtract
                              ).then_inc(s["set_v"], 1)
            dve.wait_ge(s["set_a"], 2)
            dve.tensor_tensor(lbt[:, :, :, 0:1], lbt[:, :, :, 0:1], lbt[:, :, :, 1:2], ALU.add).then_inc(s["set_v"], 1)
            link(dve.tensor_scalar(sT[:, :, :], sT[:, :, :], 1.0, None, ALU.add))
            link(dve.reciprocal(sT[:, :, :], sT[:, :, :]))
            dve.tensor_tensor(sT[:, :, :], sT[:, :, :], c0, ALU.mult).then_inc(s["silu_done"], 1)
            dve.wait_ge(s["set_a"], 3)
            dve.tensor_tensor(lbc[:, :, :, 0:1], lbx[:, :, :, 1:2], lbt[:, :, :, 1:2], ALU.subtract)
            link(dve.tensor_tensor(lbc[:, :, :, 1:2], lbx[:, :, :, 0:1], lbt[:, :, :, 1:2], ALU.subtract))
            for _ in range(2):
                dve.nop().then_inc(s["row_taken"], 1)
            for l in range(DEPTH):
                fb = first_block(l)
                nb = NB - fb
                with dve.Fori(0, MOD_TILES // 8) as i:
                    for r in range(2):
                        dve.wait_ge(s["slot_free"], i * 8 + (t["tiles"] + 4 * r + 4))
                        dve.tensor_copy(arena[0:2, bass.ds(i * 2048 + (ROWS + 1024 * r), 1024)], PS[r][0:2, :]
                                        ).then_inc(s["row_taken"], 1)
                dve.wait_ge(s["row_taken"], MOD_TILES // SLOTS * (l + 1) + 2)
                dve.wait_ge(s["layer_in"], 144 * (l + 1))
                dve.wait_ge(s["modT_done"], l + 1)
                link(dve.tensor_tensor(modp[:, :, :], bank[4][:, 0:64].rearrange("p (n s) -> p n s", s=2), bT, ALU.add))
                for n in range(2):
                    link(dve.tensor_scalar(modA[:, n, :, :], modp[:, n * 16 + 8:n * 16 + 16, :], 1.0, None, ALU.add))
                    link(dve.tensor_tensor(modA[:, n, :, :], modA[:, n, :, :],
                                           nw[:, n, :].unsqueeze(2).broadcast_to([P, KD, 2]), ALU.mult))
                for h in range(2):
                    last = dve.tensor_tensor(grow[0:2, h * 1024:h * 1024 + 1024], rows[0:2, 4096 + h * 1024:5120 + h * 1024],
                                             brow[0:2, h * 1024:h * 1024 + 1024], ALU.add)
                last.then_inc(s["mod_done"], 1)
                end(f"mod{l}")
                norm(list(range(NB)), xin, 0, xn, hT)
                end(f"norm{l}")
                project(range(0, 5))
                t["tiles"] += MOD_TILES + IN_TILES + OUT_TILES
                end(f"projA{l}")

                dve.memset(Bx[:, :, 0:1], 0.0)
                for i in range(2):
                    dve.memset(Qt[i], 0.0)
                    last = dve.memset(Kt[i], 0.0)
                link(last)
                per = 2 * (11 if l else 8) + 4
                with link.loop(2, per) as pr:
                    for dr in range(2):
                        def n_(per_dir, k):
                            return pr * (2 * per_dir) + (4 * l + dr) * per_dir + k

                        def save(way):
                            count = pr * 2 + (4 * l + way + 1)
                            dve.wait_ge(s["st_out"], count)
                            for e in range(2):
                                dst = mix[:, fb:, bass.ds(pr * P + 64 * e, 64)]
                                src = bank[4 + e][:, fb * 64:NB * 64].rearrange("p (c d) -> p c d", d=64)
                                if way == 0:
                                    last = dve.tensor_copy(dst, src)
                                else:
                                    last = dve.tensor_tensor(dst, src, dst, ALU.add)
                            last.then_inc(s["st_saved"], 1)
                            dve.wait_ge(s["st_saved"], count)

                        if dr == 0:
                            link(dve.tensor_copy(q_s, arena[:, bass.ds(pr * TOK + 12288, TOK)]))
                            dve.tensor_scalar(Qh, q_s, -1.0, 80.0, ALU.mult, ALU.min).then_inc(s["hg_qarg"], 1)
                        dve.tensor_copy(lbst[:, dr, :], small[:, bass.ds(pr * 2 + (92 + 4 * dr), 2)])
                        link(dve.tensor_copy(z_s, arena[:, bass.ds(pr * TOK + (12288 + (2 + 2 * dr) * TOK), TOK)]))
                        dve.scalar_tensor_tensor(out=t_s, in0=z_s, scalar=-1.0, in1=z_s, op0=ALU.mult, op1=ALU.min
                                                 ).then_inc(s["hg_absz"], 1)
                        if dr == 0:
                            dve.wait_ge(s["hg_qexp"], pr + (2 * l + 1))
                            link(dve.tensor_scalar(Qh, Qh, 1.0, None, ALU.add))
                            link(dve.reciprocal(Qh, Qh))
                            link(dve.tensor_tensor(q_s, q_s, Qh, ALU.mult))
                        dve.wait_ge(s["hg_lsig"], n_(1, 1))
                        link(dve.scalar_tensor_tensor(out=lf_s, in0=z_s, scalar=0.0, in1=t_s, op0=ALU.min,
                                                      op1=ALU.subtract))
                        dve.tensor_tensor(k_s, lf_s, z_s, ALU.subtract).then_inc(s["hg_karg"], 1)
                        if l:
                            lb, lm = lbst[:, dr, 0:1], lbst[:, dr, 1:2]
                            link(dve.tensor_scalar(lf_s, lf_s, lm, None, ALU.add))
                            link(dve.tensor_scalar(z_s, lf_s, lb, None, ALU.subtract))
                            dve.scalar_tensor_tensor(out=t_s, in0=z_s, scalar=-1.0, in1=z_s, op0=ALU.mult,
                                                     op1=ALU.min).then_inc(s["hg_mix"], 1)
                            dve.wait_ge(s["hg_mixed"], pr * 2 + (dr + 1))
                            link(dve.scalar_tensor_tensor(out=lf_s, in0=lf_s, scalar=lb, in1=t_s, op0=ALU.max,
                                                          op1=ALU.add))
                        if dr:
                            save(0)
                        dve.memset(Asc, 0.0)
                        link(dve.memset(ones, 1.0))
                        for c in range(NB):
                            last = dve.tensor_tensor_scan(Bx[:, c, 1:P + 1], ones, lf_s[:, c * P:(c + 1) * P], 0.0,
                                                          ALU.mult, ALU.add)
                        last.then_inc(s["hg_qk"], 1)
                        dve.wait_ge(s["hg_qk"], n_(1, 1))
                        incl, excl = Bx[:, :, 1:P + 1], Bx[:, :, 0:P]

                        def diff(lv):
                            H = 1 << lv
                            if lv >= 2:
                                dve.wait_ge(s["lv_ops"], n_(LEVELS, lv - 1))
                            dl, drt = lv_halves(chunks3(Dl[lv % 2]), lv)
                            il, ir = lv_halves(incl, lv)
                            xl, xr = lv_halves(excl, lv)
                            ref = xr[:, :, :, 0:1].broadcast_to([P, NB, P // (2 * H), H])
                            dve.tensor_tensor(dl, ref, il if dr == 0 else xl, ALU.subtract)
                            dve.tensor_tensor(drt, ir if dr == 0 else xr, ref, ALU.subtract).then_inc(s["lv_diff"], 1)

                        def ops(lv):
                            dve.wait_ge(s["lv_exp"], n_(LEVELS, lv + 1))
                            if lv >= 2:
                                dve.wait_ge(s["lv_pe"], n_(LEVELS + 1, lv))
                            if lv == 0:
                                dve.wait_ge(s["hg_k"], n_(1, 1))
                            qs, ks = (1, 0) if dr == 0 else (0, 1)
                            E = lv_halves(chunks3(Dl[lv % 2]), lv)
                            qh = Qt[lv % 2].rearrange("p (c e b h) -> p c e b h", c=NB, e=2, h=1 << lv)
                            ql = lv_halves(chunks3(q_s), lv)[qs]
                            for e in range(2):
                                own = slice(64 * e, 64 * e + 64)
                                dve.tensor_tensor(qh[own, :, e], E[qs][own], ql[own], ALU.mult)
                            dve.tensor_tensor(lv_halves(chunks3(Kt[lv % 2]), lv)[ks], E[ks],
                                              lv_halves(chunks3(k_s), lv)[ks], ALU.mult).then_inc(s["lv_ops"], 1)

                        def merge(lv):
                            dve.wait_ge(s["lv_pe"], n_(LEVELS + 1, lv + 2))
                            if lv >= 0:
                                dve.wait_ge(s["lv_used"], n_(LEVELS + 1, lv + 1))
                            dve.memset(small[:, 159:160], 0.0)
                            for e in range(2):
                                if lv >= 0:
                                    dst = lv_halves(Asc[:, e], lv)[1 - dr]
                                    mk = lv_halves(masks[:, dr, lv:lv + 1, :], lv)[1 - dr].broadcast_to(
                                        [P, NB, P >> (lv + 1), 1 << lv])
                                    src = PS[lv % 3][:, 0:TOK].rearrange(
                                        "p (c e b h) -> p c e b h", c=NB, e=2, h=1 << lv)[:, :, e]
                                else:
                                    dst = Asc[:, e]
                                    mk = masks[:, dr, LEVELS, :].unsqueeze(1).broadcast_to([P, NB, P])
                                    src = chunks3(PS[1 + e][:, 0:TOK])
                                last = dve.copy_predicated(dst, mk, src)
                            last.then_inc(s["lv_used"], 1)

                        diff(0)
                        for lv in range(LEVELS):
                            if lv + 1 < LEVELS:
                                diff(lv + 1)
                            ops(lv)
                            merge(lv - 1)
                        dve.wait_ge(s["lv_ops"], n_(LEVELS, LEVELS))
                        dve.tensor_tensor(chunks3(Dl[0]), Bx[:, :, P:P + 1].broadcast_to([P, NB, P]),
                                          incl if dr == 0 else excl, ALU.subtract).then_inc(s["st_diff"], 1)
                        merge(LEVELS - 1)
                        dve.wait_ge(s["st_exp"], n_(1, 1))
                        dve.tensor_tensor(Qh, Qh, q_s, ALU.mult)
                        dve.tensor_tensor(Kh, Kh, k_s, ALU.mult).then_inc(s["st_ops"], 1)
                        dve.memset(Sh[:, 0, :], 0.0)
                        dve.wait_ge(s["st_u"], n_(1, 1))
                        u = chunks3(PS[1][:, 0:TOK])
                        dve.tensor_copy(Ub[0:64, :, :], u[0:64, :, 0:64])
                        link(dve.tensor_copy(Ub[64:128, :, :], u[64:128, :, 64:128]))
                        order = [0, 1, 2, 3, 4, 5] if dr == 0 else [1, 0, 5, 4, 3, 2]
                        for n in range(NB - 1):
                            c = order[n]
                            op = dve.scalar_tensor_tensor(out=Sh[:, n + 1, :], in0=Sh[:, n, :], scalar=Fd[:, c:c + 1],
                                                          in1=Ub[:, c, :], op0=ALU.mult, op1=ALU.add)
                            if n < NB - 2:
                                link(op)
                            else:
                                op.then_inc(s["st_hist"], 1)
                        if dr:
                            save(1)
                end(f"hg{l}")

                ho = mix[:, fb:, 0:256]
                g4 = gS[:, fb:, :].rearrange("p c (h d) -> p c h d", d=64)
                gin = hvg[:, fb:, 256:512]
                gt = gT[:, fb:, :]
                link(dve.tensor_tensor(gS[:, fb:, :], ho, ho, ALU.mult))
                link(dve.tensor_reduce(rr[:, fb:, :], g4, AX, ALU.add))
                dve.tensor_scalar(rr[:, fb:, :], rr[:, fb:, :], 1.0 / 64, EPS, ALU.mult, ALU.add).then_inc(s["ro_ms"], 1)
                dve.tensor_scalar(gt, gin, -1.0, 80.0, ALU.mult, ALU.min).then_inc(s["ro_garg"], 1)
                dve.wait_ge(s["ro_g"], l + 1)
                link(dve.tensor_scalar(gt, gt, 1.0, None, ALU.add))
                link(dve.reciprocal(gt, gt))
                link(dve.tensor_tensor(gt, gt, gin, ALU.mult))
                link(dve.tensor_tensor(gt, gt, hnw.unsqueeze(1).broadcast_to([P, nb, 256]), ALU.mult))
                dve.wait_ge(s["ro_r"], l + 1)
                for c in range(fb, NB):
                    h4 = mix[:, c, 0:256].rearrange("p (h d) -> p h d", d=64)
                    last = dve.tensor_tensor(h4, h4, rr[:, c, :].unsqueeze(2).broadcast_to([P, 4, 64]), ALU.mult)
                link(last)
                link(dve.tensor_tensor(ho, ho, gt, ALU.mult))
                end(f"readout{l}")
                project(range(5, 12))
                end(f"projB{l}")

                for j in range(4):
                    b = CB + j
                    def four(ap):
                        return ap.rearrange("p (g o i) -> p g o i", o=2, i=16)
                    def half(ap):
                        return ap.rearrange("p (h f i) -> p h f i", f=2, i=16)
                    xi = four(sqk[:, b, :])
                    x1, x2 = (xi[:, :, o, :].rearrange("p (h f) i -> p h f i", f=2) for o in range(2))
                    yo = four(rq)
                    y1, y2 = (yo[:, :, o, :].rearrange("p (h f) i -> p h f i", f=2) for o in range(2))
                    cs, sn = (tt[:, j, :].rearrange("p (f i) -> p f i", f=2).unsqueeze(1).broadcast_to([P, 8, 2, 16])
                              for tt in (cosT, sinT))
                    t1, t2 = half(rt[:, 0:256]), half(rt[:, 256:512])
                    dve.tensor_tensor(t1, x1, cs, ALU.mult)
                    link(dve.tensor_tensor(t2, x2, sn, ALU.mult))
                    if j:
                        dve.wait_ge(s["rope_T"], NB * l + b)
                    link(dve.tensor_tensor(y1, t1, t2, ALU.subtract))
                    dve.tensor_tensor(t1, x2, cs, ALU.mult)
                    link(dve.tensor_tensor(t2, x1, sn, ALU.mult))
                    dve.tensor_tensor(y2, t1, t2, ALU.add).then_inc(s["rope_ready"], 1)
                    dve.wait_ge(s["rope_ready"], 4 * l + j + 1)
                end(f"rope{l}")

                U = len(units(l))
                u0, n0 = t.get("units", 1), 4 * NAT_H * l + 1
                stage_queries(q12[0:64, 0:TOK])
                for kv in range(SWA_KV):
                    with link.loop(3, links_of("swa", l)) as g:
                        attention("swa", l, g + kv * 3, g * U + (u0 + kv * 3 * U), None)
                with link.loop(NAT_H, links_of("nat", l)) as h:
                    attention("nat", l, h, h * U + (u0 + 6 * U), h * 4 + n0)
                t["units"] = u0 + 12 * U
                end(f"attn{l}")
                base = t.get("mixb", 0)
                for i, b in enumerate(range(fb, NB)):
                    dve.wait_ge(s["mixT_done"], base + i + 1)
                    dve.tensor_copy(mixT[:, 4:8, b * P:(b + 1) * P], bank[1].rearrange("p (k t) -> p k t", t=P)
                                    ).then_inc(s["mixT_used"], 1)
                t["mixb"] = base + nb
                end(f"mixT{l}")
                t["gate"] = t.get("gate", 0) + 2 + nb
                dve.wait_ge(s["gate_in"], 16 * t["gate"])
                base = t.get("y", 0)
                for i, b in enumerate(range(fb, NB)):
                    for tl in range(OUT_TILES):
                        n = base + i * OUT_TILES + tl
                        st = 1 if b < CB else 0
                        cols = slice(tl * TW, (tl + 1) * TW)
                        dve.wait_ge(s["y_done"], n + 1)
                        dve.tensor_tensor(ytmp, bank[n % 4][:, 0:TW], gateb[:, st, cols], ALU.mult
                                          ).then_inc(s["y_used"], 1)
                        dve.wait_ge(s["y_used"], n + 1)
                        link(dve.tensor_tensor(xw[:, b, cols], xw[:, b, cols], ytmp, ALU.add))
                    dve.nop().then_inc(s["x_ready"], 1)
                t["y"] = base + OUT_TILES * nb
                end(f"mix{l}")

                for b0 in passes_of(l):
                    ps_ = t.get("pass", 0)
                    norm([b0, b0 + 1], xl, 1, xp, hP)
                    t["tiles"] += WQ_TILES
                    end(f"pnorm{l}{b0}")
                    retrieve(ps_)
                    for tb in range(2):
                        dve.wait_ge(s["selT_done"], 2 * ps_ + tb + 1)
                        dve.tensor_copy(kT[:, :, tb * P:(tb + 1) * P],
                                        bank[4 + tb][:, 0:384].rearrange("p (v t) -> p v t", v=3))
                    end(f"topk{l}{b0}")
                    gb = ps_ * (PASS // 4)

                    def one_hots(i, first):
                        for g in range(GD):
                            for v, dst in ((0, oneR), (1, oneB)):
                                if not first:
                                    dve.wait_ge(s["one_used" if v else "rows_ready"], i * GD + (gb + g + 1 - GD))
                                at = arena[:, bass.ds(i * (4 * GD) + (KT0 + v * PASS + 4 * g), 4)]
                                last = dve.tensor_tensor(dst[g], iota[:, :].unsqueeze(1).broadcast_to([P, 4, P]),
                                                         at.unsqueeze(2).broadcast_to([P, 4, P]), ALU.is_equal)
                            last.then_inc(s["one_ready"], 1)

                    one_hots(0, True)
                    with dve.Fori(1, PASS // (4 * GD)) as i:
                        one_hots(i, False)
                    end(f"gbuild{l}{b0}")
                    cb = ps_ * PK
                    t0 = t["tiles"]

                    def u_low(i, c):
                        dve.wait_ge(s["u_hi"], i * SLOTS + (cb + c + 1))
                        dve.tensor_tensor(wS[:, 1, :], ring[:, c % SLOTS, 0:D], wS[:, 0, :].bitcast(F32), ALU.subtract
                                          ).then_inc(s["u_lo"], 1)

                    def step(i, c, first=False, last=False):
                        if not last:
                            u_low(i, c + 1)
                        dve.wait_ge(s["gelu_done"], i * SLOTS + (cb + c + 1))
                        if not (first and c < 2):
                            dve.wait_ge(s["gated"], i * SLOTS + (cb + c - 1))
                        dve.tensor_tensor(gel[2 + c % 2], gel[c % 2], arena[:, bass.ds(i * (SLOTS * PASS) + c * PASS, PASS)],
                                          ALU.mult).then_inc(s["gfull"], 1)
                        dve.wait_ge(s["g_hi"], i * SLOTS + (cb + c + 1))
                        dve.tensor_tensor(gS_[:, 2 * (c % 2) + 1, :], gel[2 + c % 2], gS_[:, 2 * (c % 2), :].bitcast(F32),
                                          ALU.subtract).then_inc(s["gated"], 1)
                        dve.wait_ge(s["v_hi"], i * SLOTS + (cb + c + 1))
                        dve.tensor_tensor(wS[:, 3, :], ring[:, c, D:2 * D], wS[:, 2, :].bitcast(F32), ALU.subtract
                                          ).then_inc(s["slot_free"], 1)

                    u_low(0, 0)
                    for c in range(SLOTS):
                        step(0, c, True)
                    with dve.Fori(1, PK // SLOTS - 1) as i:
                        for c in range(SLOTS):
                            step(i, c)
                    for c in range(SLOTS):
                        step(PK // SLOTS - 1, c, last=(c == SLOTS - 1))
                    t["tiles"] += PK
                    t["pass"] = ps_ + 1
                    end(f"gemm{l}{b0}")
                    t["gate"] += 3
                    dve.wait_ge(s["gate_in"], 16 * t["gate"])
                    for tb in range(2):
                        link(dve.tensor_tensor(yP, PS[2 + tb][:, :], gbP, ALU.mult))
                        dve.tensor_tensor(xr[:, tb, :], xr[:, tb, :], yP, ALU.add).then_inc(s["xr_ready"], 1)
                        dve.wait_ge(s["xr_ready"], 2 * ps_ + tb + 1)
                    end(f"pres{l}{b0}")
            base = t["norm"]
            dve.wait_ge(s["nrm_in"], 80)
            dve.wait_ge(s["sq_done"], base + 4)
            dve.tensor_scalar(ss[:, 0:4], ss[:, 0:4], 1.0 / D, EPS, ALU.mult, ALU.add).then_inc(s["var_ready"], 1)
            dve.wait_ge(s["rms_ready"], t["var"] + 1)
            for i in range(4):
                if i >= 2:
                    dve.wait_ge(s[f"fin_out{i % 2}"], 16)
                dve.scalar_tensor_tensor(out=xp[i % 2], in0=xf[:, i, :], scalar=rs[:, i:i + 1], in1=gbP,
                                         op0=ALU.mult, op1=ALU.mult).then_inc(s["fin_ready"], 1)



def shape_tables():
    ident = np.eye(P, dtype=np.float32)
    iota = np.broadcast_to(np.arange(P, dtype=np.float32), (P, P)).copy()
    a = np.arange(P)
    s_, t_ = a[:, None], a[None, :]
    masks = np.zeros((P, 2, LEVELS + 1, P), np.uint8)
    for lv in range(LEVELS):
        H = 1 << lv
        same = (s_ // (2 * H)) == (t_ // (2 * H))
        masks[:, 0, lv] = same & (s_ % (2 * H) < H) & (t_ % (2 * H) >= H)
        masks[:, 1, lv] = same & (s_ % (2 * H) >= H) & (t_ % (2 * H) < H)
    masks[:, :, LEVELS] = (s_ == t_)[:, None, :]
    pos = np.arange(SEQ)
    inv = (10000.0 ** (-np.arange(16, dtype=np.float32) / 16)).astype(np.float32)
    ang = np.concatenate([(pos // GRID_W)[:, None].astype(np.float32) * inv,
                          (pos % GRID_W)[:, None].astype(np.float32) * inv], axis=1)
    rope = np.stack([np.cos(ang), np.sin(ang)]).astype(np.float32).reshape(2, 4, P, 32).transpose(2, 0, 1, 3)
    swam = np.stack([np.where(t_ >= s_, 0.0, NEG), np.where(t_ <= s_, 0.0, NEG)], axis=1).astype(np.float32)
    col = np.arange(GRID_W)
    start = np.clip(col - NAT_COLS // 2, 0, GRID_W - NAT_COLS)
    ok = (col[None, :] >= start[:, None]) & (col[None, :] < start[:, None] + NAT_COLS)
    natm = np.tile(np.where(ok, 0.0, NEG).astype(np.float32), (2, 1))
    return {"ident": ident, "iota": iota, "masks": masks.reshape(P, -1).view(np.float32).copy(),
            "rope": rope.reshape(P, 256).copy(), "swam": swam.reshape(P, 256).copy(), "natm": natm}


def tiles_of(w, width):
    n = w.shape[1] // width
    return w.reshape(KD, P, n, width).transpose(2, 1, 0, 3)


def lay_out(a):
    L = DEPTH
    A = {"x": a["x"][0], "ctx": a["ctx"][0]}
    A["c"] = np.stack([a["c"][0].reshape(KD, P).T, a["c_ctx"].reshape(KD, P).T], axis=2)
    A["lb"] = a["hgrn_lb_logits"].reshape(2, L, 2, P).transpose(3, 0, 2, 1)
    wcat, wq, ex, bT, nw, rpb, subk, bgate = [], [], [], [], [], [], [], []
    for l in range(L):
        wm = np.split(a["w_mod"][l], 6, axis=1)
        wm = np.concatenate([wm[i] for i in (0, 1, 3, 4, 2, 5)], axis=1)
        wi = a["w_in"][l]
        wi = np.concatenate([wi[:, 0:1920], wi[:, 2688:3072], wi[:, 1920:2688]], axis=1)
        wcat.append(np.concatenate([tiles_of(w, TW).reshape(-1, P, TILE_F) for w in (wm, wi, a["w_out"][l])]))
        wq.append(a["peer_wq"][l].reshape(KD, P, WQ_TILES, 2, P).transpose(2, 1, 3, 0, 4).reshape(WQ_TILES, P, TILE_F))
        u = a["peer_u"][l].reshape(P, PK, KD, P).transpose(1, 3, 2, 0).reshape(PK, P, D)
        v = a["peer_v"][l].reshape(P, PK, D).transpose(1, 0, 2)
        ex.append(np.concatenate([u, v], axis=2))
        bm = np.split(a["b_mod"][l], 6)
        bm_ = np.concatenate([bm[i].reshape(KD, P).T for i in (0, 1, 3, 4)], axis=1)
        bT.append(np.repeat(bm_[:, :, None], 2, axis=2).reshape(P, 64))
        bgate.append(np.concatenate([bm[2], bm[5]]))
        nw.append(np.concatenate([a["norm_mix_w"][l].reshape(KD, P).T, a["norm_ffn_w"][l].reshape(KD, P).T], axis=1))
        r = a["nat_rpb"][l]
        wide = np.zeros((NAT_H, 15, 127), r.dtype)
        wide[:, :, 48:79] = r
        rpb.append(np.stack([wide[:, :, 63 - c:127 - c] for c in range(GRID_W)], axis=1).reshape(NAT_H, GRID_W, 960))
        subk.append(a["peer_subkeys"][l].reshape(16, P, P).transpose(2, 0, 1).reshape(P, 2048))
    A["wcat"], A["wq"], A["experts"], A["bT"], A["nw"] = map(np.stack, (wcat, wq, ex, bT, nw))
    A["rpb"], A["subk"], A["bgate"] = map(np.stack, (rpb, subk, bgate))
    A["sink"], A["hnw"] = a["swa_sink"], a["hgrn_norm_w"]
    A["fnw"] = a["final_norm_w"].reshape(1, D)
    A.update(shape_tables())
    return {k: np.ascontiguousarray(v) for k, v in A.items()}


def declare(nc, arrays):
    d = {k: nc.dram_tensor(f"in_{k}", v.shape, mybir.dt.from_np(v.dtype), kind="ExternalInput").ap()
         for k, v in arrays.items()}
    d["xs"] = nc.dram_tensor("xs", (TOK, D), F32).ap()
    d["gates"] = nc.dram_tensor("gates", (DEPTH, 2, 2 * D), F32).ap()
    return d


def kernel(**inputs):
    import concourse.bacc as bacc
    from concourse.bass_utils import run_bass_kernel_spmd

    arrays = lay_out({k: np.asarray(v) for k, v in inputs.items()})
    nc = bacc.Bacc("TRN2", target_bir_lowering=False, num_devices=1)
    d = declare(nc, arrays)
    out = nc.dram_tensor("out", (SEQ, D), F32, kind="ExternalOutput").ap()
    build(nc, d, out)
    r = run_bass_kernel_spmd(nc, [{f"in_{k}": v for k, v in arrays.items()}], core_ids=[0])
    return r.results[0]["out"].reshape(1, SEQ, D)
```
